# Optimizing a Trainium2 kernel written in Bass

```python
import numpy as np
import jax, jax.numpy as jnp
from jax import lax

D_MODEL = 1024
BATCH = 1
SEQ = 256
DEPTH = 2

N_MIXERS = 4
ALPHA = (2.0 * DEPTH) ** 0.25
BETA = (8.0 * DEPTH) ** -0.25
LN_EPS = 1e-5
NEG_INF = -1e30
TINY = 1e-30
ROPE_THETA = 10000.0

MLSTM_HEADS = 8
MLSTM_QK_DIM = D_MODEL // MLSTM_HEADS // 2
MLSTM_V_DIM = D_MODEL // MLSTM_HEADS
MLSTM_CONV = 4
MLSTM_CHUNK = 64

NSA_HEADS = 16
NSA_KV_HEADS = 4
NSA_HEAD_DIM = D_MODEL // NSA_HEADS
CMP_STRIDE = 16
CMP_BLK = 2 * CMP_STRIDE
SEL_BLK = 64
N_SEL = 16
NSA_WINDOW = 512
NSA_QB = 32
FORCE_SCORE = 1e4

DIL_HEADS = 16
DIL_HEAD_DIM = D_MODEL // DIL_HEADS
DIL_GROUPS = ((128, 1), (512, 4), (2048, 16))

POOL_WINDOWS = (2, 4, 8, 16)
POOL_GROUP = D_MODEL // len(POOL_WINDOWS)

N_EXPERTS = 64
TOP_K = 8
N_EXPERT_GROUPS = 8
TOPK_GROUPS = 4
EXPERT_FF = 256
SHARED_FF = 256
ROUTED_SCALE = 2.5
ROW_BLK = 128

PLE_DIM = 256

kernel_name = "hybrid_mlstm_nsa_dilated_pool_moe"

def _n_uses(m):
    return (DEPTH - m + N_MIXERS - 1) // N_MIXERS

def split_cols(t, sizes):
    return jnp.split(t, np.cumsum(sizes)[:-1].tolist(), axis=-1)

def layer_norm(x, g, b):
    xf = x.astype(jnp.float32)
    mu = xf.mean(-1, keepdims=True)
    var = jnp.square(xf - mu).mean(-1, keepdims=True)
    return ((xf - mu) * lax.rsqrt(var + LN_EPS) * g + b).astype(x.dtype)

def rope(t, pos):
    half = t.shape[-1] // 2
    inv = ROPE_THETA ** (-jnp.arange(half, dtype=jnp.float32) / half)
    ang = pos.astype(jnp.float32)[:, None] * inv[None, :]
    cos, sin = jnp.cos(ang)[:, None, :], jnp.sin(ang)[:, None, :]
    tf = t.astype(jnp.float32)
    t1, t2 = tf[..., :half], tf[..., half:]
    return jnp.concatenate([t1 * cos - t2 * sin, t1 * sin + t2 * cos], -1).astype(t.dtype)

def masked_softmax(s, mask):
    s = jnp.where(mask, s, NEG_INF)
    m = s.max(-1, keepdims=True)
    e = jnp.where(mask, jnp.exp(s - m), 0.0)
    return e / jnp.maximum(e.sum(-1, keepdims=True), TINY)

def swiglu(t, wg, wu, wd):
    return (jax.nn.silu(t @ wg) * (t @ wu)) @ wd

def causal_dwconv(x, w):
    return lax.conv_general_dilated(x, w[:, None, :], window_strides=(1,),
                                    padding=[(w.shape[0] - 1, 0)],
                                    dimension_numbers=('NWC', 'WIO', 'NWC'),
                                    feature_group_count=x.shape[-1])

def mlstm_chunk_step(carry, inp):
    C, n, m = carry
    q, k, v, ig, lf = inp
    L = q.shape[2]
    tri = jnp.arange(L)[:, None] >= jnp.arange(L)[None, :]
    b = jnp.cumsum(lf, axis=-1)
    logD = jnp.where(tri, b[..., :, None] - b[..., None, :] + ig[..., None, :], NEG_INF)
    inter = b + m[..., None]
    m_t = jnp.maximum(inter, logD.max(-1))
    s = jnp.einsum('bhtd,bhsd->bhts', q, k) * jnp.exp(logD - m_t[..., None])
    w_inter = jnp.exp(inter - m_t)
    num = w_inter[..., None] * jnp.einsum('bhtd,bhdv->bhtv', q, C) + jnp.einsum('bhts,bhsv->bhtv', s, v)
    den = w_inter * jnp.einsum('bhtd,bhd->bht', q, n) + s.sum(-1)
    h = num / jnp.maximum(jnp.abs(den), jnp.exp(-m_t))[..., None]
    bL = b[..., -1]
    logw = bL[..., None] - b + ig
    m_new = jnp.maximum(bL + m, logw.max(-1))
    w = jnp.exp(logw - m_new[..., None])
    decay = jnp.exp(bL + m - m_new)
    C_new = decay[..., None, None] * C + jnp.einsum('bhs,bhsd,bhsv->bhdv', w, k, v)
    n_new = decay[..., None] * n + jnp.einsum('bhs,bhsd->bhd', w, k)
    return (C_new, n_new, m_new), h

def mlstm_mixer(x, w_in, conv_w, ig_bias, fg_bias, norm_g, w_out):
    B, S, _ = x.shape
    H, dk, dv, L = MLSTM_HEADS, MLSTM_QK_DIM, MLSTM_V_DIM, MLSTM_CHUNK
    qk, v, o, ig, fg = split_cols(x @ w_in, [2 * H * dk, H * dv, H * dv, H, H])
    q, k = jnp.split(jax.nn.silu(causal_dwconv(qk, conv_w)), 2, axis=-1)
    f32 = jnp.float32
    q = q.reshape(B, S, H, dk).astype(f32) * dk ** -0.5
    k = k.reshape(B, S, H, dk).astype(f32)
    v = v.reshape(B, S, H, dv).astype(f32)
    ig = ig.astype(f32) + ig_bias.astype(f32)
    lf = jax.nn.log_sigmoid(fg.astype(f32) + fg_bias.astype(f32))
    nc = S // L
    c4 = lambda t: t.reshape(B, nc, L, H, t.shape[-1]).transpose(1, 0, 3, 2, 4)
    c3 = lambda t: t.reshape(B, nc, L, H).transpose(1, 0, 3, 2)
    init = (jnp.zeros((B, H, dk, dv), f32), jnp.zeros((B, H, dk), f32), jnp.zeros((B, H), f32))
    _, h = lax.scan(mlstm_chunk_step, init, (c4(q), c4(k), c4(v), c3(ig), c3(lf)))
    h = h.transpose(1, 0, 3, 2, 4).reshape(B, S, H, dv)
    mu = h.mean(-1, keepdims=True)
    hn = (h - mu) * lax.rsqrt(jnp.square(h - mu).mean(-1, keepdims=True) + LN_EPS)
    hn = hn.reshape(B, S, H * dv) * norm_g
    out = hn * jax.nn.sigmoid(o.astype(f32))
    return out.astype(x.dtype) @ w_out

def nsa_mixer(x, w_in, cmp_pos_k, cmp_pos_v, cmp_wk, cmp_wv, w_out):
    B, S, _ = x.shape
    H, G, dh = NSA_HEADS, NSA_KV_HEADS, NSA_HEAD_DIM
    J = H // G
    kv = G * dh
    q, kc, vc, ks, vs, kw, vw, g = split_cols(x @ w_in, [H * dh] + [kv] * 6 + [3 * H])
    pos = jnp.arange(S)
    q = rope(q.reshape(B, S, H, dh), pos)

    def compress(t, pos_emb, w):
        ch = t.reshape(B, S // CMP_STRIDE, CMP_STRIDE, G, dh)
        blocks = jnp.concatenate([ch[:, :-1], ch[:, 1:]], axis=2)
        return jnp.einsum('bclgd,lde->bcge', blocks + pos_emb[None, None, :, None, :], w)

    n_cmp = S // CMP_STRIDE - 1
    cmp_end = jnp.arange(n_cmp) * CMP_STRIDE + CMP_BLK - 1
    kc = rope(compress(kc.reshape(B, S, G, dh), cmp_pos_k, cmp_wk), cmp_end)
    vc = compress(vc.reshape(B, S, G, dh), cmp_pos_v, cmp_wv)
    n_sblk = S // SEL_BLK
    n_sel = min(N_SEL, n_sblk)
    ks_blk = rope(ks.reshape(B, S, G, dh), pos).reshape(B, n_sblk, SEL_BLK, G, dh).transpose(0, 3, 1, 2, 4)
    vs_blk = vs.reshape(B, n_sblk, SEL_BLK, G, dh).transpose(0, 3, 1, 2, 4)
    padw = ((0, 0), (NSA_WINDOW, 0), (0, 0), (0, 0))
    kw_pad = jnp.pad(rope(kw.reshape(B, S, G, dh), pos), padw)
    vw_pad = jnp.pad(vw.reshape(B, S, G, dh), padw)
    c_idx, s_idx = jnp.arange(n_cmp), jnp.arange(n_sblk)
    overlap = ((c_idx[:, None] * CMP_STRIDE + CMP_BLK - 1 >= s_idx[None, :] * SEL_BLK)
               & (c_idx[:, None] * CMP_STRIDE < (s_idx[None, :] + 1) * SEL_BLK)).astype(jnp.float32)
    n_qb = S // NSA_QB
    qb = q.reshape(B, n_qb, NSA_QB, G, J, dh).transpose(1, 0, 3, 4, 2, 5)
    gb = jax.nn.sigmoid(g.astype(jnp.float32)).reshape(B, n_qb, NSA_QB, G, J, 3).transpose(1, 0, 3, 4, 2, 5)
    q0s = jnp.arange(n_qb, dtype=jnp.int32) * NSA_QB
    scale = dh ** -0.5
    bi = jnp.arange(B)[:, None, None, None]
    gi = jnp.arange(G)[None, :, None, None]

    def block(args):
        qi, gate, q0 = args
        t = q0 + jnp.arange(NSA_QB)
        s = jnp.einsum('bgjqd,bcgd->bgjqc', qi, kc).astype(jnp.float32) * scale
        p_cmp = masked_softmax(s, cmp_end[None, :] <= t[:, None])
        o_cmp = jnp.einsum('bgjqc,bcgd->bgjqd', p_cmp, vc)
        imp = jnp.einsum('bgjqc,cn->bgqn', p_cmp, overlap)
        qblk = t // SEL_BLK
        forced = (s_idx[None, :] == 0) | (s_idx[None, :] == qblk[:, None]) | (s_idx[None, :] == qblk[:, None] - 1)
        imp = jnp.where(forced, FORCE_SCORE, jnp.where(s_idx[None, :] > qblk[:, None], NEG_INF, imp))
        _, sel = lax.top_k(imp, n_sel)
        k_sel = ks_blk[bi, gi, sel]
        v_sel = vs_blk[bi, gi, sel].reshape(B, G, NSA_QB, n_sel * SEL_BLK, dh)
        s = jnp.einsum('bgjqd,bgqnkd->bgjqnk', qi, k_sel).astype(jnp.float32) * scale
        kpos = sel[..., None] * SEL_BLK + jnp.arange(SEL_BLK)
        valid = (kpos <= t[None, None, :, None, None]).reshape(B, G, 1, NSA_QB, n_sel * SEL_BLK)
        p_slc = masked_softmax(s.reshape(B, G, J, NSA_QB, n_sel * SEL_BLK), valid)
        o_slc = jnp.einsum('bgjqm,bgqmd->bgjqd', p_slc, v_sel)
        kwin = lax.dynamic_slice_in_dim(kw_pad, q0, NSA_WINDOW + NSA_QB, axis=1)
        vwin = lax.dynamic_slice_in_dim(vw_pad, q0, NSA_WINDOW + NSA_QB, axis=1)
        wpos = q0 - NSA_WINDOW + jnp.arange(NSA_WINDOW + NSA_QB)
        dist = t[:, None] - wpos[None, :]
        wvalid = (dist >= 0) & (dist < NSA_WINDOW) & (wpos[None, :] >= 0)
        s = jnp.einsum('bgjqd,bkgd->bgjqk', qi, kwin).astype(jnp.float32) * scale
        o_win = jnp.einsum('bgjqk,bkgd->bgjqd', masked_softmax(s, wvalid), vwin)
        return gate[..., 0:1] * o_cmp + gate[..., 1:2] * o_slc + gate[..., 2:3] * o_win

    o = lax.map(block, (qb, gb, q0s))
    o = o.transpose(1, 0, 4, 2, 3, 5).reshape(B, S, H * dh)
    return o.astype(x.dtype) @ w_out

def dilated_band_attn(q, k, v, window, dil):
    B, S, H, dh = q.shape
    steps = window // dil
    span = steps * dil
    sp = -(-S // span) * span
    nb = sp // span
    padw = ((0, 0), (0, sp - S), (0, 0), (0, 0))
    blocks = lambda t: jnp.pad(t, padw).reshape(B, nb, steps, dil, H, dh)
    band = lambda t: jnp.concatenate(
        [jnp.pad(t, ((0, 0), (1, 0), (0, 0), (0, 0), (0, 0), (0, 0)))[:, :-1], t], axis=2)
    qb = blocks(q)
    kband, vband = band(blocks(k)), band(blocks(v))
    s = jnp.einsum('bnqrhd,bnkrhd->bnrhqk', qb, kband).astype(jnp.float32) * dh ** -0.5
    qi, kj = jnp.arange(steps), jnp.arange(2 * steps)
    dist = steps + qi[:, None] - kj[None, :]
    valid = ((dist >= 0) & (dist <= steps))[None] & ~((jnp.arange(nb) == 0)[:, None, None] & (kj < steps)[None, None, :])
    s = jnp.where(valid[None, :, None, None], s, NEG_INF)
    m = s.max(-1, keepdims=True)
    e = jnp.exp(s - m)
    den = e.sum(-1, keepdims=True)
    o = jnp.einsum('bnrhqk,bnkrhd->bnqrhd', e / den, vband).reshape(B, sp, H, dh)[:, :S]
    lse = (m + jnp.log(den))[..., 0].transpose(0, 1, 4, 2, 3).reshape(B, sp, H)[:, :S]
    return o, lse

def dilated_mixer(x, w_in, w_out):
    B, S, _ = x.shape
    H, dh = DIL_HEADS, DIL_HEAD_DIM
    parts = split_cols(x @ w_in, [H * dh] * (2 * len(DIL_GROUPS) + 1))
    v = parts[-1].reshape(B, S, H, dh)
    pos = jnp.arange(S)
    outs, lses = [], []
    for gi_, (window, dil) in enumerate(DIL_GROUPS):
        q = rope(parts[2 * gi_].reshape(B, S, H, dh), pos)
        k = rope(parts[2 * gi_ + 1].reshape(B, S, H, dh), pos)
        o, lse = dilated_band_attn(q, k, v, window, dil)
        outs.append(o)
        lses.append(lse)
    wts = jax.nn.softmax(jnp.stack(lses, 0), axis=0)
    o = jnp.einsum('gbsh,gbshd->bshd', wts, jnp.stack(outs, 0))
    return o.reshape(B, S, H * dh).astype(x.dtype) @ w_out

def pool_mixer(x, w_grp, scale):
    B, S, _ = x.shape
    xf = x.astype(jnp.float32)
    cs = lax.cumsum(xf, axis=1)
    cnt = jnp.arange(1, S + 1, dtype=jnp.float32)[None, :, None]
    outs = []
    for g, w in enumerate(POOL_WINDOWS):
        sl = slice(g * POOL_GROUP, (g + 1) * POOL_GROUP)
        c = cs[..., sl]
        lagged = jnp.pad(c, ((0, 0), (w, 0), (0, 0)))[:, :S]
        mean = (c - lagged) / jnp.minimum(cnt, float(w))
        outs.append((mean - xf[..., sl]).astype(x.dtype) @ w_grp[g])
    return jnp.concatenate(outs, -1) * scale

def routed_experts(xf, eidx, gw, w_gate, w_up, w_down):
    T, D = xf.shape
    A = T * TOP_K
    flat_e = eidx.reshape(A)
    order = jnp.argsort(flat_e)
    sorted_e = flat_e[order]
    counts = jnp.bincount(flat_e, length=N_EXPERTS)
    padded = (counts + ROW_BLK - 1) // ROW_BLK * ROW_BLK
    pad_end = jnp.cumsum(padded)
    pad_start = pad_end - padded
    start = jnp.cumsum(counts) - counts
    dest = pad_start[sorted_e] + (jnp.arange(A) - start[sorted_e])
    n_blk = -(-A // ROW_BLK) + N_EXPERTS
    tok = order // TOP_K
    rows = jnp.zeros((n_blk * ROW_BLK, D), xf.dtype).at[dest].set(xf[tok])
    blk_expert = jnp.minimum(jnp.searchsorted(pad_end, jnp.arange(n_blk) * ROW_BLK, side='right'), N_EXPERTS - 1)

    def expert_block(args):
        xb, e = args
        return swiglu(xb, w_gate[e], w_up[e], w_down[e])

    out = lax.map(expert_block, (rows.reshape(n_blk, ROW_BLK, D), blk_expert)).reshape(-1, D)
    contrib = out[dest].astype(jnp.float32) * gw.reshape(A)[order][:, None]
    return jax.ops.segment_sum(contrib, tok, num_segments=T)

def moe_ffn(x, router_w, router_bias, w_gate, w_up, w_down, ws_gate, ws_up, ws_down):
    B, S, D = x.shape
    T = B * S
    xf = x.reshape(T, D)
    scores = jax.nn.sigmoid((xf @ router_w).astype(jnp.float32))
    biased = scores + router_bias.astype(jnp.float32)
    per = N_EXPERTS // N_EXPERT_GROUPS
    grp_score = lax.top_k(biased.reshape(T, N_EXPERT_GROUPS, per), 2)[0].sum(-1)
    _, gidx = lax.top_k(grp_score, TOPK_GROUPS)
    gmask = jax.nn.one_hot(gidx, N_EXPERT_GROUPS, dtype=jnp.float32).sum(1) > 0
    emask = jnp.repeat(gmask, per, axis=1)
    _, eidx = lax.top_k(jnp.where(emask, biased, NEG_INF), TOP_K)
    gw = jnp.take_along_axis(scores, eidx, axis=1)
    gw = gw / gw.sum(-1, keepdims=True) * ROUTED_SCALE
    routed = routed_experts(xf, eidx, gw, w_gate, w_up, w_down)
    shared = swiglu(xf, ws_gate, ws_up, ws_down).astype(jnp.float32)
    return (routed + shared).astype(x.dtype).reshape(B, S, D)

def setup_inputs(seed: int = 0) -> dict:
    key = jax.random.key(seed)
    kit = iter(list(jax.random.split(key, 40)))
    f32 = jnp.float32

    def nrm(shape, scale):
        return jax.random.normal(next(kit), shape, f32) * scale

    D = D_MODEL
    nA, nB, nC, nD = (_n_uses(m) for m in range(N_MIXERS))
    mH, dk, dv = MLSTM_HEADS, MLSTM_QK_DIM, MLSTM_V_DIM
    nH, nG, ndh = NSA_HEADS, NSA_KV_HEADS, NSA_HEAD_DIM
    dH, ddh = DIL_HEADS, DIL_HEAD_DIM
    mlstm_in = 2 * mH * dk + 2 * mH * dv + 2 * mH
    nsa_in = nH * ndh + 6 * nG * ndh + 3 * nH
    dil_in = (2 * len(DIL_GROUPS) + 1) * dH * ddh
    return {
        "x": nrm((BATCH, SEQ, D), 1.0),
        "p": nrm((DEPTH, BATCH, SEQ, PLE_DIM), 1.0),
        "ln_g": 1.0 + nrm((DEPTH, 2, D), 0.02),
        "ln_b": nrm((DEPTH, 2, D), 0.02),
        "mlstm_w_in": nrm((nA, D, mlstm_in), D ** -0.5),
        "mlstm_conv": nrm((nA, MLSTM_CONV, 2 * mH * dk), MLSTM_CONV ** -0.5),
        "mlstm_ig_bias": nrm((nA, mH), 0.1),
        "mlstm_fg_bias": jnp.linspace(3.0, 6.0, mH, dtype=f32)[None, :] + nrm((nA, mH), 0.1),
        "mlstm_norm_g": 1.0 + nrm((nA, mH * dv), 0.02),
        "mlstm_w_out": nrm((nA, mH * dv, D), BETA * (mH * dv) ** -0.5),
        "nsa_w_in": nrm((nB, D, nsa_in), D ** -0.5),
        "nsa_cmp_pos_k": nrm((nB, CMP_BLK, ndh), 0.02),
        "nsa_cmp_pos_v": nrm((nB, CMP_BLK, ndh), 0.02),
        "nsa_cmp_wk": nrm((nB, CMP_BLK, ndh, ndh), (CMP_BLK * ndh) ** -0.5),
        "nsa_cmp_wv": nrm((nB, CMP_BLK, ndh, ndh), (CMP_BLK * ndh) ** -0.5),
        "nsa_w_out": nrm((nB, nH * ndh, D), BETA * (nH * ndh) ** -0.5),
        "dil_w_in": nrm((nC, D, dil_in), D ** -0.5),
        "dil_w_out": nrm((nC, dH * ddh, D), BETA * (dH * ddh) ** -0.5),
        "pool_w": nrm((nD, len(POOL_WINDOWS), POOL_GROUP, POOL_GROUP), BETA * POOL_GROUP ** -0.5),
        "pool_scale": 1.0 + nrm((nD, D), 0.1),
        "router_w": nrm((DEPTH, D, N_EXPERTS), D ** -0.5),
        "router_bias": nrm((DEPTH, N_EXPERTS), 0.01),
        "exp_w_gate": nrm((DEPTH, N_EXPERTS, D, EXPERT_FF), D ** -0.5),
        "exp_w_up": nrm((DEPTH, N_EXPERTS, D, EXPERT_FF), D ** -0.5),
        "exp_w_down": nrm((DEPTH, N_EXPERTS, EXPERT_FF, D), BETA * EXPERT_FF ** -0.5),
        "sh_w_gate": nrm((DEPTH, D, SHARED_FF), D ** -0.5),
        "sh_w_up": nrm((DEPTH, D, SHARED_FF), D ** -0.5),
        "sh_w_down": nrm((DEPTH, SHARED_FF, D), BETA * SHARED_FF ** -0.5),
        "ple_w": nrm((DEPTH, PLE_DIM, D), BETA * PLE_DIM ** -0.5),
        "ple_gate_w": nrm((DEPTH, D, D), D ** -0.5),
    }

def reference(x, p, ln_g, ln_b, mlstm_w_in, mlstm_conv, mlstm_ig_bias, mlstm_fg_bias, mlstm_norm_g,
              mlstm_w_out, nsa_w_in, nsa_cmp_pos_k, nsa_cmp_pos_v, nsa_cmp_wk, nsa_cmp_wv, nsa_w_out,
              dil_w_in, dil_w_out, pool_w, pool_scale, router_w, router_bias, exp_w_gate, exp_w_up,
              exp_w_down, sh_w_gate, sh_w_up, sh_w_down, ple_w, ple_gate_w):
    for i in range(DEPTH):
        kind, j = i % N_MIXERS, i // N_MIXERS
        if kind == 0:
            y = mlstm_mixer(x, mlstm_w_in[j], mlstm_conv[j], mlstm_ig_bias[j], mlstm_fg_bias[j],
                            mlstm_norm_g[j], mlstm_w_out[j])
        elif kind == 1:
            y = nsa_mixer(x, nsa_w_in[j], nsa_cmp_pos_k[j], nsa_cmp_pos_v[j], nsa_cmp_wk[j],
                          nsa_cmp_wv[j], nsa_w_out[j])
        elif kind == 2:
            y = dilated_mixer(x, dil_w_in[j], dil_w_out[j])
        else:
            y = pool_mixer(x, pool_w[j], pool_scale[j])
        x = layer_norm(ALPHA * x + y, ln_g[i, 0], ln_b[i, 0])
        f = moe_ffn(x, router_w[i], router_bias[i], exp_w_gate[i], exp_w_up[i], exp_w_down[i],
                    sh_w_gate[i], sh_w_up[i], sh_w_down[i])
        x = layer_norm(ALPHA * x + f, ln_g[i, 1], ln_b[i, 1])
        x = x + (jax.nn.sigmoid(x @ ple_gate_w[i]) * (p[i] @ ple_w[i])).astype(x.dtype)
    return x


_drawn_inputs = setup_inputs


def setup_inputs(seed=0):
    import zlib

    import numpy as np

    out = dict(_drawn_inputs(seed))
    spreads = {}
    factors = {'mlstm_ig_bias': 64.0,
     'mlstm_norm_g': 2.667,
     'nsa_cmp_pos_k': 22.846,
     'nsa_cmp_pos_v': 7.541}
    for name, (base, spread) in spreads.items():
        noise = np.random.default_rng([zlib.crc32(name.encode()), seed]).standard_normal(out[name].shape)
        drawn = base * np.exp(spread * noise) if base else spread * noise
        out[name] = __import__('jax').numpy.asarray(drawn.astype(out[name].dtype))
    for name, factor in factors.items():
        out[name] = (out[name] * factor).astype(out[name].dtype)
    return out
```

```python
from contextlib import ExitStack

import numpy as np
import concourse.bass as bass
from concourse import mybir

F32 = mybir.dt.float32
ALU = mybir.AluOpType
ACT = mybir.ActivationFunctionType
AX = mybir.AxisListType

P = 128
D = 1024
T = 256
NT = T // P
KD = D // P
DEPTH = 2
ALPHA = (2.0 * DEPTH) ** 0.25
EPS = 1e-5
BIG = 1e30

MH, MDK, MDV, MCONV = 8, 64, 128, 4
NH, NG, NDH = 16, 4, 64
NJ = NH // NG
CSTR, CBLK = 16, 32
NCMP = T // CSTR - 1
NE, TOPK, NEG, TOPG, FF = 64, 8, 8, 4, 256
SCALE_R = 2.5
PLE = 256

SLOT = 2048
RING = 12
EPB = 4
NB_WORK = 4


def tail_groups(layer):
    before = [("xT", g) for g in range(4)] + ["logits", "sh_gate", "sh_up", "cwT"]
    after = [("xT2", g) for g in range(4)] + ["pT"] + [("pg", q) for q in range(4)]
    return [(layer, g) for g in before], [(layer, g) for g in after]


def mlstm_groups():
    heads = [("S", 0)]
    for h in range(MH):
        heads += ([("S", h + 1)] if h + 1 < MH else []) + [("num", h)]
    return ([("x0T", g) for g in range(4)] + ["gates", "convT"] + [("qk", g) for g in range(4)] + ["gateT"]
            + [("B", g) for g in range(4)] + [("v", g) for g in range(4)] + [("o", g) for g in range(4)]
            + heads + [("mT", g) for g in range(4)])


def nsa_groups():
    units = []
    for u in range(NUNIT + 1):
        units += ([("US", u)] if u < NUNIT else []) + ([("UT", u - 1)] if u else [])
    return ([("x1T", g) for g in range(4)] + ["g", "pos"]
            + ["q0", "q1", "rq0", "q2", "rq1", "q3", "rq2", "kc", "rq3", "vc", "ks", "vs", "rks", "kw", "vw", "rkw"]
            + ["cmp0", "cmp1", "kcrot", "vcT"] + [("cs", t, par) for t in range(NT) for par in range(2)]
            + [("pcT", 0), ("pcT", 1)] + units + [("nT", g) for g in range(4)])


NUNIT = 2 * NH
LOOP_GROUPS = 2 * EPB
N_BODIES = NE // EPB

AT, LOOP_AT = {}, []
_n = 0
for _layer, _mixer in enumerate((mlstm_groups(), nsa_groups())):
    _before, _after = tail_groups(_layer)
    for _g in [(_layer, g) for g in _mixer] + _before:
        AT[_g] = _n
        _n += 1
    LOOP_AT.append(_n)
    _n += LOOP_GROUPS * N_BODIES
    for _g in _after:
        AT[_g] = _n
        _n += 1

PIECES_MIX = (12, 10)
LOOP_PIECES = 3 * EPB
PIECE_LOOP, PIECE_MIX, PIECE_OUT, PIECE_SH, PIECE_PLE = [], [], [], [], []
_n = 0
for _layer in range(DEPTH):
    PIECE_MIX.append(_n)
    _n += PIECES_MIX[_layer]
    PIECE_OUT.append(_n)
    _n += 4
    PIECE_SH.append(_n)
    _n += 3
    PIECE_LOOP.append(_n)
    _n += LOOP_PIECES * N_BODIES
    PIECE_PLE.append(_n)
    _n += 5


def landed_value(n):
    extra = sum(3 for m in range(PIECE_MIX[1], PIECE_MIX[1] + 4) if m <= n and m % RING == n % RING)
    return 16 * (n // RING + 1 + extra)


BODY = [("g", 0), ("u", 0), ("g", 1), ("u", 1), ("d", 0), ("g", 2), ("u", 2), ("d", 1), ("g", 3), ("u", 3), ("d", 2), ("d", 3)]

USED = {}
_rows = 0
ROWS_BEFORE_LOOP = []
for _layer in range(DEPTH):
    _names = ([("qk", g) for g in range(4)] + [("v", g) for g in range(4)] + [("o", g) for g in range(4)] if _layer == 0
              else ["q0", "q1", "q2", "q3", "kc", "vc", "ks", "vs", "kw", "vw"])
    for _j, _g in enumerate(_names):
        USED[PIECE_MIX[_layer] + _j] = ("bank", AT[(_layer, _g)])
    for _j in range(4):
        _rows += 1
        USED[PIECE_OUT[_layer] + _j] = ("rows", _rows)
    USED[PIECE_SH[_layer]] = ("bank", AT[(_layer, "sh_gate")])
    USED[PIECE_SH[_layer] + 1] = ("bank", AT[(_layer, "sh_up")])
    _rows += 1
    USED[PIECE_SH[_layer] + 2] = ("rows", _rows)
    ROWS_BEFORE_LOOP.append(_rows)
    for _i in range(N_BODIES):
        for _j, (_kind, _e) in enumerate(BODY):
            if _kind == "d":
                _rows += 1
                USED[PIECE_LOOP[_layer] + _i * LOOP_PIECES + _j] = ("rows", _rows)
            else:
                USED[PIECE_LOOP[_layer] + _i * LOOP_PIECES + _j] = ("bank", LOOP_AT[_layer] + _i * LOOP_GROUPS + 2 * _e + (_kind == "u"))
    for _j in range(4):
        _rows += 1
        USED[PIECE_PLE[_layer] + _j] = ("rows", _rows)
    USED[PIECE_PLE[_layer] + 4] = ("bank", AT[(_layer, ("pg", 3))])


CONST_COLS = {}


def constants():
    parts = []

    def add(name, a):
        a = np.asarray(a, np.float32).reshape(P, -1)
        at = sum(x.shape[1] for x in parts)
        CONST_COLS[name] = (at, at + a.shape[1])
        parts.append(a)

    idx = np.arange(P)
    add("ident", np.eye(P))
    rot = np.zeros((P, P))
    for m in range(P):
        if m % NDH < NDH // 2:
            rot[m + NDH // 2, m] = -1.0
        else:
            rot[m - NDH // 2, m] = 1.0
    add("rot", rot)
    tri_s = np.where(idx[:, None] <= idx[None, :], 0.0, -BIG)
    add("mask_st", np.concatenate([tri_s, np.zeros((P, P))], 1))
    add("mask_ts", np.concatenate([tri_s.T, np.zeros((P, P)), tri_s.T], 1))
    sel = np.zeros((P, MH, P))
    for h in range(MH):
        sel[h, h, :] = 1.0
    add("sel", sel)
    half = NDH // 2
    inv = (np.float32(10000.0) ** (-np.arange(half, dtype=np.float32) / np.float32(half))).astype(np.float32)

    def table(pos):
        ang = pos.astype(np.float32)[None, :] * inv[idx % half][:, None]
        return np.cos(ang.astype(np.float32)), np.sin(ang.astype(np.float32))

    cos, sin = table(np.arange(T))
    add("cos", cos)
    add("sin", sin)
    end = np.arange(CSTR) * CSTR + CBLK - 1
    cos, sin = table(end)
    add("cos_c", cos)
    add("sin_c", sin)
    t = idx[:, None, None] + P * np.arange(NT)[None, :, None]
    ok = end[None, None, :] <= t
    add("cmask_add", np.where(ok, 0.0, -BIG))
    add("cmask_mul", np.where(ok, 1.0, 0.0))
    add("before", np.broadcast_to(np.arange(NEG)[None, :] < np.arange(NEG)[:, None], (P, NEG, NEG)))
    return np.concatenate(parts, 1)


CONSTS = constants()


class Chain:

    def __init__(self, eng, semaphore):
        self.eng, self.sem, self.n = eng, semaphore, {}

    def step(self, ins, semaphore=None):
        s = semaphore or self.sem
        self.n[str(s)] = n = self.n.get(str(s), 0) + 1
        ins.then_inc(s, 1)
        self.eng.wait_ge(s, n)


def build(nc, a, out):
    ctx = ExitStack()
    with ctx:
        def sb(name, shape):
            return ctx.enter_context(nc.sbuf_tensor(name, shape, F32))

        sems = {}

        def sem(name):
            if name not in sems:
                sems[name] = ctx.enter_context(nc.semaphore(name))
            return sems[name]

        ring = sb("ring", [P, RING, SLOT])
        x = sb("x", [P, NT, D])
        xT = sb("xT", [P, KD, T])
        z = sb("z", [P, NT, D])
        bufA = sb("bufA", [P, 2048])
        bufB = sb("bufB", [P, NT * MH * (MDV + 1)])
        bufC = sb("bufC", [P, 2048])
        bufD = sb("bufD", [P, 2048])
        ln_p = sb("ln_p", [P, 2, D])
        const = sb("const", [P, CONSTS.shape[1]])
        router = sb("router", [P, KD, NE])
        rbias = sb("rbias", [P, NE])
        silu = sb("silu", [P, 2, 512])
        hid = sb("hid", [P, 2, 512])
        cw_b = sb("cw_b", [P, EPB, T])
        p_in = sb("p_in", [P, NT, PLE])
        pT = sb("pT", [P, 2, T])
        wgates = sb("wgates", [P, KD, 48])
        cwT = sb("cwT", [NE, T])
        score = sb("score", [P, NT, NE])
        biased = sb("biased", [P, NT, NE])
        cand = sb("cand", [P, NT, NE])
        cw = sb("cw", [P, NT, NE])
        top8 = sb("top8", [P, NT, 8])
        grp8 = sb("grp8", [P, NT * NEG, 8])
        grp = sb("grp", [P, NT * NEG])
        rank = sb("rank", [P, NT * NEG])
        gcmp = sb("gcmp", [P, NT, NEG, NEG])
        geq = sb("geq", [P, NT, NEG, NEG])
        rsum = sb("rsum", [P, NT])
        lnst = sb("lnst", [P, NT, 2, 6])
        lnmv = sb("lnmv", [P, NT, 2])
        conv_in = sb("conv_in", [32, P])
        conv_w = sb("conv_w", [P, 32])
        gbias = sb("gbias", [MH, 2])
        gbuf = sb("gbuf", [MH, 8, T])
        gtok = sb("gtok", [P, 4, MH])
        den2 = sb("den2", [P, 2])
        hmv = sb("hmv", [P, NT, MH, 2])
        hst = sb("hst", [P, 6])
        pos_in = sb("pos_in", [CBLK, 2, P])
        posT = sb("posT", [P, 2, CBLK])
        kc_raw = sb("kc_raw", [P, 2, 16])
        kcT = sb("kcT", [P, 2, 16])
        kc_t = sb("kc_t", [P, 2, 16])
        gsig = sb("gsig", [P, NT, NH, 3])
        cst16 = sb("cst16", [P, NT, NH])
        nden = sb("nden", [P, NT, NH])
        nmax = sb("nmax", [P, 2, NT])
        acc = ctx.enter_context(nc.psum_tensor("acc", [P, NT, D], F32))
        work = [ctx.enter_context(nc.psum_tensor(f"work{b}", [P, 512], F32)) for b in range(NB_WORK)]
        cw_dram = nc.dram_tensor("cw_dram", [DEPTH, NE, T], F32, kind="Internal").ap()

        def cst(name):
            lo, hi = CONST_COLS[name]
            return const[:, lo:hi]

        ident = cst("ident")

        landed = [sem(f"landed{s}") for s in range(RING)]
        rows_used = sem("rows_used")
        bank_full = [sem(f"bank_full{b}") for b in range(NB_WORK)]
        bank_free = [sem(f"bank_free{b}") for b in range(NB_WORK)]
        ld_cwb = [sem(f"ld_cwb{e}") for e in range(EPB)]

        def full(ins, g):
            return ins.then_inc(bank_full[AT[g] % NB_WORK], 1)

        def wait_full(eng, g):
            eng.wait_ge(bank_full[AT[g] % NB_WORK], AT[g] // NB_WORK + 1)
            return work[AT[g] % NB_WORK]

        def free(ins, g):
            return ins.then_inc(bank_free[AT[g] % NB_WORK], 1)

        def wait_free(pe, g):
            if AT[g] >= NB_WORK:
                pe.wait_ge(bank_free[AT[g] % NB_WORK], AT[g] // NB_WORK)
            return work[AT[g] % NB_WORK]

        def wait_read(eng, g):
            eng.wait_ge(bank_free[AT[g] % NB_WORK], AT[g] // NB_WORK + 1)

        qk = bufA[:].rearrange("p (c t) -> p c t", c=8)
        v_aug = bufB[:].rearrange("p (t h e) -> p t h e", t=NT, h=MH)
        sig_o = bufC[:].rearrange("p (t c) -> p t c", t=NT)
        hm = bufD[:].rearrange("p (t h e) -> p t h e", t=NT, h=MH)
        hm_flat = bufD[:].rearrange("p (t c) -> p t c", t=NT)
        mixT = bufA[:].rearrange("p (k t) -> p k t", k=KD)
        z_flat = z[:].rearrange("p t c -> p (t c)")
        silu_flat = silu[:].rearrange("p b c -> p (b c)")
        hid_flat = hid[:].rearrange("p b c -> p (b c)")

        def decay(h):
            if h < 5:
                return z_flat[:, 384 * h:384 * (h + 1)]
            if h < 7:
                return silu_flat[:, 384 * (h - 5):384 * (h - 4)]
            return hid_flat[:, 0:384]

        pt_m = [hid_flat[:, 384:768], cw_b[:].rearrange("p e t -> p (e t)")[:, 0:384]]
        cmp_w = [z_flat.rearrange("p (l e) -> p l e", e=NDH), bufD[:].rearrange("p (l e) -> p l e", e=NDH)]
        kp = bufC[:].rearrange("p (v half g t) -> p v half g t", v=2, half=2, g=2)
        kT_sw = bufB[:, 0:1024].rearrange("p (s g t) -> p s g t", s=2, g=2)
        v_sw = bufB[:, 1024:2048].rearrange("p (s t c) -> p s t c", s=2, t=NT)
        o_flat = bufC[:].rearrange("p (t c) -> p t c", t=NT)
        o_v = bufC[:].rearrange("p (t h e) -> p t h e", t=NT, h=NH)
        acc_h = acc[:].rearrange("p t (h e) -> p t h e", h=NH)
        cs_s = hid_flat[:, 0:512].rearrange("p (t h c) -> p t h c", t=NT, h=NH)
        cs_p = silu_flat.rearrange("p (t h c) -> p t h c", t=NT, h=NH)
        vrep_in = cw_b[:].rearrange("p e t -> p (e t)")[:, 0:256].rearrange("p (g r c) -> p g r c", g=2, r=4)
        vrep = cw_b[:].rearrange("p e t -> p (e t)")[:, 256:512]
        v_blk = z_flat[:, 1024:2048].rearrange("p (g j e) -> p g j e", g=NG, j=NJ)
        pcT = bufD[:, 1024:2048].rearrange("p (t g c) -> p t g c", t=NT, g=NG)
        u_s = [z_flat[:, 0:384], z_flat[:, 384:768]]
        u_p = [silu_flat[:, 0:384], silu_flat[:, 384:768]]
        u_pT = [bufD[:, 0:384], bufD[:, 384:768]]

        def head_rows(h):
            g = h // NJ
            return slice((g % 2) * NDH, (g % 2 + 1) * NDH), g // 2, (g // 2) * NJ + h % NJ

        block = ctx.enter_context(nc.Block())

        @block.sync
        def _(sp):
            def col(w, lo):
                return w.rearrange("(p k) n -> p k n", k=KD)[:, :, lo:lo + 256]

            def row(w, j, k=KD):
                return w.rearrange("(p k) n -> p k n", k=k)[:, 2 * j:2 * j + 2, :]

            def wait_slot(n, i=0):
                if n >= RING:
                    how, at = USED[n - RING]
                    if how == "rows":
                        sp.wait_ge(rows_used, i * EPB + at)
                    else:
                        sp.wait_ge(bank_full[at % NB_WORK], i * (LOOP_GROUPS // NB_WORK) + (at // NB_WORK + 1))

            def load(n, src):
                wait_slot(n)
                dst = ring[:, n % RING, :].rearrange("p (k n) -> p k n", k=src.shape[1])
                sp.dma_start(dst, src).then_inc(landed[n % RING], 16)

            for layer in range(DEPTH):
                w_in = a["mlstm_w_in" if layer == 0 else "nsa_w_in"][0]
                w_out = a["mlstm_w_out" if layer == 0 else "nsa_w_out"][0]
                n0 = PIECE_MIX[layer]
                for j in range(PIECES_MIX[layer]):
                    if layer == 1 and j < 4:
                        wait_slot(n0 + j)
                        dst = ring[:, (n0 + j) % RING, :].rearrange("p (k c g n) -> p k c g n", k=KD, c=2, g=2)
                        for c in range(2):
                            for par in range(2):
                                lo = ((2 * (j // 2) + par) * NJ + (j % 2) * 2 + c) * NDH
                                src = w_in.rearrange("(p k) n -> p k n", k=KD)[:, :, lo:lo + NDH]
                                sp.dma_start(dst[:, :, c, par, :], src).then_inc(landed[(n0 + j) % RING], 16)
                    else:
                        load(n0 + j, col(w_in, 256 * j))
                for j in range(4):
                    load(PIECE_OUT[layer] + j, row(w_out, j))
                load(PIECE_SH[layer], col(a["sh_w_gate"][layer], 0))
                load(PIECE_SH[layer] + 1, col(a["sh_w_up"][layer], 0))
                load(PIECE_SH[layer] + 2, row(a["sh_w_down"][layer], 0, 2))
                n0 = PIECE_LOOP[layer]
                exp_w = {k: a[n][layer] for k, n in (("g", "exp_w_gate"), ("u", "exp_w_up"), ("d", "exp_w_down"))}
                for j, (kind, e) in enumerate(BODY):
                    wait_slot(n0 + j)
                    src = exp_w[kind][e].rearrange("(p k) n -> p (k n)", p=P)
                    sp.dma_start(ring[:, (n0 + j) % RING, :], src).then_inc(landed[(n0 + j) % RING], 16)
                with sp.Fori(0, N_BODIES - 1) as i:
                    for j, (kind, e) in enumerate(BODY):
                        wait_slot(n0 + LOOP_PIECES + j, i)
                        src = exp_w[kind][bass.ds(i * EPB + (EPB + e), 1)].rearrange("a (p k) n -> p (a k n)", p=P)
                        sp.dma_start(ring[:, (n0 + j) % RING, :], src).then_inc(landed[(n0 + j) % RING], 16)
                n0 = PIECE_PLE[layer]
                load(n0, row(a["ple_w"][layer], 0, 2))
                for j in range(4):
                    load(n0 + 1 + j, row(a["ple_gate_w"][layer], j))
            sp.wait_ge(sem("ple_done"), DEPTH)
            sp.dma_start(out[0].rearrange("(t p) d -> p t d", p=P), x[:]).then_inc(sem("stored"), 16)
            sp.wait_ge(sem("stored"), 16)

        @block.gpsimd
        def _(pool):
            pool.dma_start(x[:], a["x"][0].rearrange("(t p) d -> p t d", p=P)).then_inc(sem("ld_x"), 16)
            pool.dma_start(const[:], a["consts"]).then_inc(sem("ld_const"), 16)
            in_w = [a[n][0].rearrange("(p k) n -> p k n", k=KD) for n in ("mlstm_w_in", "nsa_w_in")]
            pool.dma_start(wgates[:, :, 0:16], in_w[0][:, :, 3072:3088]).then_inc(sem("ld_gw"), 16)
            pool.dma_start(conv_in[:], a["mlstm_conv"][0].rearrange("j (c q) -> (j c) q", q=P)).then_inc(sem("ld_conv"), 16)
            pool.dma_start(gbias[:, 0:1], a["mlstm_ig_bias"].rearrange("a h -> h a")).then_inc(sem("ld_gbias"), 16)
            pool.dma_start(gbias[:, 1:2], a["mlstm_fg_bias"].rearrange("a h -> h a")).then_inc(sem("ld_gbias"), 16)
            pool.memset(v_aug[:, :, :, MDV:MDV + 1], 1.0).then_inc(sem("ones_v"), 1)
            pool.dma_start(ln_p[:, 0, :], a["mlstm_norm_g"][0].partition_broadcast(P)).then_inc(sem("ld_norm"), 16)
            for layer in range(DEPTH):
                if layer:
                    pool.wait_ge(sem("cw_ready"), layer)
                pool.dma_start(router[:], a["router_w"][layer].rearrange("(p k) n -> p k n", k=KD)).then_inc(sem("ld_router"), 16)
                pool.dma_start(rbias[:], a["router_bias"][layer].partition_broadcast(P)).then_inc(sem("ld_router"), 16)
                if layer == 1:
                    wait_read(pool, (0, "gates"))
                    pool.dma_start(wgates[:], in_w[1][:, :, 2560:2608]).then_inc(sem("ld_gw"), 16)
                    for i, n in enumerate(("nsa_cmp_pos_k", "nsa_cmp_pos_v")):
                        for par in range(2):
                            pool.dma_start(pos_in[:, i, par * NDH:(par + 1) * NDH], a[n][0]).then_inc(sem("ld_pos"), 16)
                    pool.wait_ge(sem("ple_done"), 1)
                    for i, n in enumerate(("nsa_cmp_wk", "nsa_cmp_wv")):
                        for par in range(2):
                            dst = cmp_w[i][par * NDH:(par + 1) * NDH]
                            pool.dma_start(dst, a[n][0].rearrange("l d e -> d l e")).then_inc(sem("ld_cmpw"), 16)
                for k in range(2):
                    if layer or k:
                        pool.wait_ge(sem("ln_done"), 2 * layer + k)
                    else:
                        pool.wait_ge(sem("norm_g_used"), 1)
                    pool.dma_start(ln_p[:, 0, :], a["ln_g"][layer, k].partition_broadcast(P)).then_inc(sem("ld_ln"), 16)
                    pool.dma_start(ln_p[:, 1, :], a["ln_b"][layer, k].partition_broadcast(P)).then_inc(sem("ld_ln"), 16)
                    if k == 0:
                        if layer:
                            wait_read(pool, (0, "pT"))
                        pool.dma_start(p_in[:], a["p"][layer, 0].rearrange("(t p) d -> p t d", p=P)).then_inc(sem("ld_p"), 16)
                        wait_read(pool, (layer, "cwT"))
                        pool.dma_start(cw_dram[layer], cwT[:]).then_inc(sem("cw_stored"), 16)
                        pool.wait_ge(sem("cw_stored"), 16 * (layer + 1))
                        for e in range(EPB):
                            pool.dma_start(cw_b[:, e, :], cw_dram[layer, e].partition_broadcast(P)).then_inc(ld_cwb[e], 16)
                        with pool.Fori(0, N_BODIES - 1) as i:
                            for e in range(EPB):
                                pool.wait_ge(sem("hid_ready"), i * EPB + (layer * (NE + 2) + e + 3))
                                src = cw_dram[layer][bass.ds(i * EPB + (EPB + e), 1)].rearrange("a t -> (a t)").partition_broadcast(P)
                                pool.dma_start(cw_b[:, e, :], src).then_inc(ld_cwb[e], 16)

        @block.tensor
        def _(pe):
            mm = nc.tensor.matmul

            def transposes(layer, name, src):
                for g in range(4):
                    ps = wait_free(pe, (layer, (name, g)))
                    for kk in range(2):
                        for t in range(NT):
                            c = (kk * NT + t) * P
                            last = nc.tensor.transpose(ps[:, c:c + P], src[:, t, 2 * g + kk::KD], ident)
                    full(last, (layer, (name, g)))

            def piece(n):
                pe.wait_ge(landed[n % RING], landed_value(n))
                return ring[:, n % RING, :]

            def proj_T(layer, name, n, interleaved=False):
                w = piece(n).rearrange("p (k c) -> p k c", k=KD)
                ps = wait_free(pe, (layer, name))
                for c in range(2):
                    cols = slice(c, None, 2) if interleaved else slice(c * P, (c + 1) * P)
                    for k in range(KD):
                        last = mm(ps[:, c * T:(c + 1) * T], w[:, k, cols], xT[:, k, :], start=(k == 0), stop=(k == KD - 1))
                full(last, (layer, name))

            def proj_tok(layer, name, n):
                w = piece(n).rearrange("p (k c) -> p k c", k=KD)
                ps = wait_free(pe, (layer, name))
                for t in range(NT):
                    for k in range(KD):
                        last = mm(ps[:, t * 256:(t + 1) * 256], xT[:, k, t * P:(t + 1) * P], w[:, k, :], start=(k == 0), stop=(k == KD - 1))
                full(last, (layer, name))

            def rows_to_acc(srcT, n, j, first, last_piece):
                w = piece(n).rearrange("p (k c) -> p k c", k=2)
                for i in range(2):
                    for t in range(NT):
                        for half in range(2):
                            last = mm(acc[:, t, half * 512:(half + 1) * 512], srcT[:, 2 * j + i, t * P:(t + 1) * P],
                                      w[:, i, half * 512:(half + 1) * 512], start=(first and i == 0), stop=(last_piece and i == 1))
                return last.then_inc(rows_used, 1)

            def mlstm():
                pe.wait_ge(sem("ld_const"), 16)
                pe.wait_ge(sem("ld_x"), 16)
                transposes(0, "x0T", x[:])
                for g in range(4):
                    wait_read(pe, (0, ("x0T", g)))
                pe.wait_ge(sem("ld_gw"), 16)
                ps = wait_free(pe, (0, "gates"))
                for i in range(2):
                    for k in range(KD):
                        last = mm(ps[0:MH, i * T:(i + 1) * T], wgates[:, k, i * MH:(i + 1) * MH], xT[:, k, :], start=(k == 0), stop=(k == KD - 1))
                full(last, (0, "gates"))
                pe.wait_ge(sem("ld_conv"), 16)
                ps = wait_free(pe, (0, "convT"))
                full(nc.tensor.transpose(ps[:, 0:32], conv_in[:], ident[0:32, 0:32]), (0, "convT"))
                for g in range(4):
                    proj_T(0, ("qk", g), PIECE_MIX[0] + g)
                pe.wait_ge(sem("grows"), 1)
                ps = wait_free(pe, (0, "gateT"))
                for i, r in enumerate((4, 6)):
                    for t in range(NT):
                        last = nc.tensor.transpose(ps[:, (2 * i + t) * MH:(2 * i + t + 1) * MH], gbuf[:, r, t * P:(t + 1) * P], ident[0:MH, 0:MH])
                full(last, (0, "gateT"))
                for g in range(4):
                    ps = wait_free(pe, (0, ("B", g)))
                    for i in range(2):
                        h = 2 * g + i
                        last = mm(ps[:, i * T:(i + 1) * T], cst("sel")[0:MH, h * P:(h + 1) * P], gbuf[:, 5, :], start=True, stop=True)
                    full(last, (0, ("B", g)))
                for g in range(4):
                    proj_tok(0, ("v", g), PIECE_MIX[0] + 4 + g)
                for g in range(4):
                    proj_tok(0, ("o", g), PIECE_MIX[0] + 8 + g)

                pe.wait_ge(sem("qk_ready"), 4)
                pe.wait_ge(sem("ones_v"), 1)

                def scores(h):
                    rows, tile = slice((h % 2) * MDK, (h % 2 + 1) * MDK), h // 2
                    ps = wait_free(pe, (0, ("S", h)))
                    mm(ps[:, 0:T], qk[rows, 4 + tile, 0:P], qk[rows, tile, :], start=True, stop=True)
                    last = mm(ps[:, T:T + P], qk[rows, 4 + tile, P:T], qk[rows, tile, P:T], start=True, stop=True)
                    full(last, (0, ("S", h)))

                scores(0)
                for h in range(MH):
                    if h + 1 < MH:
                        scores(h + 1)
                    wait_read(pe, (0, ("S", h)))
                    if h == 0:
                        for g in range(4):
                            wait_read(pe, (0, ("v", g)))
                    ps = wait_free(pe, (0, ("num", h)))
                    pt = pt_m[h % 2]
                    mm(ps[:, 0:MDV + 1], pt[:, 0:P], v_aug[:, 0, h, :], start=True, stop=True)
                    mm(ps[:, 256:256 + MDV + 1], pt[:, P:T], v_aug[:, 0, h, :], start=True, stop=False)
                    full(mm(ps[:, 256:256 + MDV + 1], pt[:, T:T + P], v_aug[:, 1, h, :], start=False, stop=True), (0, ("num", h)))
                pe.wait_ge(sem("mix_ready"), 1)
                transposes(0, "mT", hm_flat)
                for g in range(4):
                    wait_read(pe, (0, ("mT", g)))
                for j in range(4):
                    rows_to_acc(mixT, PIECE_OUT[0] + j, j, j == 0, j == 3)

            def nsa():
                pe.wait_ge(sem("ple_done"), 1)
                transposes(1, "x1T", x[:])
                for g in range(4):
                    wait_read(pe, (1, ("x1T", g)))
                pe.wait_ge(sem("ld_gw"), 32)
                ps = wait_free(pe, (1, "g"))
                for t in range(NT):
                    for k in range(KD):
                        last = mm(ps[:, t * 48:(t + 1) * 48], xT[:, k, t * P:(t + 1) * P], wgates[:, k, :], start=(k == 0), stop=(k == KD - 1))
                full(last, (1, "g"))
                pe.wait_ge(sem("ld_pos"), 64)
                ps = wait_free(pe, (1, "pos"))
                for i in range(2):
                    last = nc.tensor.transpose(ps[:, i * CBLK:(i + 1) * CBLK], pos_in[:, i, :], ident[0:CBLK, 0:CBLK])
                full(last, (1, "pos"))

                def rotate(name, raw, n):
                    wait_read(pe, (1, ("q0", "q1", "q2", "q3", "ks", "kw")[n - 1]))
                    ps = wait_free(pe, (1, name))
                    full(mm(ps[:, :], cst("rot"), raw, start=True, stop=True), (1, name))

                m0 = PIECE_MIX[1]
                proj_T(1, "q0", m0 + 0)
                proj_T(1, "q1", m0 + 1)
                rotate("rq0", silu[:, 0, :], 1)
                proj_T(1, "q2", m0 + 2)
                rotate("rq1", silu[:, 1, :], 2)
                proj_T(1, "q3", m0 + 3)
                rotate("rq2", silu[:, 0, :], 3)
                proj_T(1, "kc", m0 + 4)
                rotate("rq3", silu[:, 1, :], 4)
                proj_T(1, "vc", m0 + 5)
                proj_T(1, "ks", m0 + 6)
                proj_tok(1, "vs", m0 + 7)
                rotate("rks", silu[:, 0, :], 5)
                proj_T(1, "kw", m0 + 8)
                proj_tok(1, "vw", m0 + 9)
                rotate("rkw", silu[:, 1, :], 6)
                pe.wait_ge(sem("ld_cmpw"), 64)
                wait_read(pe, (1, "kc"))
                wait_read(pe, (1, "vc"))
                for par in range(2):
                    rows = slice(par * NDH, (par + 1) * NDH)
                    ps = wait_free(pe, (1, f"cmp{par}"))
                    for i in range(2):
                        for l in range(CBLK):
                            half, at = l // CSTR, l % CSTR
                            lo = at + half * CSTR
                            src = kp[rows, i, half, :, lo:lo + (NCMP - 1) * CSTR + 1:CSTR]
                            dst = ps[rows, i * 32:i * 32 + 2 * NCMP].rearrange("p (g c) -> p g c", g=2)
                            last = mm(dst, cmp_w[i][rows, l, :], src, start=(l == 0), stop=(l == CBLK - 1))
                    full(last, (1, f"cmp{par}"))
                for par in range(2):
                    wait_read(pe, (1, f"cmp{par}"))
                ps = wait_free(pe, (1, "kcrot"))
                full(mm(ps[:, 0:32], cst("rot"), kc_raw[:].rearrange("p g c -> p (g c)"), start=True, stop=True), (1, "kcrot"))
                ps = wait_free(pe, (1, "vcT"))
                for g in range(2):
                    last = nc.tensor.transpose(ps[:, g * P:(g + 1) * P], vrep_in[:, g].rearrange("p r c -> p (r c)"), ident)
                full(last, (1, "vcT"))
                pe.wait_ge(sem("kc_ready"), 1)
                for t in range(NT):
                    for par in range(2):
                        ps = wait_free(pe, (1, ("cs", t, par)))
                        for i in range(NH // 2):
                            h = (2 * (i // NJ) + par) * NJ + i % NJ
                            rows, pair, tile = head_rows(h)
                            last = mm(ps[:, i * 16:i * 16 + NCMP], qk[rows, tile, t * P:(t + 1) * P], kcT[rows, pair, 0:NCMP], start=True, stop=True)
                        full(last, (1, ("cs", t, par)))
                pe.wait_ge(sem("pc_ready"), 1)
                pcs = silu_flat.rearrange("p (t g c) -> p t g c", t=NT, g=NG)
                for t in range(NT):
                    ps = wait_free(pe, (1, ("pcT", t)))
                    for g in range(NG):
                        last = nc.tensor.transpose(ps[:, g * P:(g + 1) * P], pcs[:, t, g, :], ident)
                    full(last, (1, ("pcT", t)))
                wait_read(pe, (1, "vcT"))
                for t in range(NT):
                    wait_read(pe, (1, ("pcT", t)))
                for half in range(2):
                    for g in range(2 * half, 2 * half + 2):
                        for t in range(NT):
                            last = mm(acc[:, t, g * 256:(g + 1) * 256], pcT[:, t, g, :], v_blk[:, g].rearrange("p j e -> p (j e)"), start=True, stop=True)
                    last.then_inc(sem("pv_half"), 1)

                def u_scores(u):
                    h, br = u % NH, u // NH
                    rows, pair, tile = head_rows(h)
                    ps = wait_free(pe, (1, ("US", u)))
                    mm(ps[:, 0:P], qk[rows, tile, 0:P], kT_sw[rows, br, pair, 0:P], start=True, stop=True)
                    full(mm(ps[:, P:P + T], qk[rows, tile, P:T], kT_sw[rows, br, pair, :], start=True, stop=True), (1, ("US", u)))

                def u_turn(u):
                    pe.wait_ge(sem("u_exp"), u + 1)
                    ps = wait_free(pe, (1, ("UT", u)))
                    for c in range(3):
                        last = nc.tensor.transpose(ps[:, c * P:(c + 1) * P], u_p[u % 2][:, c * P:(c + 1) * P], ident)
                    full(last, (1, ("UT", u)))

                def u_values(u):
                    h, br = u % NH, u // NH
                    g = h // NJ
                    wait_read(pe, (1, ("UT", u)))
                    if h % 8 == 0:
                        pe.wait_ge(sem("o_half"), 2 * br + h // 8 + 1)
                    pt, vv = u_pT[u % 2], v_sw[:, br, :, g * NDH:(g + 1) * NDH]
                    mm(acc_h[:, 0, h, :], pt[:, 0:P], vv[:, 0, :], start=True, stop=True)
                    mm(acc_h[:, 1, h, :], pt[:, P:T], vv[:, 0, :], start=True, stop=False)
                    last = mm(acc_h[:, 1, h, :], pt[:, T:T + P], vv[:, 1, :], start=False, stop=True)
                    last.then_inc(sem("u_pv"), 1)

                for u in range(NUNIT + 1):
                    if u < NUNIT:
                        u_scores(u)
                    if u:
                        u_turn(u - 1)
                        if u > 1:
                            u_values(u - 2)
                u_values(NUNIT - 1)
                pe.wait_ge(sem("o_half"), 6)
                transposes(1, "nT", o_flat)
                for g in range(4):
                    wait_read(pe, (1, ("nT", g)))
                for j in range(4):
                    rows_to_acc(mixT, PIECE_OUT[1] + j, j, j == 0, j == 3)

            def tail(layer):
                pe.wait_ge(sem("ln_done"), 2 * layer + 1)
                transposes(layer, "xT", x[:])
                for g in range(4):
                    wait_read(pe, (layer, ("xT", g)))
                pe.wait_ge(sem("ld_router"), 32 * (layer + 1))
                ps = wait_free(pe, (layer, "logits"))
                for t in range(NT):
                    for k in range(KD):
                        last = mm(ps[:, t * NE:(t + 1) * NE], xT[:, k, t * P:(t + 1) * P], router[:, k, :], start=(k == 0), stop=(k == KD - 1))
                full(last, (layer, "logits"))
                n = PIECE_SH[layer]
                proj_T(layer, "sh_gate", n, True)
                proj_T(layer, "sh_up", n + 1, True)
                wait_read(pe, (layer, "sh_up"))
                pe.wait_ge(sem("acc_read"), 2 * layer + 1)
                hid_v = hid[:].rearrange("p b (f t) -> p b f t", f=2)
                rows_to_acc(hid_v[:, 1], n + 2, 0, True, True)
                pe.wait_ge(sem("cw_ready"), layer + 1)
                ps = wait_free(pe, (layer, "cwT"))
                for t in range(NT):
                    last = nc.tensor.transpose(ps[0:NE, t * P:(t + 1) * P], cw[:, t, :], ident)
                full(last, (layer, "cwT"))

                g0, n0 = LOOP_AT[layer], PIECE_LOOP[layer]
                uses = LOOP_GROUPS // NB_WORK
                with pe.Fori(0, N_BODIES) as i:
                    for j, (kind, e) in enumerate(BODY):
                        n = n0 + j
                        w = ring[:, n % RING, :]
                        pe.wait_ge(landed[n % RING], i * 16 + landed_value(n))
                        if kind == "d":
                            wv = w.rearrange("p (k c) -> p k c", k=2)
                            pe.wait_ge(sem("hid_ready"), i * EPB + (layer * (NE + 2) + e + 3))
                            for k in range(2):
                                for t in range(NT):
                                    for half in range(2):
                                        last = mm(acc[:, t, half * 512:(half + 1) * 512], hid_v[:, e % 2, k, t * P:(t + 1) * P],
                                                  wv[:, k, half * 512:(half + 1) * 512], start=False, stop=True, skip_group_check=True)
                            last.then_inc(rows_used, 1)
                        else:
                            g = g0 + 2 * e + (kind == "u")
                            wv = w.rearrange("p (k c) -> p k c", k=KD)
                            pe.wait_ge(bank_free[g % NB_WORK], i * uses + g // NB_WORK)
                            ps = work[g % NB_WORK]
                            for c in range(2):
                                for k in range(KD):
                                    last = mm(ps[:, c * T:(c + 1) * T], wv[:, k, c::2], xT[:, k, :], start=(k == 0), stop=(k == KD - 1))
                            last.then_inc(bank_full[g % NB_WORK], 1)

                pe.wait_ge(sem("ln_done"), 2 * layer + 2)
                transposes(layer, "xT2", x[:])
                pe.wait_ge(sem("ld_p"), 16 * (layer + 1))
                ps = wait_free(pe, (layer, "pT"))
                for k in range(2):
                    for t in range(NT):
                        c = (k * NT + t) * P
                        last = nc.tensor.transpose(ps[:, c:c + P], p_in[:, t, k::2], ident)
                full(last, (layer, "pT"))
                for g in range(4):
                    wait_read(pe, (layer, ("xT2", g)))
                wait_read(pe, (layer, "pT"))
                pe.wait_ge(sem("acc_read"), 2 * layer + 2)
                n = PIECE_PLE[layer]
                rows_to_acc(pT[:], n, 0, True, True)
                banks = [wait_free(pe, (layer, ("pg", q))) for q in range(4)]
                for j in range(4):
                    w = piece(n + 1 + j).rearrange("p (k c) -> p k c", k=2)
                    for i in range(2):
                        for q in range(4):
                            t, half = q // 2, q % 2
                            last = mm(banks[q][:, :], xT[:, 2 * j + i, t * P:(t + 1) * P], w[:, i, half * 512:(half + 1) * 512],
                                      start=(j == 0 and i == 0), stop=(j == 3 and i == 1))
                            if j == 3 and i == 1:
                                full(last, (layer, ("pg", q)))
                    if j < 3:
                        last.then_inc(rows_used, 1)

            mlstm()
            tail(0)
            nsa()
            tail(1)

        @block.scalar
        def _(act):
            af = nc.scalar.activation
            chain = Chain(act, sem("act_step"))

            def mlstm():
                act.wait_ge(sem("gabs"), 1)
                chain.step(af(gbuf[:, 2, :], gbuf[:, 2, :], ACT.Exp, scale=-1.0))
                af(gbuf[:, 2, :], gbuf[:, 2, :], ACT.Ln, bias=1.0).then_inc(sem("glog"), 1)
                act.wait_ge(sem("gneg"), 1)
                af(gbuf[:, 6, :], gbuf[:, 6, :], ACT.Exp).then_inc(sem("grows"), 1)
                for g in range(4):
                    wait_read(act, (0, ("qk", g)))
                    v = qk[:, 2 * g:2 * g + 2, :]
                    af(v, v, ACT.Silu).then_inc(sem("qk_ready"), 1)
                for h in range(MH):
                    wait_read(act, (0, ("B", h // 2)))
                    af(decay(h), decay(h), ACT.Exp).then_inc(sem("decay_ready"), 1)
                for g in range(4):
                    ps = wait_full(act, (0, ("v", g)))
                    src = ps[:, :].rearrange("p (t h e) -> p t h e", t=NT, h=2)
                    for t in range(NT):
                        last = nc.scalar.copy(v_aug[:, t, 2 * g:2 * g + 2, 0:MDV], src[:, t])
                    free(last, (0, ("v", g)))
                for g in range(4):
                    ps = wait_full(act, (0, ("o", g)))
                    src = ps[:, :].rearrange("p (t c) -> p t c", t=NT)
                    free(af(sig_o[:, :, g * 256:(g + 1) * 256], src, ACT.Sigmoid), (0, ("o", g)))
                act.wait_ge(sem("hvar"), 1)
                af(hmv[:, :, :, 1], hmv[:, :, :, 1], ACT.Sqrt).then_inc(sem("hstd"), 1)

            def norm(n):
                act.wait_ge(sem("ln_var"), n)
                af(lnmv[:, :, 1], lnmv[:, :, 1], ACT.Sqrt).then_inc(sem("ln_std"), 1)

            def nsa():
                ps = wait_full(act, (1, "g"))
                free(af(gsig[:].rearrange("p t h c -> p t (h c)"), ps[:, 0:96].rearrange("p (t c) -> p t c", t=NT), ACT.Sigmoid), (1, "g"))
                for n, name in enumerate(("q0", "q1", "q2", "q3", "ks", "kw")):
                    ps = wait_full(act, (1, name))
                    if n >= 2:
                        act.wait_ge(sem("rope_done"), n - 1)
                    free(nc.scalar.copy(silu[:, n % 2, :], ps[:, :]), (1, name))
                    if name in ("ks", "kw"):
                        v = "vs" if name == "ks" else "vw"
                        ps = wait_full(act, (1, v))
                        free(nc.scalar.copy(v_sw[:, name == "kw"].rearrange("p t c -> p (t c)"), ps[:, :]), (1, v))
                act.wait_ge(sem("cs_ready"), 1)
                af(cs_s[:, :, :, 0:NCMP], cs_s[:, :, :, 0:NCMP], ACT.Exp, scale=NDH ** -0.5).then_inc(sem("cs_exp"), 1)
                for t in range(NT):
                    ps = wait_full(act, (1, ("pcT", t)))
                    free(nc.scalar.copy(pcT[:, t].rearrange("p g c -> p (g c)"), ps[:, :]), (1, ("pcT", t)))

                def turned(u):
                    ps = wait_full(act, (1, ("UT", u)))
                    if u >= 2:
                        act.wait_ge(sem("u_pv"), u - 1)
                    free(nc.scalar.copy(u_pT[u % 2], ps[:, 0:384]), (1, ("UT", u)))

                for u in range(NUNIT):
                    act.wait_ge(sem("u_max"), u + 1)
                    if u == 0:
                        act.wait_ge(sem("pcs_read"), 1)
                    if u >= 2:
                        wait_full(act, (1, ("UT", u - 2)))
                    h = u % NH
                    if h % 8 == 0:
                        act.wait_ge(sem("o_half"), 2 * (u // NH) + h // 8)
                    s, p = u_s[u % 2], u_p[u % 2]
                    af(p[:, 0:P], s[:, 0:P], ACT.Exp, scale=NDH ** -0.5, bias=nmax[:, u % 2, 0:1], accum_out=nden[:, 0, h:h + 1])
                    af(p[:, P:P + T], s[:, P:P + T], ACT.Exp, scale=NDH ** -0.5, bias=nmax[:, u % 2, 1:2],
                       accum_out=nden[:, 1, h:h + 1]).then_inc(sem("u_exp"), 1)
                    if u:
                        turned(u - 1)
                turned(NUNIT - 1)

            def tail(layer):
                ps = wait_full(act, (layer, "logits"))
                free(af(score[:].rearrange("p t e -> p (t e)"), ps[:, 0:NT * NE], ACT.Sigmoid), (layer, "logits"))
                ps = wait_full(act, (layer, "sh_gate"))
                free(af(silu[:, 1, :], ps[:, :], ACT.Silu), (layer, "sh_gate"))
                wait_read(act, (layer, "sh_up"))
                g0, uses = LOOP_AT[layer], LOOP_GROUPS // NB_WORK
                with act.Fori(0, N_BODIES) as i:
                    for e in range(EPB):
                        g = g0 + 2 * e
                        act.wait_ge(bank_full[g % NB_WORK], i * uses + (g // NB_WORK + 1))
                        act.wait_ge(sem("hid_ready"), i * EPB + (layer * (NE + 2) + e + 1))
                        af(silu[:, e % 2, :], work[g % NB_WORK][:, :], ACT.Silu).then_inc(bank_free[g % NB_WORK], 1)
                norm(2 * layer + 2)
                for q in range(4):
                    ps = wait_full(act, (layer, ("pg", q)))
                    free(af(sig_o[:, q // 2, (q % 2) * 512:(q % 2 + 1) * 512], ps[:, :], ACT.Sigmoid), (layer, ("pg", q)))

            mlstm()
            norm(1)
            tail(0)
            nsa()
            norm(3)
            tail(1)

        @block.vector
        def _(dve):
            chain = Chain(dve, sem("dve_step"))
            step = chain.step
            copy, ts, tt, stt = nc.vector.tensor_copy, nc.vector.tensor_scalar, nc.vector.tensor_tensor, nc.vector.scalar_tensor_tensor

            def copies_T(layer, name, dst):
                for g in range(4):
                    ps = wait_full(dve, (layer, (name, g)))
                    free(copy(dst[:, 2 * g:2 * g + 2, :].rearrange("p k t -> p (k t)"), ps[:, :]), (layer, (name, g)))

            def mlstm():
                copies_T(0, "x0T", xT)
                step(nc.vector.memset(gbuf[:, 7, :], 1.0))
                ps = wait_full(dve, (0, "gates"))
                dve.wait_ge(sem("ld_gbias"), 32)
                ts(gbuf[:, 0, :], ps[0:MH, 0:T], gbias[:, 0:1], None, ALU.add)
                free(ts(gbuf[:, 1, :], ps[0:MH, T:2 * T], gbias[:, 1:2], None, ALU.add), (0, "gates"))
                wait_read(dve, (0, "gates"))
                stt(gbuf[:, 2, :], gbuf[:, 1, :], -1.0, gbuf[:, 1, :], ALU.mult, ALU.max).then_inc(sem("gabs"), 1)
                dve.wait_ge(sem("glog"), 1)
                step(stt(gbuf[:, 1, :], gbuf[:, 1, :], 0.0, gbuf[:, 2, :], ALU.min, ALU.subtract))
                step(nc.vector.tensor_tensor_scan(gbuf[:, 3, :], gbuf[:, 7, :], gbuf[:, 1, :], 0.0, ALU.mult, ALU.add))
                step(tt(gbuf[:, 4, :], gbuf[:, 0, :], gbuf[:, 3, :], ALU.subtract))
                step(nc.vector.tensor_tensor_scan(gbuf[:, 5, :], gbuf[:, 4, :], gbuf[:, 4, :], 0.0, ALU.max, ALU.max))
                step(stt(gbuf[:, 6, :], gbuf[:, 3, :], -1.0, gbuf[:, 5, :], ALU.mult, ALU.subtract))
                ts(gbuf[:, 5, :], gbuf[:, 5, :], -1.0, None, ALU.mult).then_inc(sem("gneg"), 1)
                ps = wait_full(dve, (0, "convT"))
                free(copy(conv_w[:], ps[:, 0:32]), (0, "convT"))
                wait_read(dve, (0, "convT"))
                for g in range(4):
                    ps = wait_full(dve, (0, ("qk", g)))
                    for c in range(2):
                        ch = 2 * g + c
                        y, src = qk[:, ch, :], ps[:, c * T:(c + 1) * T]
                        step(ts(y, src, conv_w[:, 3 * 8 + ch:3 * 8 + ch + 1], None, ALU.mult))
                        for back in range(1, MCONV):
                            j = (MCONV - 1 - back) * 8 + ch
                            last = stt(y[:, back:T], src[:, 0:T - back], conv_w[:, j:j + 1], y[:, back:T], ALU.mult, ALU.add)
                            if back < MCONV - 1:
                                step(last)
                    free(last, (0, ("qk", g)))
                ps = wait_full(dve, (0, "gateT"))
                free(copy(gtok[:].rearrange("p a h -> p (a h)"), ps[:, 0:4 * MH]), (0, "gateT"))
                wait_read(dve, (0, "gateT"))
                for g in range(4):
                    ps = wait_full(dve, (0, ("B", g)))
                    for i in range(2):
                        h = 2 * g + i
                        d = decay(h)
                        stt(d[:, 0:T], ps[:, i * T:(i + 1) * T], gtok[:, 0, h:h + 1], cst("mask_st"), ALU.add, ALU.min)
                        last = stt(d[:, T:T + P], ps[:, i * T + P:(i + 1) * T], gtok[:, 1, h:h + 1], cst("mask_st")[:, 0:P], ALU.add, ALU.min)
                    free(last, (0, ("B", g)))

                def weighted(h):
                    ps = wait_full(dve, (0, ("S", h)))
                    dve.wait_ge(sem("decay_ready"), h + 1)
                    free(stt(pt_m[h % 2], ps[:, 0:384], MDK ** -0.5, decay(h), ALU.mult, ALU.mult), (0, ("S", h)))

                weighted(0)
                for h in range(MH):
                    if h + 1 < MH:
                        weighted(h + 1)
                    ps = wait_full(dve, (0, ("num", h)))
                    v = ps[:, :].rearrange("p (t e) -> p t e", t=NT)
                    step(copy(den2[:], v[:, :, MDV]))
                    step(stt(den2[:], den2[:], -1.0, den2[:], ALU.mult, ALU.max))
                    step(tt(den2[:], den2[:], gtok[:, 2:4, h], ALU.max))
                    step(nc.vector.reciprocal(den2[:], den2[:]))
                    for t in range(NT):
                        last = ts(hm[:, t, h, :], v[:, t, 0:MDV], den2[:, t:t + 1], None, ALU.mult)
                    free(last, (0, ("num", h)))
                    wait_read(dve, (0, ("num", h)))
                    for t in range(NT):
                        step(nc.vector.bn_stats(hst[:], hm[:, t, h, :]))
                        step(nc.vector.bn_aggr(hmv[:, t, h, :], hst[:]))
                ts(hmv[:, :, :, 1], hmv[:, :, :, 1], EPS, None, ALU.add).then_inc(sem("hvar"), 1)
                dve.wait_ge(sem("hstd"), 1)
                step(nc.vector.reciprocal(hmv[:, :, :, 1], hmv[:, :, :, 1]))
                for h in range(MH):
                    for t in range(NT):
                        last = ts(hm[:, t, h, :], hm[:, t, h, :], hmv[:, t, h, 0:1], hmv[:, t, h, 1:2], ALU.subtract, ALU.mult)
                step(last)
                dve.wait_ge(sem("ld_norm"), 16)
                for t in range(NT):
                    last = tt(hm_flat[:, t, :], hm_flat[:, t, :], ln_p[:, 0, :], ALU.mult)
                step(last, sem("norm_g_used"))
                for g in range(4):
                    wait_read(dve, (0, ("o", g)))
                tt(bufD[:], bufD[:], bufC[:], ALU.mult).then_inc(sem("mix_ready"), 1)
                copies_T(0, "mT", mixT)

            def norm(n):
                layer, k = (n - 1) // 2, (n - 1) % 2
                dve.wait_ge(rows_used, ROWS_BEFORE_LOOP[layer] + (NE if k else -1))
                for t in range(NT):
                    last = stt(z[:, t, :], x[:, t, :], ALPHA, acc[:, t, :], ALU.mult, ALU.add)
                step(last, sem("acc_read"))
                for t in range(NT):
                    for half in range(2):
                        last = nc.vector.bn_stats(lnst[:, t, half, :], z[:, t, half * 512:(half + 1) * 512])
                step(last)
                for t in range(NT):
                    last = nc.vector.bn_aggr(lnmv[:, t, :], lnst[:, t].rearrange("p a b -> p (a b)"))
                step(last)
                ts(lnmv[:, :, 1], lnmv[:, :, 1], EPS, None, ALU.add).then_inc(sem("ln_var"), 1)
                dve.wait_ge(sem("ln_std"), n)
                step(nc.vector.reciprocal(lnmv[:, :, 1], lnmv[:, :, 1]))
                dve.wait_ge(sem("ld_ln"), 32 * n)
                for t in range(NT):
                    step(ts(z[:, t, :], z[:, t, :], lnmv[:, t, 0:1], lnmv[:, t, 1:2], ALU.subtract, ALU.mult))
                for t in range(NT):
                    step(tt(z[:, t, :], z[:, t, :], ln_p[:, 0, :], ALU.mult))
                for t in range(NT):
                    last = tt(x[:, t, :], z[:, t, :], ln_p[:, 1, :], ALU.add)
                step(last, sem("ln_done"))

            def choose(layer):
                wait_read(dve, (layer, "logits"))
                dve.wait_ge(sem("ld_router"), 32 * (layer + 1))
                for t in range(NT):
                    last = tt(biased[:, t, :], score[:, t, :], rbias[:], ALU.add)
                step(last)
                for t in range(NT):
                    for g in range(NEG):
                        last = nc.vector.max(grp8[:, t * NEG + g, :], biased[:, t, g * 8:(g + 1) * 8])
                step(last)
                step(tt(grp[:], grp8[:, :, 0], grp8[:, :, 1], ALU.add))
                g3 = grp[:].rearrange("p (t g) -> p t g", t=NT)
                for t in range(NT):
                    other = g3[:, t, :].unsqueeze(1).to_broadcast([P, NEG, NEG])
                    own = g3[:, t, :].unsqueeze(2).to_broadcast([P, NEG, NEG])
                    tt(gcmp[:, t], other, own, ALU.is_gt)
                    last = tt(geq[:, t], other, own, ALU.is_equal)
                step(last)
                for t in range(NT):
                    last = tt(geq[:, t], geq[:, t], cst("before").rearrange("p (a b) -> p a b", a=NEG), ALU.mult)
                step(last)
                step(tt(gcmp[:], gcmp[:], geq[:], ALU.add))
                step(nc.vector.reduce_sum(rank[:], gcmp[:].rearrange("p t a b -> p (t a) b"), axis=AX.X))
                step(ts(grp[:], rank[:], float(TOPG) - 0.5, None, ALU.is_lt))
                e3 = [v[:].rearrange("p t (g e) -> p (t g) e", g=NEG) for v in (biased, cand)]
                step(ts(rank[:], grp[:], BIG, -BIG, ALU.mult, ALU.add))
                step(tt(e3[0], e3[0], grp[:].unsqueeze(2).to_broadcast([P, NT * NEG, 8]), ALU.mult))
                step(tt(e3[0], e3[0], rank[:].unsqueeze(2).to_broadcast([P, NT * NEG, 8]), ALU.add))
                for t in range(NT):
                    last = nc.vector.max(top8[:, t, :], biased[:, t, :])
                step(last)
                for t in range(NT):
                    last = nc.vector.match_replace(cand[:, t, :], top8[:, t, :], biased[:, t, :], -3e38)
                step(last)
                step(tt(cand[:], cand[:], biased[:], ALU.not_equal))
                step(tt(cw[:], cand[:], score[:], ALU.mult))
                step(nc.vector.reduce_sum(rsum[:], cw[:], axis=AX.X))
                step(nc.vector.reciprocal(rsum[:], rsum[:]))
                for t in range(NT):
                    last = ts(cw[:, t, :], cw[:, t, :], rsum[:, t:t + 1], SCALE_R, ALU.mult, ALU.mult)
                last.then_inc(sem("cw_ready"), 1)

            def nsa():
                copies_T(1, "x1T", xT)
                ps = wait_full(dve, (1, "pos"))
                free(copy(posT[:].rearrange("p i l -> p (i l)"), ps[:, 0:2 * CBLK]), (1, "pos"))
                wait_read(dve, (1, "pos"))
                cos2 = cst("cos").unsqueeze(1).to_broadcast([P, 2, T])
                sin2 = cst("sin").unsqueeze(1).to_broadcast([P, 2, T])

                def rope(n, name, dst):
                    ps = wait_full(dve, (1, name))
                    raw = silu[:, n % 2, :].rearrange("p (c t) -> p c t", c=2)
                    tmp = hid[:, n % 2, :].rearrange("p (c t) -> p c t", c=2)
                    tt(dst, raw, cos2, ALU.mult)
                    free(tt(tmp, ps[:, :].rearrange("p (c t) -> p c t", c=2), sin2, ALU.mult), (1, name))
                    wait_read(dve, (1, name))
                    last = tt(dst, dst, tmp, ALU.add)
                    step(last, sem("rope_done"))

                def with_positions(i, name):
                    ps = wait_full(dve, (1, name))
                    for half in range(2):
                        for g in range(2):
                            src = ps[:, g * T:(g + 1) * T].rearrange("p (c l) -> p c l", l=CSTR)
                            pos = posT[:, i, half * CSTR:(half + 1) * CSTR].unsqueeze(1).to_broadcast([P, T // CSTR, CSTR])
                            last = tt(kp[:, i, half, g, :].rearrange("p (c l) -> p c l", l=CSTR), src, pos, ALU.add)
                    free(last, (1, name))

                rope(0, "rq0", qk[:, 0:2, :])
                rope(1, "rq1", qk[:, 2:4, :])
                rope(2, "rq2", qk[:, 4:6, :])
                with_positions(0, "kc")
                rope(3, "rq3", qk[:, 6:8, :])
                with_positions(1, "vc")
                rope(4, "rks", kT_sw[:, 0])
                rope(5, "rkw", kT_sw[:, 1])
                step(nc.vector.memset(kc_raw[:], 0.0))
                step(nc.vector.memset(vrep_in[:], 0.0))
                step(nc.vector.memset(silu[:], 0.0))
                for par in range(2):
                    rows = slice(par * NDH, (par + 1) * NDH)
                    ps = wait_full(dve, (1, f"cmp{par}"))
                    copy(kc_raw[rows, :, 0:NCMP], ps[rows, 0:2 * NCMP].rearrange("p (g c) -> p g c", g=2))
                    for g in range(2):
                        v = ps[rows, 32 + g * NCMP:32 + (g + 1) * NCMP].unsqueeze(1).to_broadcast([NDH, 4, NCMP])
                        last = copy(vrep_in[rows, g, :, 0:NCMP], v)
                    free(last, (1, f"cmp{par}"))
                    wait_read(dve, (1, f"cmp{par}"))
                ps = wait_full(dve, (1, "kcrot"))
                cc = cst("cos_c").unsqueeze(1).to_broadcast([P, 2, 16])
                sc = cst("sin_c").unsqueeze(1).to_broadcast([P, 2, 16])
                free(tt(kc_t[:], ps[:, 0:32].rearrange("p (g c) -> p g c", g=2), sc, ALU.mult), (1, "kcrot"))
                wait_read(dve, (1, "kcrot"))
                step(tt(kcT[:], kc_raw[:], cc, ALU.mult))
                tt(kcT[:], kcT[:], kc_t[:], ALU.add).then_inc(sem("kc_ready"), 1)
                step(nc.vector.memset(v_blk[:], 0.0))
                ps = wait_full(dve, (1, "vcT"))
                for g in range(NG):
                    for j in range(NJ):
                        rows = slice(32 * j, 32 * (j + 1))
                        last = copy(v_blk[rows, g, j, :], ps[rows, g * NDH:(g + 1) * NDH])
                free(last, (1, "vcT"))
                madd = cst("cmask_add").rearrange("p (t c) -> p t c", t=NT)
                mmul = cst("cmask_mul").rearrange("p (t c) -> p t c", t=NT)
                for t in range(NT):
                    for par in range(2):
                        ps = wait_full(dve, (1, ("cs", t, par)))
                        for pair in range(2):
                            h = (2 * pair + par) * NJ
                            src = ps[:, pair * 64:(pair + 1) * 64].rearrange("p (j c) -> p j c", j=NJ)[:, :, 0:NCMP]
                            mk = madd[:, t, 0:NCMP].unsqueeze(1).to_broadcast([P, NJ, NCMP])
                            last = tt(cs_s[:, t, h:h + NJ, 0:NCMP], src, mk, ALU.add)
                        free(last, (1, ("cs", t, par)))
                        wait_read(dve, (1, ("cs", t, par)))
                step(nc.vector.reduce_max(cst16[:], cs_s[:, :, :, 0:NCMP], axis=AX.X))
                for t in range(NT):
                    last = tt(cs_s[:, t, :, 0:NCMP], cs_s[:, t, :, 0:NCMP], cst16[:, t, :].unsqueeze(2).to_broadcast([P, NH, NCMP]), ALU.subtract)
                step(last, sem("cs_ready"))
                dve.wait_ge(sem("cs_exp"), 1)
                for t in range(NT):
                    mk = mmul[:, t, 0:NCMP].unsqueeze(1).to_broadcast([P, NH, NCMP])
                    last = tt(cs_s[:, t, :, 0:NCMP], cs_s[:, t, :, 0:NCMP], mk, ALU.mult)
                step(last)
                step(nc.vector.reduce_sum(cst16[:], cs_s[:, :, :, 0:NCMP], axis=AX.X))
                step(ts(cst16[:], cst16[:], 1e-30, None, ALU.max))
                step(nc.vector.reciprocal(cst16[:], cst16[:]))
                for t in range(NT):
                    last = tt(cs_p[:, t, :, 0:NCMP], cs_s[:, t, :, 0:NCMP], cst16[:, t, :].unsqueeze(2).to_broadcast([P, NH, NCMP]), ALU.mult)
                last.then_inc(sem("pc_ready"), 1)

                def gather_half(br, half):
                    hs = slice(8 * half, 8 * half + 8)
                    if br == 0:
                        dve.wait_ge(sem("pv_half"), half + 1)
                    else:
                        dve.wait_ge(sem("u_pv"), NH * (br - 1) + 8 * (half + 1))
                    for t in range(NT):
                        if br == 0:
                            s = gsig[:, t, hs, 0]
                        else:
                            step(nc.vector.reciprocal(nden[:, t, hs], nden[:, t, hs]))
                            step(tt(cst16[:, t, hs], nden[:, t, hs], gsig[:, t, hs, br], ALU.mult))
                            s = cst16[:, t, hs]
                        s = s.unsqueeze(2).to_broadcast([P, 8, NDH])
                        if br == 0:
                            last = tt(o_v[:, t, hs, :], acc_h[:, t, hs, :], s, ALU.mult)
                        else:
                            tmp = hid_flat[:, 0:512].rearrange("p (h e) -> p h e", h=8)
                            step(tt(tmp, acc_h[:, t, hs, :], s, ALU.mult))
                            last = tt(o_v[:, t, hs, :], o_v[:, t, hs, :], tmp, ALU.add)
                        step(last, sem("o_half") if t == NT - 1 else None)

                gather_half(0, 0)
                gather_half(0, 1)
                dve.wait_ge(sem("pv_half"), 2)
                for t in range(NT):
                    wait_full(dve, (1, ("pcT", t)))
                step(nc.vector.memset(nmax[:], 0.0), sem("pcs_read"))
                for u in range(NUNIT):
                    ps = wait_full(dve, (1, ("US", u)))
                    if u >= 2:
                        dve.wait_ge(sem("u_exp"), u - 1)
                    s = u_s[u % 2]
                    free(tt(s, ps[:, 0:384], cst("mask_ts"), ALU.add), (1, ("US", u)))
                    wait_read(dve, (1, ("US", u)))
                    nc.vector.reduce_max(nmax[:, u % 2, 0:1], s[:, 0:P], axis=AX.X, negate=True)
                    step(nc.vector.reduce_max(nmax[:, u % 2, 1:2], s[:, P:P + T], axis=AX.X, negate=True))
                    ts(nmax[:, u % 2, :], nmax[:, u % 2, :], NDH ** -0.5, None, ALU.mult).then_inc(sem("u_max"), 1)
                    if u >= 10 and (u - 10) % 8 == 0:
                        gather_half(1 + (u - 10) // NH, ((u - 10) // 8) % 2)
                gather_half(2, 1)
                copies_T(1, "nT", mixT)

            def tail(layer):
                copies_T(layer, "xT", xT)
                choose(layer)
                ps = wait_full(dve, (layer, "sh_up"))
                wait_read(dve, (layer, "sh_gate"))
                free(tt(hid[:, 1, :], silu[:, 1, :], ps[:, :], ALU.mult), (layer, "sh_up"))
                ps = wait_full(dve, (layer, "cwT"))
                free(copy(cwT[:], ps[0:NE, 0:T]), (layer, "cwT"))
                nc.vector.memset(rsum[:], 0.0).then_inc(sem("hid_ready"), 2)
                g0, uses = LOOP_AT[layer], LOOP_GROUPS // NB_WORK
                with dve.Fori(0, N_BODIES) as i:
                    for e in range(EPB):
                        g = g0 + 2 * e + 1
                        dve.wait_ge(bank_full[g % NB_WORK], i * uses + (g // NB_WORK + 1))
                        dve.wait_ge(bank_free[(g - 1) % NB_WORK], i * uses + ((g - 1) // NB_WORK + 1))
                        s = silu[:, e % 2, :]
                        tt(s, s, work[g % NB_WORK][:, :], ALU.mult).then_inc(bank_free[g % NB_WORK], 1)
                        dve.wait_ge(rows_used, i * EPB + (ROWS_BEFORE_LOOP[layer] + e - 1))
                        dve.wait_ge(ld_cwb[e], i * 16 + (16 * layer * N_BODIES + 16))
                        dve.wait_ge(bank_free[g % NB_WORK], i * uses + (g // NB_WORK + 1))
                        s3 = s.rearrange("p (f t) -> p f t", f=2)
                        h3 = hid[:, e % 2, :].rearrange("p (f t) -> p f t", f=2)
                        w3 = cw_b[:, e, :].unsqueeze(1).to_broadcast([P, 2, T])
                        last = tt(h3, s3, w3, ALU.mult)
                        last.then_inc(sem("hid_ready"), 1)
                norm(2 * layer + 2)
                copies_T(layer, "xT2", xT)
                ps = wait_full(dve, (layer, "pT"))
                free(copy(pT[:].rearrange("p k t -> p (k t)"), ps[:, :]), (layer, "pT"))
                dve.wait_ge(rows_used, ROWS_BEFORE_LOOP[layer] + NE + 1)
                for q in range(4):
                    t, c = q // 2, slice((q % 2) * 512, (q % 2 + 1) * 512)
                    wait_read(dve, (layer, ("pg", q)))
                    step(tt(z[:, t, c], sig_o[:, t, c], acc[:, t, c], ALU.mult))
                    last = tt(x[:, t, c], x[:, t, c], z[:, t, c], ALU.add)
                step(last, sem("ple_done"))

            mlstm()
            norm(1)
            tail(0)
            nsa()
            norm(3)
            tail(1)


_INS = ["x", "p", "ln_g", "ln_b", "mlstm_w_in", "mlstm_conv", "mlstm_ig_bias", "mlstm_fg_bias", "mlstm_norm_g",
        "mlstm_w_out", "nsa_w_in", "nsa_cmp_pos_k", "nsa_cmp_pos_v", "nsa_cmp_wk", "nsa_cmp_wv", "nsa_w_out",
        "router_w", "router_bias", "exp_w_gate", "exp_w_up", "exp_w_down", "sh_w_gate", "sh_w_up", "sh_w_down",
        "ple_w", "ple_gate_w"]


def kernel(**inputs):
    import concourse.bacc as _bacc
    from concourse.bass_utils import run_bass_kernel_spmd as _run

    nc = _bacc.Bacc("TRN2", target_bir_lowering=False, num_devices=1)
    arrays, aps = {}, {}
    for name in _INS:
        arr = np.ascontiguousarray(inputs[name])
        arrays[f"in_{name}"] = arr
        aps[name] = nc.dram_tensor(f"in_{name}", arr.shape, mybir.dt.from_np(arr.dtype), kind="ExternalInput").ap()
    arrays["consts"] = CONSTS
    aps["consts"] = nc.dram_tensor("consts", CONSTS.shape, F32, kind="ExternalInput").ap()
    out = nc.dram_tensor("out_0", (1, T, D), F32, kind="ExternalOutput").ap()
    build(nc, aps, out)
    r = _run(nc, [arrays], core_ids=[0])
    return r.results[0]["out_0"]
```

```python
from contextlib import ExitStack

import numpy as np
import concourse.bass as bass
from concourse import mybir

F32 = mybir.dt.float32
BF16 = mybir.dt.bfloat16
I32 = mybir.dt.int32
ALU = mybir.AluOpType
ACT = mybir.ActivationFunctionType
AX = mybir.AxisListType

P = 128
D = 1024
T = 256
NT = T // P
KD = D // P
DEPTH = 2
ALPHA = (2.0 * DEPTH) ** 0.25
EPS = 1e-5
BIG = 1e30

MH, MDK, MDV, MCONV = 8, 64, 128, 4
NH, NG, NDH = 16, 4, 64
NJ = NH // NG
CSTR, CBLK = 16, 32
NCMP = T // CSTR - 1
NE, TOPK, NEG, TOPG, FF = 64, 8, 8, 4, 256
SCALE_R = 2.5
PLE = 256

SLOT = 2048
RING = 12
EPB = 4
CAP = 64
NBLK = T // CAP
NE_PAD = NE + 2
MORE = 32
NB_WORK = 4


def tail_groups(layer):
    before = [("xT", g) for g in range(4)] + ["logits", "sh_gate", "sh_up", "rank", "xgL", "xgH"]
    after = [("xT2", g) for g in range(4)] + ["pT"] + [("pg", q) for q in range(4)]
    return [(layer, g) for g in before], [(layer, g) for g in after]


def mlstm_groups():
    heads = [("S", 0)]
    for h in range(MH):
        heads += ([("S", h + 1)] if h + 1 < MH else []) + [("num", h)]
    return ([("x0T", g) for g in range(4)] + ["gates", "convT"] + [("qk", g) for g in range(4)] + ["gateT"]
            + [("B", g) for g in range(4)] + [("v", g) for g in range(4)] + [("o", g) for g in range(4)]
            + heads + [("mT", g) for g in range(4)])


def nsa_groups():
    units = []
    for u in range(NUNIT + 1):
        units += ([("US", u)] if u < NUNIT else []) + ([("UT", u - 1)] if u else [])
    return ([("x1T", g) for g in range(4)] + ["g", "pos"]
            + ["q0", "q1", "rq0", "q2", "rq1", "q3", "rq2", "kc", "rq3", "vc", "ks", "vs", "rks", "kw", "vw", "rkw"]
            + ["cmp0", "cmp1", "kcrot", "vcT"] + [("cs", t, par) for t in range(NT) for par in range(2)]
            + [("pcT", 0), ("pcT", 1)] + units + [("nT", g) for g in range(4)])


NUNIT = 2 * NH
BODY_GROUPS = [("gu", 0), ("gu", 1), ("xgL", 1), ("xgH", 1), ("y", 0, 0), ("y", 0, 1),
               ("gu", 2), ("gu", 3), ("y", 1, 0), ("y", 1, 1), ("xgL", 0), ("xgH", 0)]
LOOP_GROUPS = len(BODY_GROUPS)
N_BODIES = NE // EPB

AT, LOOP_AT = {}, []
_n = 0
for _layer, _mixer in enumerate((mlstm_groups(), nsa_groups())):
    _before, _after = tail_groups(_layer)
    for _g in [(_layer, g) for g in _mixer] + _before:
        AT[_g] = _n
        _n += 1
    LOOP_AT.append(_n)
    _n += LOOP_GROUPS * N_BODIES
    for _g in _after:
        AT[_g] = _n
        _n += 1

PIECES_MIX = (12, 10)
LOOP_PIECES = 3 * EPB
PIECE_LOOP, PIECE_MIX, PIECE_OUT, PIECE_SH, PIECE_PLE = [], [], [], [], []
_n = 0
for _layer in range(DEPTH):
    PIECE_MIX.append(_n)
    _n += PIECES_MIX[_layer]
    PIECE_OUT.append(_n)
    _n += 4
    PIECE_SH.append(_n)
    _n += 3
    PIECE_LOOP.append(_n)
    _n += LOOP_PIECES * N_BODIES
    PIECE_PLE.append(_n)
    _n += 5


def landed_value(n):
    extra = sum(3 for m in range(PIECE_MIX[1], PIECE_MIX[1] + 4) if m <= n and m % RING == n % RING)
    return 16 * (n // RING + 1 + extra)


MORE_PIECE = [n + 5 for n in PIECE_PLE]


BODY = [("g", 0), ("u", 0), ("g", 1), ("u", 1), ("d", 0), ("d", 1), ("g", 2), ("u", 2), ("g", 3), ("u", 3), ("d", 2), ("d", 3)]

USED = {}
_rows = 0
ROWS_BEFORE_LOOP = []
for _layer in range(DEPTH):
    _names = ([("qk", g) for g in range(4)] + [("v", g) for g in range(4)] + [("o", g) for g in range(4)] if _layer == 0
              else ["q0", "q1", "q2", "q3", "kc", "vc", "ks", "vs", "kw", "vw"])
    for _j, _g in enumerate(_names):
        USED[PIECE_MIX[_layer] + _j] = ("bank", AT[(_layer, _g)])
    for _j in range(4):
        _rows += 1
        USED[PIECE_OUT[_layer] + _j] = ("rows", _rows)
    USED[PIECE_SH[_layer]] = ("bank", AT[(_layer, "sh_gate")])
    USED[PIECE_SH[_layer] + 1] = ("bank", AT[(_layer, "sh_up")])
    _rows += 1
    USED[PIECE_SH[_layer] + 2] = ("rows", _rows)
    ROWS_BEFORE_LOOP.append(_rows)
    for _i in range(N_BODIES):
        for _j, (_kind, _e) in enumerate(BODY):
            if _kind == "d" and _e % 2 == 0:
                _rows += 1
                _how = ("rows", _rows)
            else:
                _g = ("y", _e // 2, 1) if _kind == "d" else ("gu", _e)
                _how = ("bank", LOOP_AT[_layer] + _i * LOOP_GROUPS + BODY_GROUPS.index(_g))
            USED[PIECE_LOOP[_layer] + _i * LOOP_PIECES + _j] = _how
    for _j in range(4):
        _rows += 1
        USED[PIECE_PLE[_layer] + _j] = ("rows", _rows)
    USED[PIECE_PLE[_layer] + 4] = ("bank", AT[(_layer, ("pg", 3))])


CONST_COLS = {}


def constants():
    parts = []

    def add(name, a):
        a = np.asarray(a, np.float32).reshape(P, -1)
        at = sum(x.shape[1] for x in parts)
        CONST_COLS[name] = (at, at + a.shape[1])
        parts.append(a)

    idx = np.arange(P)
    add("ident", np.eye(P))
    rot = np.zeros((P, P))
    for m in range(P):
        if m % NDH < NDH // 2:
            rot[m + NDH // 2, m] = -1.0
        else:
            rot[m - NDH // 2, m] = 1.0
    add("rot", rot)
    tri_s = np.where(idx[:, None] <= idx[None, :], 0.0, -BIG)
    add("mask_st", np.concatenate([tri_s, np.zeros((P, P))], 1))
    add("mask_ts", np.concatenate([tri_s.T, np.zeros((P, P)), tri_s.T], 1))
    sel = np.zeros((P, MH, P))
    for h in range(MH):
        sel[h, h, :] = 1.0
    add("sel", sel)
    half = NDH // 2
    inv = (np.float32(10000.0) ** (-np.arange(half, dtype=np.float32) / np.float32(half))).astype(np.float32)

    def table(pos):
        ang = pos.astype(np.float32)[None, :] * inv[idx % half][:, None]
        return np.cos(ang.astype(np.float32)), np.sin(ang.astype(np.float32))

    cos, sin = table(np.arange(T))
    add("cos", cos)
    add("sin", sin)
    end = np.arange(CSTR) * CSTR + CBLK - 1
    cos, sin = table(end)
    add("cos_c", cos)
    add("sin_c", sin)
    t = idx[:, None, None] + P * np.arange(NT)[None, :, None]
    ok = end[None, None, :] <= t
    add("cmask_add", np.where(ok, 0.0, -BIG))
    add("cmask_mul", np.where(ok, 1.0, 0.0))
    add("iota", np.broadcast_to(np.arange(CAP)[None, :], (P, CAP)))
    add("earlier", idx[:, None] < idx[None, :])
    add("ones", np.ones((P, P)))
    b = np.arange(1, NBLK)[None, :]
    add("blk_floor", np.broadcast_to(CAP * b, (P, NE, NBLK - 1)))
    add("blk_id", np.broadcast_to(NBLK * np.arange(NE)[:, None] + b, (P, NE, NBLK - 1)))
    add("before", np.broadcast_to(np.arange(NEG)[None, :] < np.arange(NEG)[:, None], (P, NEG, NEG)))
    return np.concatenate(parts, 1)


CONSTS = constants()


class Chain:

    def __init__(self, eng, semaphore):
        self.eng, self.sem, self.n = eng, semaphore, {}

    def step(self, ins, semaphore=None):
        s = semaphore or self.sem
        self.n[str(s)] = n = self.n.get(str(s), 0) + 1
        ins.then_inc(s, 1)
        self.eng.wait_ge(s, n)


def build(nc, a, out):
    ctx = ExitStack()
    with ctx:
        def sb(name, shape, dt=F32):
            return ctx.enter_context(nc.sbuf_tensor(name, shape, dt))

        sems = {}

        def sem(name):
            if name not in sems:
                sems[name] = ctx.enter_context(nc.semaphore(name))
            return sems[name]

        ring = sb("ring", [P, RING, SLOT])
        x = sb("x", [P, NT, D])
        xT = sb("xT", [P, KD, T])
        z = sb("z", [P, NT, D])
        bufA = sb("bufA", [P, 2048])
        bufB = sb("bufB", [P, NT * MH * (MDV + 1)])
        bufC = sb("bufC", [P, 2048])
        bufD = sb("bufD", [P, 2048])
        ln_p = sb("ln_p", [P, 2, D])
        const = sb("const", [P, CONSTS.shape[1]])
        router = sb("router", [P, KD, NE])
        rbias = sb("rbias", [P, NE])
        silu = sb("silu", [P, 2, 512])
        hid = sb("hid", [P, 2, 512])
        cw_b = sb("cw_b", [P, EPB, T])
        p_in = sb("p_in", [P, NT, PLE])
        pT = sb("pT", [P, 2, T])
        wgates = sb("wgates", [P, KD, 48])
        onehot = sb("onehot", [P, NT, 2, CAP], BF16)
        weighted_1h = sb("weighted_1h", [P, NT, 2, CAP])
        scatter = sb("scatter", [P, T])
        slot_of = sb("slot_of", [P, NT, NE_PAD])
        more_cand = sb("more_cand", [P, NE, NBLK - 1])
        more_f = sb("more_f", [P, MORE])
        more_i = sb("more_i", [P, MORE], I32)
        more_blk = sb("more_blk", [P, MORE], I32)
        more_base = sb("more_base", [P, MORE])
        shifted = sb("shifted", [P, NT])
        score = sb("score", [P, NT, NE])
        biased = sb("biased", [P, NT, NE])
        cand = sb("cand", [P, NT, NE])
        cw = sb("cw", [P, NT, NE_PAD])
        top8 = sb("top8", [P, NT, 8])
        grp8 = sb("grp8", [P, NT * NEG, 8])
        grp = sb("grp", [P, NT * NEG])
        rank = sb("rank", [P, NT * NEG])
        gcmp = sb("gcmp", [P, NT, NEG, NEG])
        geq = sb("geq", [P, NT, NEG, NEG])
        rsum = sb("rsum", [P, NT])
        lnst = sb("lnst", [P, NT, 2, 6])
        lnmv = sb("lnmv", [P, NT, 2])
        conv_in = sb("conv_in", [32, P])
        conv_w = sb("conv_w", [P, 32])
        gbias = sb("gbias", [MH, 2])
        gtok = sb("gtok", [P, 4, MH])
        den2 = sb("den2", [P, 2])
        hmv = sb("hmv", [P, NT, MH, 2])
        hst = sb("hst", [P, 6])
        pos_in = sb("pos_in", [CBLK, 2, P])
        posT = sb("posT", [P, 2, CBLK])
        kc_raw = sb("kc_raw", [P, 2, 16])
        kcT = sb("kcT", [P, 2, 16])
        kc_t = sb("kc_t", [P, 2, 16])
        gsig = sb("gsig", [P, NT, NH, 3])
        cst16 = sb("cst16", [P, NT, NH])
        nden = sb("nden", [P, NT, NH])
        nmax = sb("nmax", [P, 2, NT])
        acc = ctx.enter_context(nc.psum_tensor("acc", [P, NT, D], F32))
        work = [ctx.enter_context(nc.psum_tensor(f"work{b}", [P, 512], F32)) for b in range(NB_WORK)]

        def cst(name):
            lo, hi = CONST_COLS[name]
            return const[:, lo:hi]

        ident = cst("ident")

        landed = [sem(f"landed{s}") for s in range(RING)]
        rows_used = sem("rows_used")
        bank_full = [sem(f"bank_full{b}") for b in range(NB_WORK)]
        bank_free = [sem(f"bank_free{b}") for b in range(NB_WORK)]
        loop_uses = LOOP_GROUPS // NB_WORK

        more_landed = [[sem(f"more_landed{layer}{k}") for k in "gud"] for layer in range(DEPTH)]
        more_done = [sem(f"more_done{layer}") for layer in range(DEPTH)]
        more = [{n: sem(f"more_{n}{layer}") for n in ("hot", "xg", "xg_read", "gu", "silu", "hid", "y", "y_read", "own")} for layer in range(DEPTH)]

        def loop_bank(layer, g):
            n = LOOP_AT[layer] + BODY_GROUPS.index(g)
            return n % NB_WORK, n // NB_WORK

        def loop_full(eng, layer, g, i):
            b, use = loop_bank(layer, g)
            eng.wait_ge(bank_full[b], i * loop_uses + (use + 1))
            return work[b]

        def loop_wait_free(pe, layer, g, i):
            b, use = loop_bank(layer, g)
            pe.wait_ge(bank_free[b], i * loop_uses + use)
            return work[b]

        def loop_read(eng, layer, g, i, last_body=False):
            b, use = loop_bank(layer, g)
            eng.wait_ge(bank_free[b], i * loop_uses + (use + 1 - (loop_uses if last_body else 0)))

        def full(ins, g):
            return ins.then_inc(bank_full[AT[g] % NB_WORK], 1)

        def wait_full(eng, g):
            eng.wait_ge(bank_full[AT[g] % NB_WORK], AT[g] // NB_WORK + 1)
            return work[AT[g] % NB_WORK]

        def free(ins, g):
            return ins.then_inc(bank_free[AT[g] % NB_WORK], 1)

        def wait_free(pe, g):
            if AT[g] >= NB_WORK:
                pe.wait_ge(bank_free[AT[g] % NB_WORK], AT[g] // NB_WORK)
            return work[AT[g] % NB_WORK]

        def wait_read(eng, g):
            eng.wait_ge(bank_free[AT[g] % NB_WORK], AT[g] // NB_WORK + 1)

        qk = bufA[:].rearrange("p (c t) -> p c t", c=8)
        v_aug = bufB[:].rearrange("p (t h e) -> p t h e", t=NT, h=MH)
        sig_o = bufC[:].rearrange("p (t c) -> p t c", t=NT)
        hm = bufD[:].rearrange("p (t h e) -> p t h e", t=NT, h=MH)
        hm_flat = bufD[:].rearrange("p (t c) -> p t c", t=NT)
        gbuf = bufD[0:MH, :].rearrange("p (r t) -> p r t", r=8)
        mixT = bufA[:].rearrange("p (k t) -> p k t", k=KD)
        z_flat = z[:].rearrange("p t c -> p (t c)")
        silu_flat = silu[:].rearrange("p b c -> p (b c)")
        hid_flat = hid[:].rearrange("p b c -> p (b c)")

        def decay(h):
            if h < 5:
                return z_flat[:, 384 * h:384 * (h + 1)]
            if h < 7:
                return silu_flat[:, 384 * (h - 5):384 * (h - 4)]
            return hid_flat[:, 0:384]

        pt_m = [hid_flat[:, 384:768], cw_b[:].rearrange("p e t -> p (e t)")[:, 0:384]]
        cmp_w = [z_flat.rearrange("p (l e) -> p l e", e=NDH), bufD[:].rearrange("p (l e) -> p l e", e=NDH)]
        kp = bufC[:].rearrange("p (v half g t) -> p v half g t", v=2, half=2, g=2)
        kT_sw = bufB[:, 0:1024].rearrange("p (s g t) -> p s g t", s=2, g=2)
        v_sw = bufB[:, 1024:2048].rearrange("p (s t c) -> p s t c", s=2, t=NT)
        o_flat = bufC[:].rearrange("p (t c) -> p t c", t=NT)
        o_v = bufC[:].rearrange("p (t h e) -> p t h e", t=NT, h=NH)
        acc_h = acc[:].rearrange("p t (h e) -> p t h e", h=NH)
        cs_s = hid_flat[:, 0:512].rearrange("p (t h c) -> p t h c", t=NT, h=NH)
        cs_p = silu_flat.rearrange("p (t h c) -> p t h c", t=NT, h=NH)
        vrep_in = cw_b[:].rearrange("p e t -> p (e t)")[:, 0:256].rearrange("p (g r c) -> p g r c", g=2, r=4)
        vrep = cw_b[:].rearrange("p e t -> p (e t)")[:, 256:512]
        v_blk = z_flat[:, 1024:2048].rearrange("p (g j e) -> p g j e", g=NG, j=NJ)
        pcT = bufD[:, 1024:2048].rearrange("p (t g c) -> p t g c", t=NT, g=NG)
        u_s = [z_flat[:, 0:384], z_flat[:, 384:768]]
        u_p = [silu_flat[:, 0:384], silu_flat[:, 384:768]]
        u_pT = [bufD[:, 0:384], bufD[:, 384:768]]

        def head_rows(h):
            g = h // NJ
            return slice((g % 2) * NDH, (g % 2 + 1) * NDH), g // 2, (g // 2) * NJ + h % NJ

        x_part = [bufA[:].bitcast(BF16).rearrange("p (s t d) -> p s t d", s=2, t=NT)[:, s] for s in range(2)]
        x_part.append(bufC[:].bitcast(BF16).rearrange("p (s t d) -> p s t d", s=2, t=NT)[:, 0])
        x_rest = bufD[:].rearrange("p (t d) -> p t d", t=NT)
        xg = z[:, 1, :].rearrange("p (k c) -> p k c", k=KD)
        y_sb = z[:, 0, :]
        sil_e = [silu[:, 0, 128 * b:128 * (b + 1)] for b in range(2)]
        hid_e = [hid[:, 0, 128 * b:128 * (b + 1)] for b in range(2)]

        block = ctx.enter_context(nc.Block())

        @block.sync
        def _(sp):
            def col(w, lo):
                return w.rearrange("(p k) n -> p k n", k=KD)[:, :, lo:lo + 256]

            def row(w, j, k=KD):
                return w.rearrange("(p k) n -> p k n", k=k)[:, 2 * j:2 * j + 2, :]

            def wait_slot(n, i=0):
                if n >= RING:
                    how, at = USED[n - RING]
                    if how == "rows":
                        sp.wait_ge(rows_used, i * (EPB // 2) + at)
                    else:
                        sp.wait_ge(bank_full[at % NB_WORK], i * (LOOP_GROUPS // NB_WORK) + (at // NB_WORK + 1))

            def load(n, src):
                wait_slot(n)
                dst = ring[:, n % RING, :].rearrange("p (k n) -> p k n", k=src.shape[1])
                sp.dma_start(dst, src).then_inc(landed[n % RING], 16)

            for layer in range(DEPTH):
                w_in = a["mlstm_w_in" if layer == 0 else "nsa_w_in"][0]
                w_out = a["mlstm_w_out" if layer == 0 else "nsa_w_out"][0]
                n0 = PIECE_MIX[layer]
                for j in range(PIECES_MIX[layer]):
                    if layer == 1 and j < 4:
                        wait_slot(n0 + j)
                        dst = ring[:, (n0 + j) % RING, :].rearrange("p (k c g n) -> p k c g n", k=KD, c=2, g=2)
                        for c in range(2):
                            for par in range(2):
                                lo = ((2 * (j // 2) + par) * NJ + (j % 2) * 2 + c) * NDH
                                src = w_in.rearrange("(p k) n -> p k n", k=KD)[:, :, lo:lo + NDH]
                                sp.dma_start(dst[:, :, c, par, :], src).then_inc(landed[(n0 + j) % RING], 16)
                    else:
                        load(n0 + j, col(w_in, 256 * j))
                for j in range(4):
                    load(PIECE_OUT[layer] + j, row(w_out, j))
                load(PIECE_SH[layer], col(a["sh_w_gate"][layer], 0))
                load(PIECE_SH[layer] + 1, col(a["sh_w_up"][layer], 0))
                load(PIECE_SH[layer] + 2, row(a["sh_w_down"][layer], 0, 2))
                n0 = PIECE_LOOP[layer]
                exp_w = {k: a[n][layer] for k, n in (("g", "exp_w_gate"), ("u", "exp_w_up"), ("d", "exp_w_down"))}
                for j, (kind, e) in enumerate(BODY):
                    wait_slot(n0 + j)
                    src = exp_w[kind][e].rearrange("(p k) n -> p (k n)", p=P)
                    sp.dma_start(ring[:, (n0 + j) % RING, :], src).then_inc(landed[(n0 + j) % RING], 16)
                with sp.Fori(0, N_BODIES - 1) as i:
                    for j, (kind, e) in enumerate(BODY):
                        wait_slot(n0 + LOOP_PIECES + j, i)
                        src = exp_w[kind][bass.ds(i * EPB + (EPB + e), 1)].rearrange("a (p k) n -> p (a k n)", p=P)
                        sp.dma_start(ring[:, (n0 + j) % RING, :], src).then_inc(landed[(n0 + j) % RING], 16)
                n0 = MORE_PIECE[layer]
                for j in range(3):
                    wait_slot(n0 + j)
                sp.wait_ge(more_done[layer], 1)
                with sp.Fori(0, MORE) as m:
                    block_id = sp.value_load(more_i[0:1, bass.ds(m, 1)], min_val=0, max_val=NE * NBLK - 1)
                    with sp.If(block_id > 0):
                        sp.wait_ge(more_done[layer], m + 1)
                        for j, kind in enumerate("gud"):
                            src = exp_w[kind][bass.ds(block_id // NBLK, 1)].rearrange("a (p k) n -> p (a k n)", p=P)
                            sp.dma_start(ring[:, (n0 + j) % RING, :], src).then_inc(more_landed[layer][j], 16)
                n0 = PIECE_PLE[layer]
                load(n0, row(a["ple_w"][layer], 0, 2))
                for j in range(4):
                    load(n0 + 1 + j, row(a["ple_gate_w"][layer], j))
                sp.wait_ge(sem("experts_done"), layer + 1)
            sp.wait_ge(sem("ple_done"), DEPTH)
            sp.dma_start(out[0].rearrange("(t p) d -> p t d", p=P), x[:]).then_inc(sem("stored"), 16)
            sp.wait_ge(sem("stored"), 16)

        @block.gpsimd
        def _(pool):
            pool.dma_start(x[:], a["x"][0].rearrange("(t p) d -> p t d", p=P)).then_inc(sem("ld_x"), 16)
            pool.dma_start(const[:], a["consts"]).then_inc(sem("ld_const"), 16)
            in_w = [a[n][0].rearrange("(p k) n -> p k n", k=KD) for n in ("mlstm_w_in", "nsa_w_in")]
            pool.dma_start(wgates[:, :, 0:16], in_w[0][:, :, 3072:3088]).then_inc(sem("ld_gw"), 16)
            pool.dma_start(conv_in[:], a["mlstm_conv"][0].rearrange("j (c q) -> (j c) q", q=P)).then_inc(sem("ld_conv"), 16)
            pool.dma_start(gbias[:, 0:1], a["mlstm_ig_bias"].rearrange("a h -> h a")).then_inc(sem("ld_gbias"), 16)
            pool.dma_start(gbias[:, 1:2], a["mlstm_fg_bias"].rearrange("a h -> h a")).then_inc(sem("ld_gbias"), 16)
            pool.memset(v_aug[:, :, :, MDV:MDV + 1], 1.0).then_inc(sem("ones_v"), 1)
            pool.dma_start(ln_p[:, 0, :], a["mlstm_norm_g"][0].partition_broadcast(P)).then_inc(sem("ld_norm"), 16)
            for layer in range(DEPTH):
                if layer:
                    pool.wait_ge(sem("cw_ready"), layer)
                pool.dma_start(router[:], a["router_w"][layer].rearrange("(p k) n -> p k n", k=KD)).then_inc(sem("ld_router"), 16)
                pool.dma_start(rbias[:], a["router_bias"][layer].partition_broadcast(P)).then_inc(sem("ld_router"), 16)
                if layer == 1:
                    wait_read(pool, (0, "gates"))
                    pool.dma_start(wgates[:], in_w[1][:, :, 2560:2608]).then_inc(sem("ld_gw"), 16)
                    for i, n in enumerate(("nsa_cmp_pos_k", "nsa_cmp_pos_v")):
                        for par in range(2):
                            pool.dma_start(pos_in[:, i, par * NDH:(par + 1) * NDH], a[n][0]).then_inc(sem("ld_pos"), 16)
                    pool.wait_ge(sem("ple_done"), 1)
                    for i, n in enumerate(("nsa_cmp_wk", "nsa_cmp_wv")):
                        for par in range(2):
                            dst = cmp_w[i][par * NDH:(par + 1) * NDH]
                            pool.dma_start(dst, a[n][0].rearrange("l d e -> d l e")).then_inc(sem("ld_cmpw"), 16)
                for k in range(2):
                    if layer or k:
                        pool.wait_ge(sem("ln_done"), 2 * layer + k)
                    else:
                        pool.wait_ge(sem("norm_g_used"), 1)
                    pool.dma_start(ln_p[:, 0, :], a["ln_g"][layer, k].partition_broadcast(P)).then_inc(sem("ld_ln"), 16)
                    pool.dma_start(ln_p[:, 1, :], a["ln_b"][layer, k].partition_broadcast(P)).then_inc(sem("ld_ln"), 16)
                    if k == 0:
                        if layer:
                            wait_read(pool, (0, "pT"))
                        pool.dma_start(p_in[:], a["p"][layer, 0].rearrange("(t p) d -> p t d", p=P)).then_inc(sem("ld_p"), 16)
                        pool.wait_ge(sem("x_part"), 3 * layer + 1)
                        tt = nc.gpsimd.tensor_tensor
                        tt(x_rest, x[:], x_part[0], ALU.subtract).then_inc(sem("x_rest"), 1)
                        pool.wait_ge(sem("x_part"), 3 * layer + 2)
                        tt(x_rest, x_rest, x_part[1], ALU.subtract).then_inc(sem("x_rest"), 1)

        @block.tensor
        def _(pe):
            mm = nc.tensor.matmul

            def transposes(layer, name, src):
                for g in range(4):
                    ps = wait_free(pe, (layer, (name, g)))
                    for kk in range(2):
                        for t in range(NT):
                            c = (kk * NT + t) * P
                            last = nc.tensor.transpose(ps[:, c:c + P], src[:, t, 2 * g + kk::KD], ident)
                    full(last, (layer, (name, g)))

            def piece(n):
                pe.wait_ge(landed[n % RING], landed_value(n))
                return ring[:, n % RING, :]

            def proj_T(layer, name, n, interleaved=False):
                w = piece(n).rearrange("p (k c) -> p k c", k=KD)
                ps = wait_free(pe, (layer, name))
                for c in range(2):
                    cols = slice(c, None, 2) if interleaved else slice(c * P, (c + 1) * P)
                    for k in range(KD):
                        last = mm(ps[:, c * T:(c + 1) * T], w[:, k, cols], xT[:, k, :], start=(k == 0), stop=(k == KD - 1))
                full(last, (layer, name))

            def proj_tok(layer, name, n):
                w = piece(n).rearrange("p (k c) -> p k c", k=KD)
                ps = wait_free(pe, (layer, name))
                for t in range(NT):
                    for k in range(KD):
                        last = mm(ps[:, t * 256:(t + 1) * 256], xT[:, k, t * P:(t + 1) * P], w[:, k, :], start=(k == 0), stop=(k == KD - 1))
                full(last, (layer, name))

            def rows_to_acc(srcT, n, j, first, last_piece):
                w = piece(n).rearrange("p (k c) -> p k c", k=2)
                for i in range(2):
                    for t in range(NT):
                        for half in range(2):
                            last = mm(acc[:, t, half * 512:(half + 1) * 512], srcT[:, 2 * j + i, t * P:(t + 1) * P],
                                      w[:, i, half * 512:(half + 1) * 512], start=(first and i == 0), stop=(last_piece and i == 1))
                return last.then_inc(rows_used, 1)

            def mlstm():
                pe.wait_ge(sem("ld_const"), 16)
                pe.wait_ge(sem("ld_x"), 16)
                transposes(0, "x0T", x[:])
                for g in range(4):
                    wait_read(pe, (0, ("x0T", g)))
                pe.wait_ge(sem("ld_gw"), 16)
                ps = wait_free(pe, (0, "gates"))
                for i in range(2):
                    for k in range(KD):
                        last = mm(ps[0:MH, i * T:(i + 1) * T], wgates[:, k, i * MH:(i + 1) * MH], xT[:, k, :], start=(k == 0), stop=(k == KD - 1))
                full(last, (0, "gates"))
                pe.wait_ge(sem("ld_conv"), 16)
                ps = wait_free(pe, (0, "convT"))
                full(nc.tensor.transpose(ps[:, 0:32], conv_in[:], ident[0:32, 0:32]), (0, "convT"))
                for g in range(4):
                    proj_T(0, ("qk", g), PIECE_MIX[0] + g)
                pe.wait_ge(sem("grows"), 1)
                ps = wait_free(pe, (0, "gateT"))
                for i, r in enumerate((4, 6)):
                    for t in range(NT):
                        last = nc.tensor.transpose(ps[:, (2 * i + t) * MH:(2 * i + t + 1) * MH], gbuf[:, r, t * P:(t + 1) * P], ident[0:MH, 0:MH])
                full(last, (0, "gateT"))
                for g in range(4):
                    ps = wait_free(pe, (0, ("B", g)))
                    for i in range(2):
                        h = 2 * g + i
                        last = mm(ps[:, i * T:(i + 1) * T], cst("sel")[0:MH, h * P:(h + 1) * P], gbuf[:, 5, :], start=True, stop=True)
                    full(last, (0, ("B", g)))
                for g in range(4):
                    proj_tok(0, ("v", g), PIECE_MIX[0] + 4 + g)
                for g in range(4):
                    proj_tok(0, ("o", g), PIECE_MIX[0] + 8 + g)

                pe.wait_ge(sem("qk_ready"), 4)
                pe.wait_ge(sem("ones_v"), 1)

                def scores(h):
                    rows, tile = slice((h % 2) * MDK, (h % 2 + 1) * MDK), h // 2
                    ps = wait_free(pe, (0, ("S", h)))
                    mm(ps[:, 0:T], qk[rows, 4 + tile, 0:P], qk[rows, tile, :], start=True, stop=True)
                    last = mm(ps[:, T:T + P], qk[rows, 4 + tile, P:T], qk[rows, tile, P:T], start=True, stop=True)
                    full(last, (0, ("S", h)))

                scores(0)
                for h in range(MH):
                    if h + 1 < MH:
                        scores(h + 1)
                    wait_read(pe, (0, ("S", h)))
                    if h == 0:
                        for g in range(4):
                            wait_read(pe, (0, ("v", g)))
                    ps = wait_free(pe, (0, ("num", h)))
                    pt = pt_m[h % 2]
                    mm(ps[:, 0:MDV + 1], pt[:, 0:P], v_aug[:, 0, h, :], start=True, stop=True)
                    mm(ps[:, 256:256 + MDV + 1], pt[:, P:T], v_aug[:, 0, h, :], start=True, stop=False)
                    full(mm(ps[:, 256:256 + MDV + 1], pt[:, T:T + P], v_aug[:, 1, h, :], start=False, stop=True), (0, ("num", h)))
                pe.wait_ge(sem("mix_ready"), 1)
                transposes(0, "mT", hm_flat)
                for g in range(4):
                    wait_read(pe, (0, ("mT", g)))
                for j in range(4):
                    rows_to_acc(mixT, PIECE_OUT[0] + j, j, j == 0, j == 3)

            def nsa():
                pe.wait_ge(sem("ple_done"), 1)
                transposes(1, "x1T", x[:])
                for g in range(4):
                    wait_read(pe, (1, ("x1T", g)))
                pe.wait_ge(sem("ld_gw"), 32)
                ps = wait_free(pe, (1, "g"))
                for t in range(NT):
                    for k in range(KD):
                        last = mm(ps[:, t * 48:(t + 1) * 48], xT[:, k, t * P:(t + 1) * P], wgates[:, k, :], start=(k == 0), stop=(k == KD - 1))
                full(last, (1, "g"))
                pe.wait_ge(sem("ld_pos"), 64)
                ps = wait_free(pe, (1, "pos"))
                for i in range(2):
                    last = nc.tensor.transpose(ps[:, i * CBLK:(i + 1) * CBLK], pos_in[:, i, :], ident[0:CBLK, 0:CBLK])
                full(last, (1, "pos"))

                def rotate(name, raw, n):
                    wait_read(pe, (1, ("q0", "q1", "q2", "q3", "ks", "kw")[n - 1]))
                    ps = wait_free(pe, (1, name))
                    full(mm(ps[:, :], cst("rot"), raw, start=True, stop=True), (1, name))

                m0 = PIECE_MIX[1]
                proj_T(1, "q0", m0 + 0)
                proj_T(1, "q1", m0 + 1)
                rotate("rq0", silu[:, 0, :], 1)
                proj_T(1, "q2", m0 + 2)
                rotate("rq1", silu[:, 1, :], 2)
                proj_T(1, "q3", m0 + 3)
                rotate("rq2", silu[:, 0, :], 3)
                proj_T(1, "kc", m0 + 4)
                rotate("rq3", silu[:, 1, :], 4)
                proj_T(1, "vc", m0 + 5)
                proj_T(1, "ks", m0 + 6)
                proj_tok(1, "vs", m0 + 7)
                rotate("rks", silu[:, 0, :], 5)
                proj_T(1, "kw", m0 + 8)
                proj_tok(1, "vw", m0 + 9)
                rotate("rkw", silu[:, 1, :], 6)
                pe.wait_ge(sem("ld_cmpw"), 64)
                wait_read(pe, (1, "kc"))
                wait_read(pe, (1, "vc"))
                for par in range(2):
                    rows = slice(par * NDH, (par + 1) * NDH)
                    ps = wait_free(pe, (1, f"cmp{par}"))
                    for i in range(2):
                        for l in range(CBLK):
                            half, at = l // CSTR, l % CSTR
                            lo = at + half * CSTR
                            src = kp[rows, i, half, :, lo:lo + (NCMP - 1) * CSTR + 1:CSTR]
                            dst = ps[rows, i * 32:i * 32 + 2 * NCMP].rearrange("p (g c) -> p g c", g=2)
                            last = mm(dst, cmp_w[i][rows, l, :], src, start=(l == 0), stop=(l == CBLK - 1))
                    full(last, (1, f"cmp{par}"))
                for par in range(2):
                    wait_read(pe, (1, f"cmp{par}"))
                ps = wait_free(pe, (1, "kcrot"))
                full(mm(ps[:, 0:32], cst("rot"), kc_raw[:].rearrange("p g c -> p (g c)"), start=True, stop=True), (1, "kcrot"))
                ps = wait_free(pe, (1, "vcT"))
                for g in range(2):
                    last = nc.tensor.transpose(ps[:, g * P:(g + 1) * P], vrep_in[:, g].rearrange("p r c -> p (r c)"), ident)
                full(last, (1, "vcT"))
                pe.wait_ge(sem("kc_ready"), 1)
                for t in range(NT):
                    for par in range(2):
                        ps = wait_free(pe, (1, ("cs", t, par)))
                        for i in range(NH // 2):
                            h = (2 * (i // NJ) + par) * NJ + i % NJ
                            rows, pair, tile = head_rows(h)
                            last = mm(ps[:, i * 16:i * 16 + NCMP], qk[rows, tile, t * P:(t + 1) * P], kcT[rows, pair, 0:NCMP], start=True, stop=True)
                        full(last, (1, ("cs", t, par)))
                pe.wait_ge(sem("pc_ready"), 1)
                pcs = silu_flat.rearrange("p (t g c) -> p t g c", t=NT, g=NG)
                for t in range(NT):
                    ps = wait_free(pe, (1, ("pcT", t)))
                    for g in range(NG):
                        last = nc.tensor.transpose(ps[:, g * P:(g + 1) * P], pcs[:, t, g, :], ident)
                    full(last, (1, ("pcT", t)))
                wait_read(pe, (1, "vcT"))
                for t in range(NT):
                    wait_read(pe, (1, ("pcT", t)))
                for half in range(2):
                    for g in range(2 * half, 2 * half + 2):
                        for t in range(NT):
                            last = mm(acc[:, t, g * 256:(g + 1) * 256], pcT[:, t, g, :], v_blk[:, g].rearrange("p j e -> p (j e)"), start=True, stop=True)
                    last.then_inc(sem("pv_half"), 1)

                def u_scores(u):
                    h, br = u % NH, u // NH
                    rows, pair, tile = head_rows(h)
                    ps = wait_free(pe, (1, ("US", u)))
                    mm(ps[:, 0:P], qk[rows, tile, 0:P], kT_sw[rows, br, pair, 0:P], start=True, stop=True)
                    full(mm(ps[:, P:P + T], qk[rows, tile, P:T], kT_sw[rows, br, pair, :], start=True, stop=True), (1, ("US", u)))

                def u_turn(u):
                    pe.wait_ge(sem("u_exp"), u + 1)
                    ps = wait_free(pe, (1, ("UT", u)))
                    for c in range(3):
                        last = nc.tensor.transpose(ps[:, c * P:(c + 1) * P], u_p[u % 2][:, c * P:(c + 1) * P], ident)
                    full(last, (1, ("UT", u)))

                def u_values(u):
                    h, br = u % NH, u // NH
                    g = h // NJ
                    wait_read(pe, (1, ("UT", u)))
                    if h % 8 == 0:
                        pe.wait_ge(sem("o_half"), 2 * br + h // 8 + 1)
                    pt, vv = u_pT[u % 2], v_sw[:, br, :, g * NDH:(g + 1) * NDH]
                    mm(acc_h[:, 0, h, :], pt[:, 0:P], vv[:, 0, :], start=True, stop=True)
                    mm(acc_h[:, 1, h, :], pt[:, P:T], vv[:, 0, :], start=True, stop=False)
                    last = mm(acc_h[:, 1, h, :], pt[:, T:T + P], vv[:, 1, :], start=False, stop=True)
                    last.then_inc(sem("u_pv"), 1)

                for u in range(NUNIT + 1):
                    if u < NUNIT:
                        u_scores(u)
                    if u:
                        u_turn(u - 1)
                        if u > 1:
                            u_values(u - 2)
                u_values(NUNIT - 1)
                pe.wait_ge(sem("o_half"), 6)
                transposes(1, "nT", o_flat)
                for g in range(4):
                    wait_read(pe, (1, ("nT", g)))
                for j in range(4):
                    rows_to_acc(mixT, PIECE_OUT[1] + j, j, j == 0, j == 3)

            def tail(layer):
                pe.wait_ge(sem("ln_done"), 2 * layer + 1)
                transposes(layer, "xT", x[:])
                for g in range(4):
                    wait_read(pe, (layer, ("xT", g)))
                pe.wait_ge(sem("ld_router"), 32 * (layer + 1))
                ps = wait_free(pe, (layer, "logits"))
                for t in range(NT):
                    for k in range(KD):
                        last = mm(ps[:, t * NE:(t + 1) * NE], xT[:, k, t * P:(t + 1) * P], router[:, k, :], start=(k == 0), stop=(k == KD - 1))
                full(last, (layer, "logits"))
                n = PIECE_SH[layer]
                proj_T(layer, "sh_gate", n, True)
                proj_T(layer, "sh_up", n + 1, True)
                wait_read(pe, (layer, "sh_up"))
                pe.wait_ge(sem("acc_read"), 2 * layer + 1)
                hid_v = hid[:].rearrange("p b (f t) -> p b f t", f=2)
                rows_to_acc(hid_v[:, 1], n + 2, 0, True, True)
                pe.wait_ge(sem("cw_ready"), layer + 1)
                ps = wait_free(pe, (layer, "rank"))
                mm(ps[:, 0:NE], cst("earlier"), cand[:, 0, :], start=True, stop=True)
                mm(ps[:, NE:2 * NE], cst("ones"), cand[:, 0, :], start=True, stop=False)
                mm(ps[:, NE:2 * NE], cst("earlier"), cand[:, 1, :], start=False, stop=True)
                mm(ps[:, 2 * NE:3 * NE], cst("ones"), cand[:, 0, :], start=True, stop=False)
                last = mm(ps[:, 2 * NE:3 * NE], cst("ones"), cand[:, 1, :], start=False, stop=True)
                full(last, (layer, "rank"))

                def gather(banks, n_slots):
                    per = KD // len(banks)
                    last = []
                    for k in range(KD):
                        dst = banks[k // per][:, (k % per) * n_slots:(k % per + 1) * n_slots]
                        for s in range(3):
                            for t in range(NT):
                                hot = onehot[:, t].rearrange("p b c -> p (b c)")[:, 0:n_slots]
                                ins = mm(dst, x_part[s][:, t, k::KD], hot, start=(s == 0 and t == 0), stop=(s == 2 and t == NT - 1))
                        if k % per == per - 1:
                            last.append(ins)
                    return last

                def gate_up(ps, w_gate, w_up, slots):
                    for i, w in enumerate((w_gate, w_up)):
                        w = w.rearrange("p (k c) -> p k c", k=KD)
                        for c in range(2):
                            for k in range(KD):
                                dst = ps[:, (2 * i + c) * CAP:(2 * i + c + 1) * CAP]
                                last = mm(dst, w[:, k, c::2], xg[:, k, slots], start=(k == 0), stop=(k == KD - 1))
                    return last

                def down(banks, rows, h, w):
                    w = w.rearrange("p (k c) -> p k c", k=2)
                    last = []
                    for half in range(2):
                        for k in range(2):
                            ins = mm(banks[half][rows, :], h[:, k * CAP:(k + 1) * CAP], w[:, k, half * 512:(half + 1) * 512],
                                     start=(k == 0), stop=(k == 1))
                        last.append(ins)
                    return last

                def turn_onehot(ps, n_slots):
                    for t in range(NT):
                        src = weighted_1h[:, t].rearrange("p b c -> p (b c)")[:, 0:n_slots]
                        last = nc.tensor.transpose(ps[0:n_slots, 256 + t * P:256 + (t + 1) * P], src, ident)
                    return last

                def scatter_add(n_slots):
                    for t in range(NT):
                        for half in range(2):
                            last = mm(acc[:, t, half * 512:(half + 1) * 512], scatter[0:n_slots, t * P:(t + 1) * P],
                                      y_sb[0:n_slots, half * 512:(half + 1) * 512], start=False, stop=True, skip_group_check=True)
                    return last

                pe.wait_ge(sem("x_part"), 3 * (layer + 1))
                pe.wait_ge(sem("hot_ready"), layer * (NE // 2 + 1) + 1)
                banks = [wait_free(pe, (layer, n)) for n in ("xgL", "xgH")]
                for n, last in zip(("xgL", "xgH"), gather(banks, 2 * CAP)):
                    full(last, (layer, n))

                n0 = PIECE_LOOP[layer]
                with pe.Fori(0, N_BODIES) as i:
                    def loop_piece(kind, e):
                        n = n0 + BODY.index((kind, e))
                        pe.wait_ge(landed[n % RING], i * 16 + landed_value(n))
                        return ring[:, n % RING, :]

                    def loop_fills(ins, g):
                        ins.then_inc(bank_full[loop_bank(layer, g)[0]], 1)

                    for pair in range(2):
                        for b in range(2):
                            e = 2 * pair + b
                            w = [loop_piece(k, e) for k in "gu"]
                            ps = loop_wait_free(pe, layer, ("gu", e), i)
                            if b == 0:
                                if pair:
                                    loop_read(pe, layer, ("xgL", 1), i)
                                    loop_read(pe, layer, ("xgH", 1), i)
                                else:
                                    loop_read(pe, layer, ("xgL", 0), i, last_body=True)
                                    loop_read(pe, layer, ("xgH", 0), i, last_body=True)
                            last = gate_up(ps, w[0], w[1], slice(b * CAP, (b + 1) * CAP))
                            if b == 0:
                                loop_fills(last, ("gu", e))
                                if pair:
                                    for half in range(2):
                                        loop_read(pe, layer, ("y", 0, half), i)
                                    scatter_add(2 * CAP)
                            else:
                                pe.wait_ge(sem("weighted_ready"), i * 2 + (layer * (NE // 2 + 1) + pair + 1))
                                loop_fills(turn_onehot(ps, 2 * CAP), ("gu", e))
                        if pair == 0:
                            pe.wait_ge(sem("hot_ready"), i * 2 + (layer * (NE // 2 + 1) + 2))
                            banks = [loop_wait_free(pe, layer, (n, 1), i) for n in ("xgL", "xgH")]
                            for n, last in zip(("xgL", "xgH"), gather(banks, 2 * CAP)):
                                loop_fills(last, (n, 1))
                        banks = [loop_wait_free(pe, layer, ("y", pair, half), i) for half in range(2)]
                        for b in range(2):
                            e = 2 * pair + b
                            pe.wait_ge(sem("hid_ready"), i * EPB + (layer * NE + e + 1))
                            w = loop_piece("d", e)
                            last = down(banks, slice(b * CAP, (b + 1) * CAP), hid_e[b], w)
                            if b == 0:
                                last[1].then_inc(rows_used, 1)
                            else:
                                for half in range(2):
                                    loop_fills(last[half], ("y", pair, half))
                    pe.wait_ge(sem("hot_ready"), i * 2 + (layer * (NE // 2 + 1) + 3))
                    banks = [loop_wait_free(pe, layer, (n, 0), i) for n in ("xgL", "xgH")]
                    for n, last in zip(("xgL", "xgH"), gather(banks, 2 * CAP)):
                        loop_fills(last, (n, 0))
                    for half in range(2):
                        loop_read(pe, layer, ("y", 1, half), i)
                    loop_read(pe, layer, ("gu", 3), i)
                    scatter_add(2 * CAP)

                for g in BODY_GROUPS[-NB_WORK:]:
                    loop_read(pe, layer, g, N_BODIES - 1)
                pe.wait_ge(more_done[layer], 1)
                s = more[layer]
                with pe.Fori(0, MORE) as m:
                    block_id = pe.value_load(more_i[0:1, bass.ds(m, 1)], min_val=0, max_val=NE * NBLK - 1)
                    with pe.If(block_id > 0):
                        pe.wait_ge(s["hot"], m + 1)
                        gather([work[0]], CAP)[0].then_inc(s["xg"], 1)
                        w = []
                        for j in range(3):
                            pe.wait_ge(more_landed[layer][j], m * 16 + 16)
                            w.append(ring[:, (MORE_PIECE[layer] + j) % RING, :])
                        pe.wait_ge(s["xg_read"], m + 1)
                        gate_up(work[1], w[0], w[1], slice(0, CAP))
                        turn_onehot(work[1], CAP).then_inc(s["gu"], 1)
                        pe.wait_ge(s["hid"], m + 1)
                        down(work[2:4], slice(0, CAP), hid_e[0], w[2])[1].then_inc(s["y"], 1)
                        pe.wait_ge(s["y_read"], m + 1)
                        scatter_add(CAP).then_inc(more_done[layer], 1)
                pe.drain().then_inc(sem("experts_done"), 1)

                pe.wait_ge(sem("ln_done"), 2 * layer + 2)
                transposes(layer, "xT2", x[:])
                pe.wait_ge(sem("ld_p"), 16 * (layer + 1))
                ps = wait_free(pe, (layer, "pT"))
                for k in range(2):
                    for t in range(NT):
                        c = (k * NT + t) * P
                        last = nc.tensor.transpose(ps[:, c:c + P], p_in[:, t, k::2], ident)
                full(last, (layer, "pT"))
                for g in range(4):
                    wait_read(pe, (layer, ("xT2", g)))
                wait_read(pe, (layer, "pT"))
                pe.wait_ge(sem("acc_read"), 2 * layer + 2)
                n = PIECE_PLE[layer]
                rows_to_acc(pT[:], n, 0, True, True)
                banks = [wait_free(pe, (layer, ("pg", q))) for q in range(4)]
                for j in range(4):
                    w = piece(n + 1 + j).rearrange("p (k c) -> p k c", k=2)
                    for i in range(2):
                        for q in range(4):
                            t, half = q // 2, q % 2
                            last = mm(banks[q][:, :], xT[:, 2 * j + i, t * P:(t + 1) * P], w[:, i, half * 512:(half + 1) * 512],
                                      start=(j == 0 and i == 0), stop=(j == 3 and i == 1))
                            if j == 3 and i == 1:
                                full(last, (layer, ("pg", q)))
                    if j < 3:
                        last.then_inc(rows_used, 1)

            mlstm()
            tail(0)
            nsa()
            tail(1)

        @block.scalar
        def _(act):
            af = nc.scalar.activation
            chain = Chain(act, sem("act_step"))

            def mlstm():
                act.wait_ge(sem("gabs"), 1)
                chain.step(af(gbuf[:, 2, :], gbuf[:, 2, :], ACT.Exp, scale=-1.0))
                af(gbuf[:, 2, :], gbuf[:, 2, :], ACT.Ln, bias=1.0).then_inc(sem("glog"), 1)
                act.wait_ge(sem("gneg"), 1)
                af(gbuf[:, 6, :], gbuf[:, 6, :], ACT.Exp).then_inc(sem("grows"), 1)
                for g in range(4):
                    wait_read(act, (0, ("qk", g)))
                    v = qk[:, 2 * g:2 * g + 2, :]
                    af(v, v, ACT.Silu).then_inc(sem("qk_ready"), 1)
                for h in range(MH):
                    wait_read(act, (0, ("B", h // 2)))
                    af(decay(h), decay(h), ACT.Exp).then_inc(sem("decay_ready"), 1)
                for g in range(4):
                    ps = wait_full(act, (0, ("v", g)))
                    src = ps[:, :].rearrange("p (t h e) -> p t h e", t=NT, h=2)
                    for t in range(NT):
                        last = nc.scalar.copy(v_aug[:, t, 2 * g:2 * g + 2, 0:MDV], src[:, t])
                    free(last, (0, ("v", g)))
                for g in range(4):
                    ps = wait_full(act, (0, ("o", g)))
                    src = ps[:, :].rearrange("p (t c) -> p t c", t=NT)
                    free(af(sig_o[:, :, g * 256:(g + 1) * 256], src, ACT.Sigmoid), (0, ("o", g)))
                act.wait_ge(sem("hvar"), 1)
                af(hmv[:, :, :, 1], hmv[:, :, :, 1], ACT.Sqrt).then_inc(sem("hstd"), 1)

            def norm(n):
                act.wait_ge(sem("ln_var"), n)
                af(lnmv[:, :, 1], lnmv[:, :, 1], ACT.Sqrt).then_inc(sem("ln_std"), 1)

            def nsa():
                ps = wait_full(act, (1, "g"))
                free(af(gsig[:].rearrange("p t h c -> p t (h c)"), ps[:, 0:96].rearrange("p (t c) -> p t c", t=NT), ACT.Sigmoid), (1, "g"))
                for n, name in enumerate(("q0", "q1", "q2", "q3", "ks", "kw")):
                    ps = wait_full(act, (1, name))
                    if n >= 2:
                        act.wait_ge(sem("rope_done"), n - 1)
                    free(nc.scalar.copy(silu[:, n % 2, :], ps[:, :]), (1, name))
                    if name in ("ks", "kw"):
                        v = "vs" if name == "ks" else "vw"
                        ps = wait_full(act, (1, v))
                        free(nc.scalar.copy(v_sw[:, name == "kw"].rearrange("p t c -> p (t c)"), ps[:, :]), (1, v))
                act.wait_ge(sem("cs_ready"), 1)
                af(cs_s[:, :, :, 0:NCMP], cs_s[:, :, :, 0:NCMP], ACT.Exp, scale=NDH ** -0.5).then_inc(sem("cs_exp"), 1)
                for t in range(NT):
                    ps = wait_full(act, (1, ("pcT", t)))
                    free(nc.scalar.copy(pcT[:, t].rearrange("p g c -> p (g c)"), ps[:, :]), (1, ("pcT", t)))

                def turned(u):
                    ps = wait_full(act, (1, ("UT", u)))
                    if u >= 2:
                        act.wait_ge(sem("u_pv"), u - 1)
                    free(nc.scalar.copy(u_pT[u % 2], ps[:, 0:384]), (1, ("UT", u)))

                for u in range(NUNIT):
                    act.wait_ge(sem("u_max"), u + 1)
                    if u == 0:
                        act.wait_ge(sem("pcs_read"), 1)
                    if u >= 2:
                        wait_full(act, (1, ("UT", u - 2)))
                    h = u % NH
                    if h % 8 == 0:
                        act.wait_ge(sem("o_half"), 2 * (u // NH) + h // 8)
                    s, p = u_s[u % 2], u_p[u % 2]
                    af(p[:, 0:P], s[:, 0:P], ACT.Exp, scale=NDH ** -0.5, bias=nmax[:, u % 2, 0:1], accum_out=nden[:, 0, h:h + 1])
                    af(p[:, P:P + T], s[:, P:P + T], ACT.Exp, scale=NDH ** -0.5, bias=nmax[:, u % 2, 1:2],
                       accum_out=nden[:, 1, h:h + 1]).then_inc(sem("u_exp"), 1)
                    if u:
                        turned(u - 1)
                turned(NUNIT - 1)

            def tail(layer):
                act.wait_ge(sem("ln_done"), 2 * layer + 1)
                nc.scalar.copy(x_part[0], x[:]).then_inc(sem("x_part"), 1)
                ps = wait_full(act, (layer, "logits"))
                free(af(score[:].rearrange("p t e -> p (t e)"), ps[:, 0:NT * NE], ACT.Sigmoid), (layer, "logits"))
                for s in range(1, 3):
                    act.wait_ge(sem("x_rest"), 2 * layer + s)
                    nc.scalar.copy(x_part[s], x_rest).then_inc(sem("x_part"), 1)
                ps = wait_full(act, (layer, "sh_gate"))
                free(af(silu[:, 1, :], ps[:, :], ACT.Silu), (layer, "sh_gate"))
                ps = wait_full(act, (layer, "xgL"))
                free(nc.scalar.copy(xg[:, 0:4, :].rearrange("p k c -> p (k c)"), ps[:, :]), (layer, "xgL"))
                with act.Fori(0, N_BODIES) as i:
                    def read(ins, g):
                        ins.then_inc(bank_free[loop_bank(layer, g)[0]], 1)

                    for pair in range(2):
                        for b in range(2):
                            ps = loop_full(act, layer, ("gu", 2 * pair + b), i)
                            af(sil_e[b], ps[:, 0:2 * CAP], ACT.Silu).then_inc(sem("silu_ready"), 1)
                        for g, dst in (((("xgL", 1), xg), (("y", 0, 0), None)) if pair == 0 else ((("y", 1, 0), None), (("xgL", 0), xg))):
                            ps = loop_full(act, layer, g, i)
                            if dst is None:
                                read(nc.scalar.copy(y_sb[:, 0:512], ps[:, :]), g)
                            else:
                                read(nc.scalar.copy(xg[:, 0:4, :].rearrange("p k c -> p (k c)"), ps[:, :]), g)
                act.wait_ge(more_done[layer], 1)
                s = more[layer]
                with act.Fori(0, MORE) as m:
                    block_id = act.value_load(more_i[0:1, bass.ds(m, 1)], min_val=0, max_val=NE * NBLK - 1)
                    with act.If(block_id > 0):
                        act.wait_ge(s["xg"], m + 1)
                        nc.scalar.copy(xg[:, :, 0:CAP], work[0][:, :].rearrange("p (k c) -> p k c", k=KD)).then_inc(s["xg_read"], 1)
                        act.wait_ge(s["gu"], m + 1)
                        af(sil_e[0], work[1][:, 0:2 * CAP], ACT.Silu).then_inc(s["silu"], 1)
                norm(2 * layer + 2)
                for q in range(4):
                    ps = wait_full(act, (layer, ("pg", q)))
                    free(af(sig_o[:, q // 2, (q % 2) * 512:(q % 2 + 1) * 512], ps[:, :], ACT.Sigmoid), (layer, ("pg", q)))

            mlstm()
            norm(1)
            tail(0)
            nsa()
            norm(3)
            tail(1)

        @block.vector
        def _(dve):
            chain = Chain(dve, sem("dve_step"))
            step = chain.step
            copy, ts, tt, stt = nc.vector.tensor_copy, nc.vector.tensor_scalar, nc.vector.tensor_tensor, nc.vector.scalar_tensor_tensor

            def copies_T(layer, name, dst):
                for g in range(4):
                    ps = wait_full(dve, (layer, (name, g)))
                    free(copy(dst[:, 2 * g:2 * g + 2, :].rearrange("p k t -> p (k t)"), ps[:, :]), (layer, (name, g)))

            def mlstm():
                copies_T(0, "x0T", xT)
                nc.vector.memset(slot_of[:], -1.0)
                step(nc.vector.memset(cw[:], 0.0))
                step(nc.vector.memset(gbuf[:, 7, :], 1.0))
                ps = wait_full(dve, (0, "gates"))
                dve.wait_ge(sem("ld_gbias"), 32)
                ts(gbuf[:, 0, :], ps[0:MH, 0:T], gbias[:, 0:1], None, ALU.add)
                free(ts(gbuf[:, 1, :], ps[0:MH, T:2 * T], gbias[:, 1:2], None, ALU.add), (0, "gates"))
                wait_read(dve, (0, "gates"))
                stt(gbuf[:, 2, :], gbuf[:, 1, :], -1.0, gbuf[:, 1, :], ALU.mult, ALU.max).then_inc(sem("gabs"), 1)
                dve.wait_ge(sem("glog"), 1)
                step(stt(gbuf[:, 1, :], gbuf[:, 1, :], 0.0, gbuf[:, 2, :], ALU.min, ALU.subtract))
                step(nc.vector.tensor_tensor_scan(gbuf[:, 3, :], gbuf[:, 7, :], gbuf[:, 1, :], 0.0, ALU.mult, ALU.add))
                step(tt(gbuf[:, 4, :], gbuf[:, 0, :], gbuf[:, 3, :], ALU.subtract))
                step(nc.vector.tensor_tensor_scan(gbuf[:, 5, :], gbuf[:, 4, :], gbuf[:, 4, :], 0.0, ALU.max, ALU.max))
                step(stt(gbuf[:, 6, :], gbuf[:, 3, :], -1.0, gbuf[:, 5, :], ALU.mult, ALU.subtract))
                ts(gbuf[:, 5, :], gbuf[:, 5, :], -1.0, None, ALU.mult).then_inc(sem("gneg"), 1)
                ps = wait_full(dve, (0, "convT"))
                free(copy(conv_w[:], ps[:, 0:32]), (0, "convT"))
                wait_read(dve, (0, "convT"))
                for g in range(4):
                    ps = wait_full(dve, (0, ("qk", g)))
                    for c in range(2):
                        ch = 2 * g + c
                        y, src = qk[:, ch, :], ps[:, c * T:(c + 1) * T]
                        step(ts(y, src, conv_w[:, 3 * 8 + ch:3 * 8 + ch + 1], None, ALU.mult))
                        for back in range(1, MCONV):
                            j = (MCONV - 1 - back) * 8 + ch
                            last = stt(y[:, back:T], src[:, 0:T - back], conv_w[:, j:j + 1], y[:, back:T], ALU.mult, ALU.add)
                            if back < MCONV - 1:
                                step(last)
                    free(last, (0, ("qk", g)))
                ps = wait_full(dve, (0, "gateT"))
                free(copy(gtok[:].rearrange("p a h -> p (a h)"), ps[:, 0:4 * MH]), (0, "gateT"))
                wait_read(dve, (0, "gateT"))
                for g in range(4):
                    ps = wait_full(dve, (0, ("B", g)))
                    for i in range(2):
                        h = 2 * g + i
                        d = decay(h)
                        stt(d[:, 0:T], ps[:, i * T:(i + 1) * T], gtok[:, 0, h:h + 1], cst("mask_st"), ALU.add, ALU.min)
                        last = stt(d[:, T:T + P], ps[:, i * T + P:(i + 1) * T], gtok[:, 1, h:h + 1], cst("mask_st")[:, 0:P], ALU.add, ALU.min)
                    free(last, (0, ("B", g)))

                def weighted(h):
                    ps = wait_full(dve, (0, ("S", h)))
                    dve.wait_ge(sem("decay_ready"), h + 1)
                    free(stt(pt_m[h % 2], ps[:, 0:384], MDK ** -0.5, decay(h), ALU.mult, ALU.mult), (0, ("S", h)))

                weighted(0)
                for h in range(MH):
                    if h + 1 < MH:
                        weighted(h + 1)
                    ps = wait_full(dve, (0, ("num", h)))
                    v = ps[:, :].rearrange("p (t e) -> p t e", t=NT)
                    step(copy(den2[:], v[:, :, MDV]))
                    step(stt(den2[:], den2[:], -1.0, den2[:], ALU.mult, ALU.max))
                    step(tt(den2[:], den2[:], gtok[:, 2:4, h], ALU.max))
                    step(nc.vector.reciprocal(den2[:], den2[:]))
                    for t in range(NT):
                        last = ts(hm[:, t, h, :], v[:, t, 0:MDV], den2[:, t:t + 1], None, ALU.mult)
                    free(last, (0, ("num", h)))
                    wait_read(dve, (0, ("num", h)))
                    for t in range(NT):
                        step(nc.vector.bn_stats(hst[:], hm[:, t, h, :]))
                        step(nc.vector.bn_aggr(hmv[:, t, h, :], hst[:]))
                ts(hmv[:, :, :, 1], hmv[:, :, :, 1], EPS, None, ALU.add).then_inc(sem("hvar"), 1)
                dve.wait_ge(sem("hstd"), 1)
                step(nc.vector.reciprocal(hmv[:, :, :, 1], hmv[:, :, :, 1]))
                for h in range(MH):
                    for t in range(NT):
                        last = ts(hm[:, t, h, :], hm[:, t, h, :], hmv[:, t, h, 0:1], hmv[:, t, h, 1:2], ALU.subtract, ALU.mult)
                step(last)
                dve.wait_ge(sem("ld_norm"), 16)
                for t in range(NT):
                    last = tt(hm_flat[:, t, :], hm_flat[:, t, :], ln_p[:, 0, :], ALU.mult)
                step(last, sem("norm_g_used"))
                for g in range(4):
                    wait_read(dve, (0, ("o", g)))
                tt(bufD[:], bufD[:], bufC[:], ALU.mult).then_inc(sem("mix_ready"), 1)
                copies_T(0, "mT", mixT)

            iota_pair = cst("iota").unsqueeze(1).unsqueeze(1).to_broadcast([P, NT, 2, CAP])

            def norm(n):
                layer, k = (n - 1) // 2, (n - 1) % 2
                if k == 0:
                    dve.wait_ge(rows_used, ROWS_BEFORE_LOOP[layer] - 1)
                else:
                    dve.wait_ge(sem("experts_done"), layer + 1)
                for t in range(NT):
                    last = stt(z[:, t, :], x[:, t, :], ALPHA, acc[:, t, :], ALU.mult, ALU.add)
                step(last, sem("acc_read"))
                for t in range(NT):
                    for half in range(2):
                        last = nc.vector.bn_stats(lnst[:, t, half, :], z[:, t, half * 512:(half + 1) * 512])
                step(last)
                for t in range(NT):
                    last = nc.vector.bn_aggr(lnmv[:, t, :], lnst[:, t].rearrange("p a b -> p (a b)"))
                step(last)
                ts(lnmv[:, :, 1], lnmv[:, :, 1], EPS, None, ALU.add).then_inc(sem("ln_var"), 1)
                dve.wait_ge(sem("ln_std"), n)
                step(nc.vector.reciprocal(lnmv[:, :, 1], lnmv[:, :, 1]))
                dve.wait_ge(sem("ld_ln"), 32 * n)
                for t in range(NT):
                    step(ts(z[:, t, :], z[:, t, :], lnmv[:, t, 0:1], lnmv[:, t, 1:2], ALU.subtract, ALU.mult))
                for t in range(NT):
                    step(tt(z[:, t, :], z[:, t, :], ln_p[:, 0, :], ALU.mult))
                for t in range(NT):
                    last = tt(x[:, t, :], z[:, t, :], ln_p[:, 1, :], ALU.add)
                step(last, sem("ln_done"))

            def choose(layer):
                wait_read(dve, (layer, "logits"))
                dve.wait_ge(sem("ld_router"), 32 * (layer + 1))
                for t in range(NT):
                    last = tt(biased[:, t, :], score[:, t, :], rbias[:], ALU.add)
                step(last)
                for t in range(NT):
                    for g in range(NEG):
                        last = nc.vector.max(grp8[:, t * NEG + g, :], biased[:, t, g * 8:(g + 1) * 8])
                step(last)
                step(tt(grp[:], grp8[:, :, 0], grp8[:, :, 1], ALU.add))
                g3 = grp[:].rearrange("p (t g) -> p t g", t=NT)
                for t in range(NT):
                    other = g3[:, t, :].unsqueeze(1).to_broadcast([P, NEG, NEG])
                    own = g3[:, t, :].unsqueeze(2).to_broadcast([P, NEG, NEG])
                    tt(gcmp[:, t], other, own, ALU.is_gt)
                    last = tt(geq[:, t], other, own, ALU.is_equal)
                step(last)
                for t in range(NT):
                    last = tt(geq[:, t], geq[:, t], cst("before").rearrange("p (a b) -> p a b", a=NEG), ALU.mult)
                step(last)
                step(tt(gcmp[:], gcmp[:], geq[:], ALU.add))
                step(nc.vector.reduce_sum(rank[:], gcmp[:].rearrange("p t a b -> p (t a) b"), axis=AX.X))
                step(ts(grp[:], rank[:], float(TOPG) - 0.5, None, ALU.is_lt))
                e3 = [v[:].rearrange("p t (g e) -> p (t g) e", g=NEG) for v in (biased, cand)]
                step(ts(rank[:], grp[:], BIG, -BIG, ALU.mult, ALU.add))
                step(tt(e3[0], e3[0], grp[:].unsqueeze(2).to_broadcast([P, NT * NEG, 8]), ALU.mult))
                step(tt(e3[0], e3[0], rank[:].unsqueeze(2).to_broadcast([P, NT * NEG, 8]), ALU.add))
                for t in range(NT):
                    last = nc.vector.max(top8[:, t, :], biased[:, t, :])
                step(last)
                for t in range(NT):
                    last = nc.vector.match_replace(cand[:, t, :], top8[:, t, :], biased[:, t, :], -3e38)
                step(last)
                step(tt(cand[:], cand[:], biased[:], ALU.not_equal))
                step(tt(cw[:, :, 0:NE], cand[:], score[:], ALU.mult))
                step(nc.vector.reduce_sum(rsum[:], cw[:, :, 0:NE], axis=AX.X))
                step(nc.vector.reciprocal(rsum[:], rsum[:]))
                for t in range(NT):
                    last = ts(cw[:, t, 0:NE], cw[:, t, 0:NE], rsum[:, t:t + 1], SCALE_R, ALU.mult, ALU.mult)
                last.then_inc(sem("cw_ready"), 1)

            def assign_slots(layer):
                ps = wait_full(dve, (layer, "rank"))
                step(stt(slot_of[:, :, 0:NE], ps[:, 0:2 * NE].rearrange("p (t e) -> p t e", t=NT), 1.0, cand[:], ALU.add, ALU.mult))
                step(ts(slot_of[:, :, 0:NE], slot_of[:, :, 0:NE], -1.0, None, ALU.add))
                more_v = more_cand[:].rearrange("p e b -> p (e b)")
                count = ps[:, 2 * NE:3 * NE].unsqueeze(2).to_broadcast([P, NE, NBLK - 1])
                free(tt(more_cand[:], count, cst("blk_floor").rearrange("p (e b) -> p e b", e=NE), ALU.is_gt), (layer, "rank"))
                wait_read(dve, (layer, "rank"))
                make_hot(0)
                step(tt(more_v, more_v, cst("blk_id"), ALU.mult))
                for r in range(MORE // 8):
                    step(nc.vector.max(more_f[:, 8 * r:8 * r + 8], more_v))
                    step(nc.vector.match_replace(more_v, more_f[:, 8 * r:8 * r + 8], more_v, 0.0))
                step(copy(more_i[:], more_f[:]))
                step(ts(more_blk[:], more_i[:], NBLK - 1, None, ALU.bitwise_and))
                step(ts(more_base[:], more_blk[:], float(CAP), None, ALU.mult), more_done[layer])

            def make_hot(first):
                slot = slot_of[:, :, bass.ds(first, 2)].unsqueeze(3).to_broadcast([P, NT, 2, CAP])
                tt(onehot[:], iota_pair, slot, ALU.is_equal).then_inc(sem("hot_ready"), 1)

            def make_weighted(first):
                weight = cw[:, :, bass.ds(first, 2)].unsqueeze(3).to_broadcast([P, NT, 2, CAP])
                tt(weighted_1h[:], onehot[:], weight, ALU.mult).then_inc(sem("weighted_ready"), 1)

            def nsa():
                copies_T(1, "x1T", xT)
                ps = wait_full(dve, (1, "pos"))
                free(copy(posT[:].rearrange("p i l -> p (i l)"), ps[:, 0:2 * CBLK]), (1, "pos"))
                wait_read(dve, (1, "pos"))
                cos2 = cst("cos").unsqueeze(1).to_broadcast([P, 2, T])
                sin2 = cst("sin").unsqueeze(1).to_broadcast([P, 2, T])

                def rope(n, name, dst):
                    ps = wait_full(dve, (1, name))
                    raw = silu[:, n % 2, :].rearrange("p (c t) -> p c t", c=2)
                    tmp = hid[:, n % 2, :].rearrange("p (c t) -> p c t", c=2)
                    tt(dst, raw, cos2, ALU.mult)
                    free(tt(tmp, ps[:, :].rearrange("p (c t) -> p c t", c=2), sin2, ALU.mult), (1, name))
                    wait_read(dve, (1, name))
                    last = tt(dst, dst, tmp, ALU.add)
                    step(last, sem("rope_done"))

                def with_positions(i, name):
                    ps = wait_full(dve, (1, name))
                    for half in range(2):
                        for g in range(2):
                            src = ps[:, g * T:(g + 1) * T].rearrange("p (c l) -> p c l", l=CSTR)
                            pos = posT[:, i, half * CSTR:(half + 1) * CSTR].unsqueeze(1).to_broadcast([P, T // CSTR, CSTR])
                            last = tt(kp[:, i, half, g, :].rearrange("p (c l) -> p c l", l=CSTR), src, pos, ALU.add)
                    free(last, (1, name))

                rope(0, "rq0", qk[:, 0:2, :])
                rope(1, "rq1", qk[:, 2:4, :])
                rope(2, "rq2", qk[:, 4:6, :])
                with_positions(0, "kc")
                rope(3, "rq3", qk[:, 6:8, :])
                with_positions(1, "vc")
                rope(4, "rks", kT_sw[:, 0])
                rope(5, "rkw", kT_sw[:, 1])
                step(nc.vector.memset(kc_raw[:], 0.0))
                step(nc.vector.memset(vrep_in[:], 0.0))
                step(nc.vector.memset(silu[:], 0.0))
                for par in range(2):
                    rows = slice(par * NDH, (par + 1) * NDH)
                    ps = wait_full(dve, (1, f"cmp{par}"))
                    copy(kc_raw[rows, :, 0:NCMP], ps[rows, 0:2 * NCMP].rearrange("p (g c) -> p g c", g=2))
                    for g in range(2):
                        v = ps[rows, 32 + g * NCMP:32 + (g + 1) * NCMP].unsqueeze(1).to_broadcast([NDH, 4, NCMP])
                        last = copy(vrep_in[rows, g, :, 0:NCMP], v)
                    free(last, (1, f"cmp{par}"))
                    wait_read(dve, (1, f"cmp{par}"))
                ps = wait_full(dve, (1, "kcrot"))
                cc = cst("cos_c").unsqueeze(1).to_broadcast([P, 2, 16])
                sc = cst("sin_c").unsqueeze(1).to_broadcast([P, 2, 16])
                free(tt(kc_t[:], ps[:, 0:32].rearrange("p (g c) -> p g c", g=2), sc, ALU.mult), (1, "kcrot"))
                wait_read(dve, (1, "kcrot"))
                step(tt(kcT[:], kc_raw[:], cc, ALU.mult))
                tt(kcT[:], kcT[:], kc_t[:], ALU.add).then_inc(sem("kc_ready"), 1)
                step(nc.vector.memset(v_blk[:], 0.0))
                ps = wait_full(dve, (1, "vcT"))
                for g in range(NG):
                    for j in range(NJ):
                        rows = slice(32 * j, 32 * (j + 1))
                        last = copy(v_blk[rows, g, j, :], ps[rows, g * NDH:(g + 1) * NDH])
                free(last, (1, "vcT"))
                madd = cst("cmask_add").rearrange("p (t c) -> p t c", t=NT)
                mmul = cst("cmask_mul").rearrange("p (t c) -> p t c", t=NT)
                for t in range(NT):
                    for par in range(2):
                        ps = wait_full(dve, (1, ("cs", t, par)))
                        for pair in range(2):
                            h = (2 * pair + par) * NJ
                            src = ps[:, pair * 64:(pair + 1) * 64].rearrange("p (j c) -> p j c", j=NJ)[:, :, 0:NCMP]
                            mk = madd[:, t, 0:NCMP].unsqueeze(1).to_broadcast([P, NJ, NCMP])
                            last = tt(cs_s[:, t, h:h + NJ, 0:NCMP], src, mk, ALU.add)
                        free(last, (1, ("cs", t, par)))
                        wait_read(dve, (1, ("cs", t, par)))
                step(nc.vector.reduce_max(cst16[:], cs_s[:, :, :, 0:NCMP], axis=AX.X))
                for t in range(NT):
                    last = tt(cs_s[:, t, :, 0:NCMP], cs_s[:, t, :, 0:NCMP], cst16[:, t, :].unsqueeze(2).to_broadcast([P, NH, NCMP]), ALU.subtract)
                step(last, sem("cs_ready"))
                dve.wait_ge(sem("cs_exp"), 1)
                for t in range(NT):
                    mk = mmul[:, t, 0:NCMP].unsqueeze(1).to_broadcast([P, NH, NCMP])
                    last = tt(cs_s[:, t, :, 0:NCMP], cs_s[:, t, :, 0:NCMP], mk, ALU.mult)
                step(last)
                step(nc.vector.reduce_sum(cst16[:], cs_s[:, :, :, 0:NCMP], axis=AX.X))
                step(ts(cst16[:], cst16[:], 1e-30, None, ALU.max))
                step(nc.vector.reciprocal(cst16[:], cst16[:]))
                for t in range(NT):
                    last = tt(cs_p[:, t, :, 0:NCMP], cs_s[:, t, :, 0:NCMP], cst16[:, t, :].unsqueeze(2).to_broadcast([P, NH, NCMP]), ALU.mult)
                last.then_inc(sem("pc_ready"), 1)

                def gather_half(br, half):
                    hs = slice(8 * half, 8 * half + 8)
                    if br == 0:
                        dve.wait_ge(sem("pv_half"), half + 1)
                    else:
                        dve.wait_ge(sem("u_pv"), NH * (br - 1) + 8 * (half + 1))
                    for t in range(NT):
                        if br == 0:
                            s = gsig[:, t, hs, 0]
                        else:
                            step(nc.vector.reciprocal(nden[:, t, hs], nden[:, t, hs]))
                            step(tt(cst16[:, t, hs], nden[:, t, hs], gsig[:, t, hs, br], ALU.mult))
                            s = cst16[:, t, hs]
                        s = s.unsqueeze(2).to_broadcast([P, 8, NDH])
                        if br == 0:
                            last = tt(o_v[:, t, hs, :], acc_h[:, t, hs, :], s, ALU.mult)
                        else:
                            tmp = hid_flat[:, 0:512].rearrange("p (h e) -> p h e", h=8)
                            step(tt(tmp, acc_h[:, t, hs, :], s, ALU.mult))
                            last = tt(o_v[:, t, hs, :], o_v[:, t, hs, :], tmp, ALU.add)
                        step(last, sem("o_half") if t == NT - 1 else None)

                gather_half(0, 0)
                gather_half(0, 1)
                dve.wait_ge(sem("pv_half"), 2)
                for t in range(NT):
                    wait_full(dve, (1, ("pcT", t)))
                step(nc.vector.memset(nmax[:], 0.0), sem("pcs_read"))
                for u in range(NUNIT):
                    ps = wait_full(dve, (1, ("US", u)))
                    if u >= 2:
                        dve.wait_ge(sem("u_exp"), u - 1)
                    s = u_s[u % 2]
                    free(tt(s, ps[:, 0:384], cst("mask_ts"), ALU.add), (1, ("US", u)))
                    wait_read(dve, (1, ("US", u)))
                    nc.vector.reduce_max(nmax[:, u % 2, 0:1], s[:, 0:P], axis=AX.X, negate=True)
                    step(nc.vector.reduce_max(nmax[:, u % 2, 1:2], s[:, P:P + T], axis=AX.X, negate=True))
                    ts(nmax[:, u % 2, :], nmax[:, u % 2, :], NDH ** -0.5, None, ALU.mult).then_inc(sem("u_max"), 1)
                    if u >= 10 and (u - 10) % 8 == 0:
                        gather_half(1 + (u - 10) // NH, ((u - 10) // 8) % 2)
                gather_half(2, 1)
                copies_T(1, "nT", mixT)

            def tail(layer):
                copies_T(layer, "xT", xT)
                choose(layer)
                ps = wait_full(dve, (layer, "sh_up"))
                wait_read(dve, (layer, "sh_gate"))
                free(tt(hid[:, 1, :], silu[:, 1, :], ps[:, :], ALU.mult), (layer, "sh_up"))
                assign_slots(layer)
                hot0 = layer * (NE // 2 + 1)
                dve.wait_ge(sem("hot_ready"), hot0 + 1)
                make_weighted(0)
                ps = wait_full(dve, (layer, "xgH"))
                free(copy(xg[:, 4:8, :].rearrange("p k c -> p (k c)"), ps[:, :]), (layer, "xgH"))
                with dve.Fori(0, N_BODIES) as i:
                    def read(ins, g):
                        ins.then_inc(bank_free[loop_bank(layer, g)[0]], 1)

                    def hidden(pair, b):
                        e = 2 * pair + b
                        ps = loop_full(dve, layer, ("gu", e), i)
                        dve.wait_ge(sem("silu_ready"), i * EPB + (layer * NE + e + 1))
                        tt(hid_e[b], sil_e[b], ps[:, 2 * CAP:4 * CAP], ALU.mult).then_inc(sem("hid_ready"), 1)
                        return ps

                    for pair in range(2):
                        if pair == 0:
                            dve.wait_ge(sem("weighted_ready"), i * 2 + (hot0 + 1))
                            make_hot(i * EPB + 2)
                        ps = hidden(pair, 0)
                        dve.wait_ge(sem("hid_ready"), i * EPB + (layer * NE + 2 * pair + 1))
                        read(nc.vector.memset(rsum[:], 0.0), ("gu", 2 * pair))
                        ps = hidden(pair, 1)
                        read(copy(scatter[:], ps[:, 256:512]), ("gu", 2 * pair + 1))
                        dve.wait_ge(sem("hot_ready"), i * 2 + (hot0 + pair + 2))
                        if pair == 0:
                            make_weighted(i * EPB + 2)
                            ps = loop_full(dve, layer, ("xgH", 1), i)
                            read(copy(xg[:, 4:8, :].rearrange("p k c -> p (k c)"), ps[:, :]), ("xgH", 1))
                            dve.wait_ge(sem("weighted_ready"), i * 2 + (hot0 + 2))
                            make_hot(i * EPB + EPB)
                            ps = loop_full(dve, layer, ("y", 0, 1), i)
                            read(copy(y_sb[:, 512:1024], ps[:, :]), ("y", 0, 1))
                        else:
                            make_weighted(i * EPB + EPB)
                            ps = loop_full(dve, layer, ("y", 1, 1), i)
                            read(copy(y_sb[:, 512:1024], ps[:, :]), ("y", 1, 1))
                            ps = loop_full(dve, layer, ("xgH", 0), i)
                            read(copy(xg[:, 4:8, :].rearrange("p k c -> p (k c)"), ps[:, :]), ("xgH", 0))
                s = more[layer]
                dve.wait_ge(sem("weighted_ready"), hot0 + NE // 2 + 1)
                with dve.Fori(0, MORE) as m:
                    block_id = dve.value_load(more_i[0:1, bass.ds(m, 1)], min_val=0, max_val=NE * NBLK - 1)
                    with dve.If(block_id > 0):
                        dve.wait_ge(more_done[layer], m + 1)
                        e = block_id // NBLK
                        ts(shifted[:], slot_of[:, :, bass.ds(e, 1)].rearrange("p t e -> p (t e)"), more_base[:, bass.ds(m, 1)], None,
                           ALU.subtract).then_inc(s["own"], 1)
                        dve.wait_ge(s["own"], m * 2 + 1)
                        iota = cst("iota").unsqueeze(1).to_broadcast([P, NT, CAP])
                        tt(onehot[:, :, 0, :], iota, shifted[:].unsqueeze(2).to_broadcast([P, NT, CAP]), ALU.is_equal).then_inc(s["own"], 1)
                        dve.wait_ge(s["own"], m * 2 + 2)
                        weight = cw[:, :, bass.ds(e, 1)].to_broadcast([P, NT, CAP])
                        tt(weighted_1h[:, :, 0, :], onehot[:, :, 0, :], weight, ALU.mult).then_inc(s["hot"], 1)
                        dve.wait_ge(s["gu"], m + 1)
                        dve.wait_ge(s["silu"], m + 1)
                        tt(hid_e[0], sil_e[0], work[1][:, 2 * CAP:4 * CAP], ALU.mult)
                        copy(scatter[0:CAP, :], work[1][0:CAP, 256:512]).then_inc(s["hid"], 1)
                        dve.wait_ge(s["y"], m + 1)
                        copy(y_sb[0:CAP, 0:512], work[2][0:CAP, :])
                        copy(y_sb[0:CAP, 512:1024], work[3][0:CAP, :]).then_inc(s["y_read"], 1)
                norm(2 * layer + 2)
                copies_T(layer, "xT2", xT)
                ps = wait_full(dve, (layer, "pT"))
                free(copy(pT[:].rearrange("p k t -> p (k t)"), ps[:, :]), (layer, "pT"))
                dve.wait_ge(rows_used, ROWS_BEFORE_LOOP[layer] + NE // 2 + 1)
                for q in range(4):
                    t, c = q // 2, slice((q % 2) * 512, (q % 2 + 1) * 512)
                    wait_read(dve, (layer, ("pg", q)))
                    step(tt(z[:, t, c], sig_o[:, t, c], acc[:, t, c], ALU.mult))
                    last = tt(x[:, t, c], x[:, t, c], z[:, t, c], ALU.add)
                step(last, sem("ple_done"))

            mlstm()
            norm(1)
            tail(0)
            nsa()
            norm(3)
            tail(1)


_INS = ["x", "p", "ln_g", "ln_b", "mlstm_w_in", "mlstm_conv", "mlstm_ig_bias", "mlstm_fg_bias", "mlstm_norm_g",
        "mlstm_w_out", "nsa_w_in", "nsa_cmp_pos_k", "nsa_cmp_pos_v", "nsa_cmp_wk", "nsa_cmp_wv", "nsa_w_out",
        "router_w", "router_bias", "exp_w_gate", "exp_w_up", "exp_w_down", "sh_w_gate", "sh_w_up", "sh_w_down",
        "ple_w", "ple_gate_w"]


def kernel(**inputs):
    import concourse.bacc as _bacc
    from concourse.bass_utils import run_bass_kernel_spmd as _run

    nc = _bacc.Bacc("TRN2", target_bir_lowering=False, num_devices=1)
    arrays, aps = {}, {}
    for name in _INS:
        arr = np.ascontiguousarray(inputs[name])
        arrays[f"in_{name}"] = arr
        aps[name] = nc.dram_tensor(f"in_{name}", arr.shape, mybir.dt.from_np(arr.dtype), kind="ExternalInput").ap()
    arrays["consts"] = CONSTS
    aps["consts"] = nc.dram_tensor("consts", CONSTS.shape, F32, kind="ExternalInput").ap()
    out = nc.dram_tensor("out_0", (1, T, D), F32, kind="ExternalOutput").ap()
    build(nc, aps, out)
    r = _run(nc, [arrays], core_ids=[0])
    return r.results[0]["out_0"]
```

```python
from contextlib import ExitStack

import numpy as np
import concourse.bass as bass
from concourse import mybir

F32 = mybir.dt.float32
BF16 = mybir.dt.bfloat16
I32 = mybir.dt.int32
ALU = mybir.AluOpType
ACT = mybir.ActivationFunctionType
AX = mybir.AxisListType

P = 128
D = 1024
T = 256
NT = T // P
KD = D // P
DEPTH = 2
ALPHA = (2.0 * DEPTH) ** 0.25
EPS = 1e-5
BIG = 1e30

MH, MDK, MDV, MCONV = 8, 64, 128, 4
NH, NG, NDH = 16, 4, 64
NJ = NH // NG
CSTR, CBLK = 16, 32
NCMP = T // CSTR - 1
NE, TOPK, NEG, TOPG, FF = 64, 8, 8, 4, 256
SCALE_R = 2.5
PLE = 256

SLOT = 2048
RING = 12
EPB = 4
CAP = 64
NBLK = T // CAP
NE_PAD = NE + 2
MORE = 32
MORE_PART, MORE_RUN = 16, 4
NB_WORK = 4


def tail_groups(layer):
    before = ["pT"] + [("xT", g) for g in range(4)] + ["logits", "sh_gate", "sh_up", "xgL", "xgH", "rank"]
    after = [("pw", q) for q in range(4)]
    return [(layer, g) for g in before], [(layer, g) for g in after]


def mlstm_groups():
    heads = [("S", 0)]
    for h in range(MH):
        heads += ([("S", h + 1)] if h + 1 < MH else []) + [("num", h)]
    return ([("x0T", g) for g in range(4)] + ["gates", "convT"] + [("qk", g) for g in range(4)] + ["gateT"]
            + [("B", g) for g in range(4)] + [("v", g) for g in range(4)] + [("o", g) for g in range(4)]
            + heads + [("mT", g) for g in range(4)])


def nsa_groups():
    units = []
    for w in range(NPAIR + 1):
        for i in range(2):
            units += ([("US", w, i)] if w < NPAIR else []) + ([("UT", w - 1, i)] if w else [])
    return ([("x1T", g) for g in range(4)] + ["g", "pos"]
            + ["q0", "q1", "rq0", "q2", "rq1", "q3", "rq2", "kc", "rq3", "vc", "ks", "kw", "rks", "rkw", "cmp0", "cmp1", "vs"]
            + ["kcrot", "vcT", ("cs", 0), ("cs", 1), "vw", ("pcT", 0), ("pcT", 1)] + units)


NSA_PIECES = {"q0": 0, "q1": 1, "q2": 2, "q3": 3, "kc": 4, "vc": 5, "ks": 6, "kw": 8, "vs": 7, "vw": 9}
NPAIR = NH
BODY_GROUPS = [("gu", 0), ("xgL", 1), ("xgH", 1), ("turn", 0), ("gu", 1), ("y", 0, 0), ("y", 0, 1),
               ("turn", 1), ("y", 1, 0), ("xgL", 0), ("xgH", 0), ("y", 1, 1)]
LOOP_GROUPS = len(BODY_GROUPS)
N_BODIES = NE // EPB

AT, LOOP_AT = {}, []
_n = 0
for _layer, _mixer in enumerate((mlstm_groups(), nsa_groups())):
    _before, _after = tail_groups(_layer)
    for _g in [(_layer, g) for g in _mixer] + _before:
        AT[_g] = _n
        _n += 1
    LOOP_AT.append(_n)
    _n += LOOP_GROUPS * N_BODIES
    for _g in _after:
        AT[_g] = _n
        _n += 1

PIECES_MIX = (12, 10)
LOOP_PIECES = 3 * EPB
PIECE_LOOP, PIECE_MIX, PIECE_OUT, PIECE_SH, PIECE_PLE = [], [], [], [], []
_n = 0
for _layer in range(DEPTH):
    PIECE_MIX.append(_n)
    _n += PIECES_MIX[_layer]
    PIECE_OUT.append(_n)
    _n += 4
    PIECE_SH.append(_n)
    _n += 3
    PIECE_LOOP.append(_n)
    _n += LOOP_PIECES * N_BODIES
    PIECE_PLE.append(_n)
    _n += 5


def landed_value(n):
    extra = sum(3 for first in (PIECE_MIX[1], PIECE_OUT[1]) for m in range(first, first + 4) if m <= n and m % RING == n % RING)
    return 16 * (n // RING + 1 + extra)


MORE_PIECE = [n + 5 for n in PIECE_PLE]


BODY = [(k, e) for pair in range(2) for e in (2 * pair, 2 * pair + 1) for k in "gu"] + [("d", e) for e in range(EPB)]

USED = {}
_rows = 0
ROWS_BEFORE_LOOP = []
for _layer in range(DEPTH):
    _names = ([("qk", g) for g in range(4)] + [("v", g) for g in range(4)] + [("o", g) for g in range(4)] if _layer == 0
              else list(NSA_PIECES))
    for _j, _g in enumerate(_names):
        USED[PIECE_MIX[_layer] + _j] = ("bank", AT[(_layer, _g)])
    for _j in range(4):
        _rows += 1
        USED[PIECE_OUT[_layer] + _j] = ("rows", _rows)
    USED[PIECE_SH[_layer]] = ("bank", AT[(_layer, "sh_gate")])
    USED[PIECE_SH[_layer] + 1] = ("bank", AT[(_layer, "sh_up")])
    _rows += 1
    USED[PIECE_SH[_layer] + 2] = ("rows", _rows)
    ROWS_BEFORE_LOOP.append(_rows)
    for _i in range(N_BODIES):
        for _j, (_kind, _e) in enumerate(BODY):
            _g = ("y", _e // 2, 1) if _kind == "d" else ("gu", _e // 2)
            USED[PIECE_LOOP[_layer] + _i * LOOP_PIECES + _j] = ("bank", LOOP_AT[_layer] + _i * LOOP_GROUPS + BODY_GROUPS.index(_g))
    USED[PIECE_PLE[_layer]] = ("bank", AT[(_layer, ("pw", 3))])
    for _j in range(1, 4):
        _rows += 1
        USED[PIECE_PLE[_layer] + _j] = ("rows", _rows)
    USED[PIECE_PLE[_layer] + 4] = ("pg", 4 * (_layer + 1))


CONST_COLS = {}


def constants():
    parts = []

    def add(name, a):
        a = np.asarray(a, np.float32).reshape(P, -1)
        at = sum(x.shape[1] for x in parts)
        CONST_COLS[name] = (at, at + a.shape[1])
        parts.append(a)

    idx = np.arange(P)
    add("ident", np.eye(P))
    rot = np.zeros((P, P))
    for m in range(P):
        if m % NDH < NDH // 2:
            rot[m + NDH // 2, m] = -1.0
        else:
            rot[m - NDH // 2, m] = 1.0
    add("rot", rot)
    tri_s = np.where(idx[:, None] <= idx[None, :], 0.0, -BIG)
    add("mask_st", np.concatenate([tri_s, np.zeros((P, P))], 1))
    add("mask_ts", tri_s.T)
    sel = np.zeros((P, MH, P))
    for h in range(MH):
        sel[h, h, :] = 1.0
    add("sel", sel)
    half = NDH // 2
    inv = (np.float32(10000.0) ** (-np.arange(half, dtype=np.float32) / np.float32(half))).astype(np.float32)

    def table(pos):
        ang = pos.astype(np.float32)[None, :] * inv[idx % half][:, None]
        return np.cos(ang.astype(np.float32)), np.sin(ang.astype(np.float32))

    cos, sin = table(np.arange(T))
    add("cos", cos)
    add("sin", sin)
    end = np.arange(CSTR) * CSTR + CBLK - 1
    cos, sin = table(end)
    add("cos_c", cos)
    add("sin_c", sin)
    t = idx[:, None, None] + P * np.arange(NT)[None, :, None]
    ok = end[None, None, :] <= t
    add("cmask_add", np.where(ok, 0.0, -BIG))
    add("cmask_mul", np.where(ok, 1.0, 0.0))
    add("iota", np.broadcast_to(np.arange(CAP)[None, :], (P, CAP)))
    add("earlier", idx[:, None] < idx[None, :])
    add("ones", np.ones((P, P)))
    b = np.arange(1, NBLK)[None, :]
    add("blk_floor", np.broadcast_to(CAP * b, (P, NE, NBLK - 1)))
    add("blk_id", np.broadcast_to(NBLK * np.arange(NE)[:, None] + b, (P, NE, NBLK - 1)))
    add("before", np.broadcast_to(np.arange(NEG)[None, :] < np.arange(NEG)[:, None], (P, NEG, NEG)))
    return np.concatenate(parts, 1)


CONSTS = constants()


class Chain:

    def __init__(self, eng, semaphore):
        self.eng, self.sem, self.n = eng, semaphore, {}

    def step(self, ins, semaphore=None):
        s = semaphore or self.sem
        self.n[str(s)] = n = self.n.get(str(s), 0) + 1
        ins.then_inc(s, 1)
        self.eng.wait_ge(s, n)


def build(nc, a, out):
    ctx = ExitStack()
    with ctx:
        def sb(name, shape, dt=F32):
            return ctx.enter_context(nc.sbuf_tensor(name, shape, dt))

        sems = {}

        def sem(name):
            if name not in sems:
                sems[name] = ctx.enter_context(nc.semaphore(name))
            return sems[name]

        ring = sb("ring", [P, RING, SLOT])
        x = sb("x", [P, NT, D])
        xT = sb("xT", [P, KD, T])
        z = sb("z", [P, NT, D])
        bufA = sb("bufA", [P, 2048])
        bufB = sb("bufB", [P, NT * MH * (MDV + 1)])
        bufC = sb("bufC", [P, 2048])
        bufD = sb("bufD", [P, 2048])
        ln_p = sb("ln_p", [P, 2, D])
        const = sb("const", [P, CONSTS.shape[1]])
        router = sb("router", [P, KD, NE])
        rbias = sb("rbias", [P, NE])
        silu = sb("silu", [P, 2, 512])
        hid = sb("hid", [P, 2, 512])
        scratch = sb("scratch", [P, 512])
        p_in = sb("p_in", [P, NT, PLE])
        pT = sb("pT", [P, 2, T])
        wgates = sb("wgates", [P, KD, 48])
        onehot = sb("onehot", [P, NT, 2, CAP], BF16)
        weighted_1h = sb("weighted_1h", [P, NT, 2, CAP])
        slot_of = sb("slot_of", [P, NT, NE_PAD])
        more_cand = sb("more_cand", [P, NE, NBLK - 1])
        more_f = sb("more_f", [P, MORE])
        more_i = sb("more_i", [P, MORE], I32)
        more_blk = sb("more_blk", [P, MORE], I32)
        more_base = sb("more_base", [P, MORE])
        shifted = sb("shifted", [P, NT])
        score = sb("score", [P, NT, NE])
        biased = sb("biased", [P, NT, NE])
        cand = sb("cand", [P, NT, NE])
        cw = sb("cw", [P, NT, NE_PAD])
        top8 = sb("top8", [P, NT, 8])
        grp8 = sb("grp8", [P, NT * NEG, 8])
        grp = sb("grp", [P, NT * NEG])
        rank = sb("rank", [P, NT * NEG])
        gcmp = sb("gcmp", [P, NT, NEG, NEG])
        geq = sb("geq", [P, NT, NEG, NEG])
        rsum = sb("rsum", [P, NT])
        lnst = sb("lnst", [P, NT, 2, 6])
        lnmv = sb("lnmv", [P, NT, 2])
        conv_in = sb("conv_in", [32, P])
        conv_w = sb("conv_w", [P, 32])
        gbias = sb("gbias", [MH, 2])
        gtok = sb("gtok", [P, 4, MH])
        den2 = sb("den2", [P, 2])
        hmv = sb("hmv", [P, NT, MH, 2])
        hst = sb("hst", [P, NT, 6])
        hbias = sb("hbias", [P, MH])
        pos_in = sb("pos_in", [CBLK, 2, P])
        posT = sb("posT", [P, 2, CBLK])
        kc_raw = sb("kc_raw", [P, 2, 16])
        kc_rot = sb("kc_rot", [P, 2, 16])
        kcT = sb("kcT", [P, 2, 2, 16])
        kc_t = sb("kc_t", [P, 2, 16])
        gsig = sb("gsig", [P, NT, NH, 3])
        cst16 = sb("cst16", [P, NT, NH])
        nden = sb("nden", [P, NT, NH])
        nmax = sb("nmax", [P, 2, 2, NT])
        ident_bf = sb("ident_bf", [P, P], BF16)
        later_bf = sb("later_bf", [P, P], BF16)
        acc = ctx.enter_context(nc.psum_tensor("acc", [P, NT, D], F32))
        work = [ctx.enter_context(nc.psum_tensor(f"work{b}", [P, 512], F32)) for b in range(NB_WORK)]

        def cst(name):
            lo, hi = CONST_COLS[name]
            return const[:, lo:hi]

        ident = cst("ident")

        landed = [sem(f"landed{s}") for s in range(RING)]
        rows_used = sem("rows_used")
        bank_full = [sem(f"bank_full{b}") for b in range(NB_WORK)]
        bank_free = [sem(f"bank_free{b}") for b in range(NB_WORK)]
        loop_uses = LOOP_GROUPS // NB_WORK

        more_landed = [[sem(f"more_landed{layer}{k}") for k in "gud"] for layer in range(DEPTH)]
        more_done = [sem(f"more_done{layer}") for layer in range(DEPTH)]
        more = [{n: sem(f"more_{n}{layer}") for n in ("hot", "xg", "xg_read", "gu", "silu", "hid", "turn", "turn_read", "y", "y_read", "own")} for layer in range(DEPTH)]

        def loop_bank(layer, g):
            n = LOOP_AT[layer] + BODY_GROUPS.index(g)
            return n % NB_WORK, n // NB_WORK

        def loop_full(eng, layer, g, i):
            b, use = loop_bank(layer, g)
            eng.wait_ge(bank_full[b], i * loop_uses + (use + 1))
            return work[b]

        def loop_wait_free(pe, layer, g, i):
            b, use = loop_bank(layer, g)
            pe.wait_ge(bank_free[b], i * loop_uses + use)
            return work[b]

        def loop_read(eng, layer, g, i, last_body=False):
            b, use = loop_bank(layer, g)
            eng.wait_ge(bank_free[b], i * loop_uses + (use + 1 - (loop_uses if last_body else 0)))

        def full(ins, g):
            return ins.then_inc(bank_full[AT[g] % NB_WORK], 1)

        def wait_full(eng, g):
            eng.wait_ge(bank_full[AT[g] % NB_WORK], AT[g] // NB_WORK + 1)
            return work[AT[g] % NB_WORK]

        def free(ins, g):
            return ins.then_inc(bank_free[AT[g] % NB_WORK], 1)

        def wait_free(pe, g):
            if AT[g] >= NB_WORK:
                pe.wait_ge(bank_free[AT[g] % NB_WORK], AT[g] // NB_WORK)
            return work[AT[g] % NB_WORK]

        def wait_read(eng, g):
            eng.wait_ge(bank_free[AT[g] % NB_WORK], AT[g] // NB_WORK + 1)

        qk = bufA[:].rearrange("p (c t) -> p c t", c=8)
        v_aug = bufB[:].rearrange("p (t h e) -> p t h e", t=NT, h=MH)
        sig_o = bufC[:].rearrange("p (t c) -> p t c", t=NT)
        hm = bufD[:].rearrange("p (t h e) -> p t h e", t=NT, h=MH)
        hm_flat = bufD[:].rearrange("p (t c) -> p t c", t=NT)
        gbuf = bufD[0:MH, :].rearrange("p (r t) -> p r t", r=8)
        mixT = bufA[:].rearrange("p (k t) -> p k t", k=KD)
        z_flat = z[:].rearrange("p t c -> p (t c)")
        silu_flat = silu[:].rearrange("p b c -> p (b c)")
        hid_flat = hid[:].rearrange("p b c -> p (b c)")

        def decay(h):
            if h < 5:
                return z_flat[:, 384 * h:384 * (h + 1)]
            if h < 7:
                return silu_flat[:, 384 * (h - 5):384 * (h - 4)]
            return hid_flat[:, 0:384]

        pt_m = [hid_flat[:, 384:768], scratch[:, 0:384]]
        cmp_w = [z_flat.rearrange("p (l e) -> p l e", e=NDH), bufD[:].rearrange("p (l e) -> p l e", e=NDH)]
        kp = bufC[:].rearrange("p (v half g t) -> p v half g t", v=2, half=2, g=2)
        kT_sw = bufB[:, 0:1024].rearrange("p (s g t) -> p s g t", s=2, g=2)
        v_sw = bufB[:, 1024:2048].rearrange("p (s t c) -> p s t c", s=2, t=NT)
        acc_pair = acc[:].rearrange("p t (w q) -> p (t w) q", q=T)
        cs_s = hid_flat[:, 0:512].rearrange("p (t h c) -> p t h c", t=NT, h=NH)
        cs_p = silu_flat.rearrange("p (t h c) -> p t h c", t=NT, h=NH)
        vrep_in = scratch[:, 0:256].rearrange("p (g r c) -> p g r c", g=2, r=4)
        v_blk = z_flat[:, 1024:2048].rearrange("p (g j e) -> p g j e", g=NG, j=NJ)
        pcT = bufD[:, 1024:2048].rearrange("p (t g c) -> p t g c", t=NT, g=NG)
        u_p = [v[:, 0:768].rearrange("p (i c) -> p i c", i=2) for v in (silu_flat, z_flat)]
        u_pT = [bufD[:, lo:lo + 768].rearrange("p (i c) -> p i c", i=2) for lo in (0, 1024)]

        def pair_heads(w):
            half, j = w % 8 // 4, w % 4
            return [(2 * half + i) * NJ + j for i in range(2)]

        def head_rows(h):
            g = h // NJ
            return slice((g % 2) * NDH, (g % 2 + 1) * NDH), g // 2, (g // 2) * NJ + h % NJ

        x_part = [bufA[:].bitcast(BF16).rearrange("p (s t d) -> p s t d", s=2, t=NT)[:, s] for s in range(2)]
        x_part.append(bufC[:].bitcast(BF16).rearrange("p (s t d) -> p s t d", s=2, t=NT)[:, 0])
        x_rest = bufD[:].rearrange("p (t d) -> p t d", t=NT)
        xg = z[:, 1, :].rearrange("p (k c) -> p k c", k=KD)
        y_sb = z[:, 0, :]
        sil_e, hid_e = silu[:, 0, 0:FF], silu[:, 0, FF:2 * FF]
        turned_e = [hid[:, pair, :] for pair in range(2)]

        block = ctx.enter_context(nc.Block())

        @block.sync
        def _(sp):
            def col(w, lo):
                return w.rearrange("(p k) n -> p k n", k=KD)[:, :, lo:lo + 256]

            def row(w, j, k=KD):
                return w.rearrange("(p k) n -> p k n", k=k)[:, 2 * j:2 * j + 2, :]

            def wait_slot(n, i=0):
                if n >= RING:
                    how, at = USED[n - RING]
                    if how == "rows":
                        sp.wait_ge(rows_used, at)
                    elif how == "pg":
                        sp.wait_ge(sem("pg_full"), at)
                    else:
                        sp.wait_ge(bank_full[at % NB_WORK], i * (LOOP_GROUPS // NB_WORK) + (at // NB_WORK + 1))

            def load(n, src):
                wait_slot(n)
                dst = ring[:, n % RING, :].rearrange("p (k n) -> p k n", k=src.shape[1])
                sp.dma_start(dst, src).then_inc(landed[n % RING], 16)

            sp.dma_start(x[:, 0], a["x"][0, 0:P]).then_inc(sem("ld_x0"), 16)
            sp.dma_start(const[:, 0:P], a["consts"][:, 0:P]).then_inc(sem("ld_ident"), 16)
            sp.dma_start(x[:, 1], a["x"][0, P:T]).then_inc(sem("ld_x1"), 16)
            for layer in range(DEPTH):
                w_in = a["mlstm_w_in" if layer == 0 else "nsa_w_in"][0]
                w_out = a["mlstm_w_out" if layer == 0 else "nsa_w_out"][0]
                n0 = PIECE_MIX[layer]
                for j in range(PIECES_MIX[layer]):
                    if layer == 1 and j < 4:
                        wait_slot(n0 + j)
                        dst = ring[:, (n0 + j) % RING, :].rearrange("p (k c g n) -> p k c g n", k=KD, c=2, g=2)
                        for c in range(2):
                            for par in range(2):
                                lo = ((2 * (j // 2) + par) * NJ + (j % 2) * 2 + c) * NDH
                                src = w_in.rearrange("(p k) n -> p k n", k=KD)[:, :, lo:lo + NDH]
                                sp.dma_start(dst[:, :, c, par, :], src).then_inc(landed[(n0 + j) % RING], 16)
                    else:
                        load(n0 + j, col(w_in, 256 * (j if layer == 0 else list(NSA_PIECES.values())[j])))
                for j in range(4):
                    if layer == 0:
                        load(PIECE_OUT[0] + j, row(w_out, j))
                        continue
                    n = PIECE_OUT[1] + j
                    wait_slot(n)
                    for c in range(2):
                        for i, h in enumerate(pair_heads(2 * j + c)):
                            dst = ring[i * NDH:(i + 1) * NDH, n % RING, c * D:(c + 1) * D]
                            sp.dma_start(dst, w_out[h * NDH:(h + 1) * NDH, :]).then_inc(landed[n % RING], 16)
                load(PIECE_SH[layer], col(a["sh_w_gate"][layer], 0))
                load(PIECE_SH[layer] + 1, col(a["sh_w_up"][layer], 0))
                load(PIECE_SH[layer] + 2, row(a["sh_w_down"][layer], 0, 2))
                n0 = PIECE_LOOP[layer]
                exp_w = {k: a[n][layer] for k, n in (("g", "exp_w_gate"), ("u", "exp_w_up"), ("d", "exp_w_down"))}
                for j, (kind, e) in enumerate(BODY):
                    wait_slot(n0 + j)
                    src = exp_w[kind][e].rearrange("(p k) n -> p (k n)", p=P)
                    sp.dma_start(ring[:, (n0 + j) % RING, :], src).then_inc(landed[(n0 + j) % RING], 16)
                with sp.Fori(0, N_BODIES - 1) as i:
                    for j, (kind, e) in enumerate(BODY):
                        wait_slot(n0 + LOOP_PIECES + j, i)
                        src = exp_w[kind][bass.ds(i * EPB + (EPB + e), 1)].rearrange("a (p k) n -> p (a k n)", p=P)
                        sp.dma_start(ring[:, (n0 + j) % RING, :], src).then_inc(landed[(n0 + j) % RING], 16)
                n0 = PIECE_PLE[layer]
                load(n0, row(a["ple_w"][layer], 0, 2))
                for j in range(4):
                    load(n0 + 1 + j, row(a["ple_gate_w"][layer], j))
                n0 = MORE_PIECE[layer]
                for j in range(3):
                    wait_slot(n0 + j)
                sp.wait_ge(more_done[layer], 1)
                with sp.Fori(0, MORE // MORE_PART) as part:
                    part_id = sp.value_load(more_i[0:1, bass.ds(part * MORE_PART, 1)], min_val=0, max_val=NE * NBLK - 1)
                    with sp.If(part_id > 0):
                        with sp.Fori(0, MORE_PART // MORE_RUN) as run:
                            run_id = sp.value_load(more_i[0:1, bass.ds(part * MORE_PART + run * MORE_RUN, 1)], min_val=0, max_val=NE * NBLK - 1)
                            with sp.If(run_id > 0):
                                with sp.Fori(0, MORE_RUN) as at:
                                    m = part * MORE_PART + run * MORE_RUN + at
                                    block_id = sp.value_load(more_i[0:1, bass.ds(m, 1)], min_val=0, max_val=NE * NBLK - 1)
                                    with sp.If(block_id > 0):
                                        sp.wait_ge(more_done[layer], m + 1)
                                        for j, kind in enumerate("gud"):
                                            src = exp_w[kind][bass.ds(block_id // NBLK, 1)].rearrange("a (p k) n -> p (a k n)", p=P)
                                            sp.dma_start(ring[:, (n0 + j) % RING, :], src).then_inc(more_landed[layer][j], 16)
                sp.wait_ge(sem("experts_done"), layer + 1)
            for t in range(NT):
                sp.wait_ge(sem("ple_done"), NT * (DEPTH - 1) + t + 1)
                sp.dma_start(out[0, t * P:(t + 1) * P], x[:, t]).then_inc(sem("stored"), 16)
            sp.wait_ge(sem("stored"), 16 * NT)

        @block.gpsimd
        def _(pool):
            in_w = [a[n][0].rearrange("(p k) n -> p k n", k=KD) for n in ("mlstm_w_in", "nsa_w_in")]
            pool.dma_start(wgates[:, :, 0:16], in_w[0][:, :, 3072:3088]).then_inc(sem("ld_gw"), 16)
            pool.dma_start(conv_in[:], a["mlstm_conv"][0].rearrange("j (c q) -> (j c) q", q=P)).then_inc(sem("ld_conv"), 16)
            pool.dma_start(gbias[:, 0:1], a["mlstm_ig_bias"].rearrange("a h -> h a")).then_inc(sem("ld_gbias"), 16)
            pool.dma_start(gbias[:, 1:2], a["mlstm_fg_bias"].rearrange("a h -> h a")).then_inc(sem("ld_gbias"), 16)
            pool.dma_start(const[:, P:], a["consts"][:, P:]).then_inc(sem("ld_const"), 16)
            pool.memset(v_aug[:, :, :, MDV:MDV + 1], 1.0).then_inc(sem("ones_v"), 1)
            pool.dma_start(ln_p[:, 0, :], a["mlstm_norm_g"][0].partition_broadcast(P)).then_inc(sem("ld_norm"), 16)
            for layer in range(DEPTH):
                if layer:
                    pool.wait_ge(sem("cw_ready"), layer)
                pool.dma_start(router[:], a["router_w"][layer].rearrange("(p k) n -> p k n", k=KD)).then_inc(sem("ld_router"), 16)
                pool.dma_start(rbias[:], a["router_bias"][layer].partition_broadcast(P)).then_inc(sem("ld_router"), 16)
                if layer == 1:
                    wait_read(pool, (0, "gates"))
                    pool.dma_start(wgates[:], in_w[1][:, :, 2560:2608]).then_inc(sem("ld_gw"), 16)
                    for i, n in enumerate(("nsa_cmp_pos_k", "nsa_cmp_pos_v")):
                        for par in range(2):
                            pool.dma_start(pos_in[:, i, par * NDH:(par + 1) * NDH], a[n][0]).then_inc(sem("ld_pos"), 16)
                    pool.wait_ge(sem("ple_done"), NT)
                    for i, n in enumerate(("nsa_cmp_wk", "nsa_cmp_wv")):
                        for par in range(2):
                            dst = cmp_w[i][par * NDH:(par + 1) * NDH]
                            pool.dma_start(dst, a[n][0].rearrange("l d e -> d l e")).then_inc(sem("ld_cmpw"), 16)
                for k in range(2):
                    if layer or k:
                        pool.wait_ge(sem("ln_done"), NT * (2 * layer + k))
                    else:
                        pool.wait_ge(sem("norm_g_used"), 1)
                    pool.dma_start(ln_p[:, 0, :], a["ln_g"][layer, k].partition_broadcast(P)).then_inc(sem("ld_ln"), 16)
                    pool.dma_start(ln_p[:, 1, :], a["ln_b"][layer, k].partition_broadcast(P)).then_inc(sem("ld_ln"), 16)
                    if k == 0:
                        if layer:
                            wait_read(pool, (0, "pT"))
                        pool.dma_start(p_in[:], a["p"][layer, 0].rearrange("(t p) d -> p t d", p=P)).then_inc(sem("ld_p"), 16)
                        pool.wait_ge(sem("x_part"), 3 * layer + 1)
                        tt = nc.gpsimd.tensor_tensor
                        tt(x_rest, x[:], x_part[0], ALU.subtract).then_inc(sem("x_rest"), 1)
                        pool.wait_ge(sem("x_part"), 3 * layer + 2)
                        tt(x_rest, x_rest, x_part[1], ALU.subtract).then_inc(sem("x_rest"), 1)

        @block.tensor
        def _(pe):
            mm = nc.tensor.matmul

            def turn_tile(banks, src, t):
                last = []
                for half in range(2):
                    for k in range(4):
                        ins = nc.tensor.transpose(banks[half][:, k * P:(k + 1) * P], src[:, t, 4 * half + k::KD], ident)
                    last.append(ins)
                return last

            def transposes(layer, name, src, ready):
                for t in range(NT):
                    pe.wait_ge(*ready[t])
                    groups = [(layer, (name, 2 * t + half)) for half in range(2)]
                    for g, last in zip(groups, turn_tile([wait_free(pe, g) for g in groups], src, t)):
                        full(last, g)

            def piece(n):
                pe.wait_ge(landed[n % RING], landed_value(n))
                return ring[:, n % RING, :]

            def proj_T(layer, name, n, interleaved=False):
                w = piece(n).rearrange("p (k c) -> p k c", k=KD)
                ps = wait_free(pe, (layer, name))
                for c in range(2):
                    cols = slice(c, None, 2) if interleaved else slice(c * P, (c + 1) * P)
                    for k in range(KD):
                        last = mm(ps[:, c * T:(c + 1) * T], w[:, k, cols], xT[:, k, :], start=(k == 0), stop=(k == KD - 1))
                full(last, (layer, name))

            def proj_tok(layer, name, n):
                w = piece(n).rearrange("p (k c) -> p k c", k=KD)
                ps = wait_free(pe, (layer, name))
                for t in range(NT):
                    for k in range(KD):
                        last = mm(ps[:, t * 256:(t + 1) * 256], xT[:, k, t * P:(t + 1) * P], w[:, k, :], start=(k == 0), stop=(k == KD - 1))
                full(last, (layer, name))

            def rows_to_acc(srcT, n, j, first, last_piece):
                w = piece(n).rearrange("p (k c) -> p k c", k=2)
                for i in range(2):
                    for t in range(NT):
                        for half in range(2):
                            last = mm(acc[:, t, half * 512:(half + 1) * 512], srcT[:, 2 * j + i, t * P:(t + 1) * P],
                                      w[:, i, half * 512:(half + 1) * 512], start=(first and i == 0), stop=(last_piece and i == 1))
                return last.then_inc(rows_used, 1)

            def wait_tile(layer, name, t):
                for half in range(2):
                    wait_read(pe, (layer, (name, 2 * t + half)))

            def out_projection(layer, mix_tile_ready):
                for t in range(NT):
                    mix_tile_ready(t)
                    for j in range(4):
                        w = piece(PIECE_OUT[layer] + j).rearrange("p (k c) -> p k c", k=2)
                        for i in range(2):
                            for half in range(2):
                                last = mm(acc[:, t, half * 512:(half + 1) * 512], mixT[:, 2 * j + i, t * P:(t + 1) * P],
                                          w[:, i, half * 512:(half + 1) * 512], start=(j == 0 and i == 0), stop=(j == 3 and i == 1))
                        if t == NT - 1:
                            last.then_inc(rows_used, 1)
                        elif j == 3:
                            last.then_inc(sem("out_tile0"), 1)

            def mlstm():
                pe.wait_ge(sem("ld_ident"), 16)
                transposes(0, "x0T", x[:], [(sem("ld_x0"), 16), (sem("ld_x1"), 16)])
                for g in range(4):
                    wait_read(pe, (0, ("x0T", g)))
                pe.wait_ge(sem("ld_gw"), 16)
                ps = wait_free(pe, (0, "gates"))
                for i in range(2):
                    for k in range(KD):
                        last = mm(ps[0:MH, i * T:(i + 1) * T], wgates[:, k, i * MH:(i + 1) * MH], xT[:, k, :], start=(k == 0), stop=(k == KD - 1))
                full(last, (0, "gates"))
                pe.wait_ge(sem("ld_conv"), 16)
                ps = wait_free(pe, (0, "convT"))
                full(nc.tensor.transpose(ps[:, 0:32], conv_in[:], ident[0:32, 0:32]), (0, "convT"))
                for g in range(4):
                    proj_T(0, ("qk", g), PIECE_MIX[0] + g)
                pe.wait_ge(sem("grows"), 1)
                pe.wait_ge(sem("ld_const"), 16)
                ps = wait_free(pe, (0, "gateT"))
                for i, r in enumerate((4, 6)):
                    for t in range(NT):
                        last = nc.tensor.transpose(ps[:, (2 * i + t) * MH:(2 * i + t + 1) * MH], gbuf[:, r, t * P:(t + 1) * P], ident[0:MH, 0:MH])
                full(last, (0, "gateT"))
                for g in range(4):
                    ps = wait_free(pe, (0, ("B", g)))
                    for i in range(2):
                        h = 2 * g + i
                        last = mm(ps[:, i * T:(i + 1) * T], cst("sel")[0:MH, h * P:(h + 1) * P], gbuf[:, 5, :], start=True, stop=True)
                    full(last, (0, ("B", g)))
                for g in range(4):
                    proj_tok(0, ("v", g), PIECE_MIX[0] + 4 + g)
                for g in range(4):
                    proj_tok(0, ("o", g), PIECE_MIX[0] + 8 + g)

                pe.wait_ge(sem("qk_ready"), 4)
                pe.wait_ge(sem("ones_v"), 1)

                def scores(h):
                    rows, tile = slice((h % 2) * MDK, (h % 2 + 1) * MDK), h // 2
                    ps = wait_free(pe, (0, ("S", h)))
                    mm(ps[:, 0:T], qk[rows, 4 + tile, 0:P], qk[rows, tile, :], start=True, stop=True)
                    last = mm(ps[:, T:T + P], qk[rows, 4 + tile, P:T], qk[rows, tile, P:T], start=True, stop=True)
                    full(last, (0, ("S", h)))

                scores(0)
                for h in range(MH):
                    if h + 1 < MH:
                        scores(h + 1)
                    wait_read(pe, (0, ("S", h)))
                    if h == 0:
                        for g in range(4):
                            wait_read(pe, (0, ("v", g)))
                    ps = wait_free(pe, (0, ("num", h)))
                    pt = pt_m[h % 2]
                    mm(ps[:, 0:MDV + 1], pt[:, 0:P], v_aug[:, 0, h, :], start=True, stop=True)
                    mm(ps[:, 256:256 + MDV + 1], pt[:, P:T], v_aug[:, 0, h, :], start=True, stop=False)
                    full(mm(ps[:, 256:256 + MDV + 1], pt[:, T:T + P], v_aug[:, 1, h, :], start=False, stop=True), (0, ("num", h)))
                transposes(0, "mT", hm_flat, [(sem("mix_ready"), t + 1) for t in range(NT)])
                out_projection(0, lambda t: wait_tile(0, "mT", t))

            def nsa():
                transposes(1, "x1T", x[:], [(sem("ple_done"), t + 1) for t in range(NT)])
                pe.wait_ge(sem("ld_gw"), 32)
                ps = wait_free(pe, (1, "g"))
                for t in range(NT):
                    wait_tile(1, "x1T", t)
                    for k in range(KD):
                        last = mm(ps[:, t * 48:(t + 1) * 48], xT[:, k, t * P:(t + 1) * P], wgates[:, k, :], start=(k == 0), stop=(k == KD - 1))
                full(last, (1, "g"))
                pe.wait_ge(sem("ld_pos"), 64)
                ps = wait_free(pe, (1, "pos"))
                for i in range(2):
                    last = nc.tensor.transpose(ps[:, i * CBLK:(i + 1) * CBLK], pos_in[:, i, :], ident[0:CBLK, 0:CBLK])
                full(last, (1, "pos"))

                def rotate(name, raw, n):
                    wait_read(pe, (1, ("q0", "q1", "q2", "q3", "ks", "kw")[n - 1]))
                    ps = wait_free(pe, (1, name))
                    full(mm(ps[:, :], cst("rot"), raw, start=True, stop=True), (1, name))

                m0 = PIECE_MIX[1]
                proj_T(1, "q0", m0 + 0)
                proj_T(1, "q1", m0 + 1)
                rotate("rq0", silu[:, 0, :], 1)
                proj_T(1, "q2", m0 + 2)
                rotate("rq1", silu[:, 1, :], 2)
                proj_T(1, "q3", m0 + 3)
                rotate("rq2", silu[:, 0, :], 3)
                proj_T(1, "kc", m0 + 4)
                rotate("rq3", silu[:, 1, :], 4)
                proj_T(1, "vc", m0 + 5)
                proj_T(1, "ks", m0 + 6)
                proj_T(1, "kw", m0 + 7)
                rotate("rks", silu[:, 0, :], 5)
                rotate("rkw", silu[:, 1, :], 6)
                pe.wait_ge(sem("ld_cmpw"), 64)
                wait_read(pe, (1, "kc"))
                wait_read(pe, (1, "vc"))
                banks = [wait_free(pe, (1, f"cmp{par}")) for par in range(2)]
                for i in range(2):
                    for l in range(CBLK):
                        half, at = l // CSTR, l % CSTR
                        lo = at + half * CSTR
                        for par in range(2):
                            rows = slice(par * NDH, (par + 1) * NDH)
                            src = kp[rows, i, half, :, lo:lo + (NCMP - 1) * CSTR + 1:CSTR]
                            dst = banks[par][rows, i * 32:i * 32 + 2 * NCMP].rearrange("p (g c) -> p g c", g=2)
                            last = mm(dst, cmp_w[i][rows, l, :], src, start=(l == 0), stop=(l == CBLK - 1))
                            if i == 1 and l == CBLK - 1:
                                full(last, (1, f"cmp{par}"))
                proj_tok(1, "vs", m0 + 8)
                for par in range(2):
                    wait_read(pe, (1, f"cmp{par}"))
                ps = wait_free(pe, (1, "kcrot"))
                full(mm(ps[:, 0:32], cst("rot"), kc_raw[:].rearrange("p g c -> p (g c)"), start=True, stop=True), (1, "kcrot"))
                ps = wait_free(pe, (1, "vcT"))
                for g in range(2):
                    last = nc.tensor.transpose(ps[:, g * P:(g + 1) * P], vrep_in[:, g].rearrange("p r c -> p (r c)"), ident)
                full(last, (1, "vcT"))
                pe.wait_ge(sem("kc_ready"), 1)
                for t in range(NT):
                    ps = wait_free(pe, (1, ("cs", t)))
                    for w in range(NH // 2):
                        last = mm(ps[:, w * 32:(w + 1) * 32], qk[:, w, t * P:(t + 1) * P], kcT[:, w // 4].rearrange("p i c -> p (i c)"), start=True, stop=True)
                    full(last, (1, ("cs", t)))
                proj_tok(1, "vw", m0 + 9)
                pe.wait_ge(sem("pc_ready"), 1)
                pcs = silu_flat.rearrange("p (t g c) -> p t g c", t=NT, g=NG)
                for t in range(NT):
                    ps = wait_free(pe, (1, ("pcT", t)))
                    for g in range(NG):
                        last = nc.tensor.transpose(ps[:, g * P:(g + 1) * P], pcs[:, t, g, :], ident)
                    full(last, (1, ("pcT", t)))
                wait_read(pe, (1, "vcT"))
                for t in range(NT):
                    wait_read(pe, (1, ("pcT", t)))

                def to_output(w, i, q, stationary, moving, first=False):
                    return mm(acc_pair[i * NDH:(i + 1) * NDH, w % 8, q], stationary, moving, start=(first and w % 2 == 0), stop=True, skip_group_check=True)

                for w in range(8):
                    for i, h in enumerate(pair_heads(w)):
                        to_output(w, i, slice(0, T), v_blk[:, h // NJ, h % NJ, :], pcT[:, :, h // NJ, :], first=True)

                def scores(w, i):
                    rows, pair, tile = head_rows(pair_heads(w)[i])
                    ps = wait_free(pe, (1, ("US", w, i)))
                    for q0, n in ((0, P), (P, T)):
                        mm(ps[:, q0:q0 + n], qk[rows, tile, q0:q0 + P], kT_sw[rows, w // 8, pair, 0:n], start=True, stop=False)
                        last = mm(ps[:, q0 + n - P:q0 + n], ident_bf[:], later_bf[:], start=False, stop=True)
                    full(last, (1, ("US", w, i)))

                def turn_probs(w, i):
                    pe.wait_ge(sem("u_scaled"), 2 * w + i + 1)
                    ps = wait_free(pe, (1, ("UT", w, i)))
                    for c in range(3):
                        last = nc.tensor.transpose(ps[:, c * P:(c + 1) * P], u_p[w % 2][:, i, c * P:(c + 1) * P], ident)
                    full(last, (1, ("UT", w, i)))

                def pair_values(w):
                    for i in range(2):
                        wait_read(pe, (1, ("UT", w, i)))
                    parts = [(u_pT[w % 2][:, i], v_sw[:, w // 8, :, h // NJ * NDH:(h // NJ + 1) * NDH]) for i, h in enumerate(pair_heads(w))]
                    for i, (pt, vv) in enumerate(parts):
                        to_output(w, i, slice(0, T), vv[:, 0, :], pt[:, 0:T])
                    for i, (pt, vv) in enumerate(parts):
                        to_output(w, i, slice(P, T), vv[:, 1, :], pt[:, T:T + P]).then_inc(sem("u_pv"), 1)

                for w in range(NPAIR + 1):
                    for i in range(2):
                        if w < NPAIR:
                            scores(w, i)
                        if w:
                            turn_probs(w - 1, i)
                    if w > 1:
                        pair_values(w - 2)
                pair_values(NPAIR - 1)
                for who in ("act", "dve"):
                    pe.wait_ge(sem("oT_read_" + who), 2)
                out_projection(1, lambda t: None)

            def tail(layer):
                pe.wait_ge(sem("ld_p"), 16 * (layer + 1))
                ps = wait_free(pe, (layer, "pT"))
                for k in range(2):
                    for t in range(NT):
                        c = (k * NT + t) * P
                        last = nc.tensor.transpose(ps[:, c:c + P], p_in[:, t, k::2], ident)
                full(last, (layer, "pT"))
                transposes(layer, "xT", x[:], [(sem("ln_done"), NT * 2 * layer + t + 1) for t in range(NT)])
                pe.wait_ge(sem("ld_router"), 32 * (layer + 1))
                ps = wait_free(pe, (layer, "logits"))
                for t in range(NT):
                    wait_tile(layer, "xT", t)
                    for k in range(KD):
                        last = mm(ps[:, t * NE:(t + 1) * NE], xT[:, k, t * P:(t + 1) * P], router[:, k, :], start=(k == 0), stop=(k == KD - 1))
                full(last, (layer, "logits"))
                n = PIECE_SH[layer]
                proj_T(layer, "sh_gate", n, True)
                proj_T(layer, "sh_up", n + 1, True)
                wait_read(pe, (layer, "sh_up"))
                pe.wait_ge(sem("acc_read"), 2 * layer + 1)
                hid_v = hid[:].rearrange("p b (f t) -> p b f t", f=2)
                rows_to_acc(hid_v[:, 1], n + 2, 0, True, True)
                pe.wait_ge(sem("cw_ready"), layer + 1)
                ps = wait_free(pe, (layer, "rank"))
                mm(ps[:, 0:NE], cst("earlier"), cand[:, 0, :], start=True, stop=True)
                mm(ps[:, NE:2 * NE], cst("ones"), cand[:, 0, :], start=True, stop=False)
                mm(ps[:, NE:2 * NE], cst("earlier"), cand[:, 1, :], start=False, stop=True)
                mm(ps[:, 2 * NE:3 * NE], cst("ones"), cand[:, 0, :], start=True, stop=False)
                last = mm(ps[:, 2 * NE:3 * NE], cst("ones"), cand[:, 1, :], start=False, stop=True)
                full(last, (layer, "rank"))

                def gather(take_bank, n_banks, n_slots):
                    per = KD // n_banks
                    last = []
                    for k in range(KD):
                        if k % per == 0:
                            bank = take_bank(k // per)
                        dst = bank[:, (k % per) * n_slots:(k % per + 1) * n_slots]
                        for s in range(3):
                            for t in range(NT):
                                hot = onehot[:, t].rearrange("p b c -> p (b c)")[:, 0:n_slots]
                                ins = mm(dst, x_part[s][:, t, k::KD], hot, start=(s == 0 and t == 0), stop=(s == 2 and t == NT - 1))
                        if k % per == per - 1:
                            last.append(ins)
                    return last

                def gate_up(ps, w, wait_high=None):
                    for i in range(2):
                        for k in range(KD):
                            if wait_high and i == 0 and k == KD // 2:
                                wait_high()
                            for b in range(len(w)):
                                wk = w[b][i].rearrange("p (k c) -> p k c", k=KD)[:, k, :]
                                slots = slice(b * CAP, (b + 1) * CAP)
                                last = mm(ps[slots, i * FF:(i + 1) * FF], xg[:, k, slots], wk, start=(k == 0), stop=(k == KD - 1))
                    return last

                def turn_hidden(ps):
                    for k in range(2):
                        last = nc.tensor.transpose(ps[:, k * P:(k + 1) * P], hid_e[:, k::2], ident)
                    return last

                def turn_weighted(ps, n_slots):
                    for t in range(NT):
                        src = weighted_1h[:, t].rearrange("p b c -> p (b c)")[:, 0:n_slots]
                        last = nc.tensor.transpose(ps[0:n_slots, 2 * P + t * P:2 * P + (t + 1) * P], src, ident)
                    return last

                def down(banks, turned, w):
                    last = []
                    for half in range(2):
                        for k in range(2):
                            for b in range(len(w)):
                                wk = w[b].rearrange("p (k c) -> p k c", k=2)[:, k, half * 512:(half + 1) * 512]
                                c = k * P + b * CAP
                                ins = mm(banks[half][b * CAP:(b + 1) * CAP, :], turned[:, c:c + CAP], wk, start=(k == 0), stop=(k == 1))
                        last.append(ins)
                    return last

                def scatter_half(turned, n_slots, half):
                    for t in range(NT):
                        src = turned[0:n_slots, 2 * P + t * P:2 * P + (t + 1) * P]
                        c = slice(half * 512, (half + 1) * 512)
                        last = mm(acc[:, t, c], src, y_sb[0:n_slots, c], start=False, stop=True, skip_group_check=True)
                    return last

                pe.wait_ge(sem("x_part"), 3 * (layer + 1))
                pe.wait_ge(sem("hot_ready"), layer * (NE // 2 + 1) + 1)
                for n, last in zip(("xgL", "xgH"), gather(lambda half: wait_free(pe, (layer, ("xgL", "xgH")[half])), 2, 2 * CAP)):
                    full(last, (layer, n))

                n0 = PIECE_LOOP[layer]
                with pe.Fori(0, N_BODIES) as i:
                    def loop_piece(kind, e):
                        n = n0 + BODY.index((kind, e))
                        pe.wait_ge(landed[n % RING], i * 16 + landed_value(n))
                        return ring[:, n % RING, :]

                    def loop_fills(ins, g):
                        ins.then_inc(bank_full[loop_bank(layer, g)[0]], 1)

                    def loop_gather(pair, n):
                        pe.wait_ge(sem("hot_ready"), i * 2 + (layer * (NE // 2 + 1) + n))
                        take_bank = lambda half: loop_wait_free(pe, layer, (("xgL", "xgH")[half], pair), i)
                        for g, last in zip(("xgL", "xgH"), gather(take_bank, 2, 2 * CAP)):
                            loop_fills(last, (g, pair))

                    def loop_gate_up(pair):
                        w = [[loop_piece(k, 2 * pair + b) for k in "gu"] for b in range(2)]
                        ps = loop_wait_free(pe, layer, ("gu", pair), i)
                        low, high = [lambda g=g: loop_read(pe, layer, (g, pair), i, last_body=(pair == 0)) for g in ("xgL", "xgH")]
                        low()
                        loop_fills(gate_up(ps, w, high), ("gu", pair))

                    def loop_turn(pair):
                        pe.wait_ge(sem("weighted_ready"), i * 2 + (layer * (NE // 2 + 1) + pair + 1))
                        loop_read(pe, layer, ("gu", pair), i)
                        ps = loop_wait_free(pe, layer, ("turn", pair), i)
                        turn_hidden(ps)
                        loop_fills(turn_weighted(ps, 2 * CAP), ("turn", pair))

                    def loop_down(pair):
                        loop_read(pe, layer, ("turn", pair), i)
                        w = [loop_piece("d", 2 * pair + b) for b in range(2)]
                        banks = [loop_wait_free(pe, layer, ("y", pair, half), i) for half in range(2)]
                        for half, last in enumerate(down(banks, turned_e[pair], w)):
                            loop_fills(last, ("y", pair, half))

                    def loop_scatter(pair):
                        for half in range(2):
                            loop_read(pe, layer, ("y", pair, half), i)
                            scatter_half(turned_e[pair], 2 * CAP, half)

                    loop_gate_up(0)
                    loop_gather(1, 2)
                    loop_turn(0)
                    loop_gate_up(1)
                    loop_down(0)
                    loop_turn(1)
                    loop_gather(0, 3)
                    loop_scatter(0)
                    loop_down(1)
                    loop_scatter(1)

                for g in BODY_GROUPS[-NB_WORK:]:
                    loop_read(pe, layer, g, N_BODIES - 1)
                pe.wait_ge(more_done[layer], 1)
                s = more[layer]
                with pe.Fori(0, MORE // MORE_PART) as part:
                    part_id = pe.value_load(more_i[0:1, bass.ds(part * MORE_PART, 1)], min_val=0, max_val=NE * NBLK - 1)
                    with pe.If(part_id > 0):
                        with pe.Fori(0, MORE_PART // MORE_RUN) as run:
                            run_id = pe.value_load(more_i[0:1, bass.ds(part * MORE_PART + run * MORE_RUN, 1)], min_val=0, max_val=NE * NBLK - 1)
                            with pe.If(run_id > 0):
                                with pe.Fori(0, MORE_RUN) as at:
                                    m = part * MORE_PART + run * MORE_RUN + at
                                    block_id = pe.value_load(more_i[0:1, bass.ds(m, 1)], min_val=0, max_val=NE * NBLK - 1)
                                    with pe.If(block_id > 0):
                                        pe.wait_ge(s["hot"], m + 1)
                                        gather(lambda _: work[0], 1, CAP)[0].then_inc(s["xg"], 1)
                                        turn_weighted(work[2], CAP)
                                        w = []
                                        for j in range(3):
                                            pe.wait_ge(more_landed[layer][j], m * 16 + 16)
                                            w.append(ring[:, (MORE_PIECE[layer] + j) % RING, :])
                                        pe.wait_ge(s["xg_read"], m + 1)
                                        gate_up(work[1], [w[0:2]]).then_inc(s["gu"], 1)
                                        pe.wait_ge(s["hid"], m + 1)
                                        turn_hidden(work[2]).then_inc(s["turn"], 1)
                                        pe.wait_ge(s["turn_read"], m + 1)
                                        down([work[3], work[0]], turned_e[0], w[2:3])[1].then_inc(s["y"], 1)
                                        pe.wait_ge(s["y_read"], m + 1)
                                        scatter_half(turned_e[0], CAP, 0)
                                        scatter_half(turned_e[0], CAP, 1).then_inc(more_done[layer], 1)
                pe.drain().then_inc(sem("experts_done"), 1)

                w = piece(PIECE_PLE[layer]).rearrange("p (k c) -> p k c", k=2)
                for q in range(4):
                    t, half = q // 2, q % 2
                    ps = wait_free(pe, (layer, ("pw", q)))
                    for k in range(2):
                        last = mm(ps[:, :], pT[:, k, t * P:(t + 1) * P], w[:, k, half * 512:(half + 1) * 512], start=(k == 0), stop=(k == 1))
                    full(last, (layer, ("pw", q)))
                def turn_x(t):
                    pe.wait_ge(sem("ln_done"), NT * (2 * layer + 1) + t + 1)
                    for last in turn_tile([acc[:, t, half * 512:(half + 1) * 512] for half in range(2)], x[:], t):
                        last.then_inc(sem("xT2_full"), 1)

                def gate_product(q):
                    t, half = q // 2, q % 2
                    for j in range(4):
                        w = piece(PIECE_PLE[layer] + 1 + j).rearrange("p (k c) -> p k c", k=2)
                        for i in range(2):
                            last = mm(acc[:, t, half * 512:(half + 1) * 512], xT[:, 2 * j + i, t * P:(t + 1) * P],
                                      w[:, i, half * 512:(half + 1) * 512], start=(j == 0 and i == 0), stop=(j == 3 and i == 1))
                        if j == 3:
                            last.then_inc(sem("pg_full"), 1)
                        elif q == 3:
                            last.then_inc(rows_used, 1)

                turn_x(0)
                pe.wait_ge(sem("xT2_read_act"), 3 * layer + 2)
                gate_product(0)
                turn_x(1)
                gate_product(1)
                pe.wait_ge(sem("xT2_read_act"), 3 * (layer + 1))
                pe.wait_ge(sem("xT2_read_dve"), layer + 1)
                gate_product(2)
                gate_product(3)

            mlstm()
            tail(0)
            nsa()
            tail(1)

        @block.scalar
        def _(act):
            af = nc.scalar.activation
            chain = Chain(act, sem("act_step"))

            def copies_T(layer, name, dst):
                for g in (0, 1, 3):
                    t, half = g // 2, g % 2
                    ps = wait_full(act, (layer, (name, g)))
                    free(nc.scalar.copy(dst[:, 4 * half:4 * half + 4, t * P:(t + 1) * P], ps[:, :].rearrange("p (k c) -> p k c", k=4)), (layer, (name, g)))

            def mlstm():
                copies_T(0, "x0T", xT)
                act.wait_ge(sem("gabs"), 1)
                chain.step(af(gbuf[:, 2, :], gbuf[:, 2, :], ACT.Exp, scale=-1.0))
                af(gbuf[:, 2, :], gbuf[:, 2, :], ACT.Ln, bias=1.0).then_inc(sem("glog"), 1)
                act.wait_ge(sem("gneg"), 1)
                af(gbuf[:, 6, :], gbuf[:, 6, :], ACT.Exp).then_inc(sem("grows"), 1)
                for g in range(4):
                    wait_read(act, (0, ("qk", g)))
                    v = qk[:, 2 * g:2 * g + 2, :]
                    af(v, v, ACT.Silu).then_inc(sem("qk_ready"), 1)
                for h in range(MH):
                    wait_read(act, (0, ("B", h // 2)))
                    af(decay(h), decay(h), ACT.Exp).then_inc(sem("decay_ready"), 1)
                for g in range(4):
                    ps = wait_full(act, (0, ("v", g)))
                    src = ps[:, :].rearrange("p (t h e) -> p t h e", t=NT, h=2)
                    for t in range(NT):
                        last = nc.scalar.copy(v_aug[:, t, 2 * g:2 * g + 2, 0:MDV], src[:, t])
                    free(last, (0, ("v", g)))
                for g in range(4):
                    ps = wait_full(act, (0, ("o", g)))
                    src = ps[:, :].rearrange("p (t c) -> p t c", t=NT)
                    free(af(sig_o[:, :, g * 256:(g + 1) * 256], src, ACT.Sigmoid), (0, ("o", g)))
                act.wait_ge(sem("hvar"), 1)
                af(hmv[:, :, :, 1], hmv[:, :, :, 1], ACT.Sqrt).then_inc(sem("hstd"), 1)
                act.wait_ge(sem("hbias"), 1)
                for h in range(MH):
                    last = af(hm[:, 1, h, :], hm[:, 1, h, :], ACT.Identity, scale=hmv[:, 1, h, 1:2], bias=hbias[:, h:h + 1])
                last.then_inc(sem("hnorm1"), 1)
                copies_T(0, "mT", mixT)

            def norm(n):
                for t in range(NT):
                    act.wait_ge(sem("ln_var"), NT * (n - 1) + t + 1)
                    af(lnmv[:, t, 1:2], lnmv[:, t, 1:2], ACT.Sqrt).then_inc(sem("ln_std"), 1)

            def nsa():
                copies_T(1, "x1T", xT)
                ps = wait_full(act, (1, "g"))
                free(af(gsig[:].rearrange("p t h c -> p t (h c)"), ps[:, 0:96].rearrange("p (t c) -> p t c", t=NT), ACT.Sigmoid), (1, "g"))
                for n, name in enumerate(("q0", "q1", "q2", "q3", "ks", "kw")):
                    ps = wait_full(act, (1, name))
                    if n >= 2:
                        act.wait_ge(sem("rope_done"), n - 1)
                    scale = NDH ** -0.5 if name in ("ks", "kw") else 1.0
                    free(af(silu[:, n % 2, :], ps[:, :], ACT.Copy, scale=scale), (1, name))

                def values(v):
                    ps = wait_full(act, (1, v))
                    free(nc.scalar.copy(v_sw[:, v == "vw"].rearrange("p t c -> p (t c)"), ps[:, :]), (1, v))

                values("vs")
                act.wait_ge(sem("cs_ready"), 1)
                af(cs_s[:, :, :, 0:NCMP], cs_s[:, :, :, 0:NCMP], ACT.Exp, scale=NDH ** -0.5).then_inc(sem("cs_exp"), 1)
                values("vw")
                for t in range(NT):
                    ps = wait_full(act, (1, ("pcT", t)))
                    free(nc.scalar.copy(pcT[:, t].rearrange("p g c -> p (g c)"), ps[:, :]), (1, ("pcT", t)))

                def turned(w, i):
                    ps = wait_full(act, (1, ("UT", w, i)))
                    if w >= 2:
                        act.wait_ge(sem("u_pv"), 2 * (w - 2) + i + 1)
                    free(nc.scalar.copy(u_pT[w % 2][:, i], ps[:, 0:384]), (1, ("UT", w, i)))

                for w in range(NPAIR):
                    for i, h in enumerate(pair_heads(w)):
                        act.wait_ge(sem("u_max"), 2 * w + i + 1)
                        if w >= 2:
                            wait_full(act, (1, ("UT", w - 2, i)))
                        ps, p = wait_full(act, (1, ("US", w, i))), u_p[w % 2][:, i]
                        af(p[:, 0:P], ps[:, 0:P], ACT.Exp, bias=nmax[:, w % 2, i, 0:1], accum_out=nden[:, 0, h:h + 1])
                        free(af(p[:, P:P + T], ps[:, P:P + T], ACT.Exp, bias=nmax[:, w % 2, i, 1:2],
                                accum_out=nden[:, 1, h:h + 1]), (1, ("US", w, i)))
                        if w:
                            turned(w - 1, i)
                for i in range(2):
                    turned(NPAIR - 1, i)
                for half in range(2):
                    act.wait_ge(sem("u_pv"), 2 * (8 + 4 * half + 2))
                    nc.scalar.copy(mixT[:, 4 * half:4 * half + 2], acc_pair[:, 4 * half:4 * half + 2]).then_inc(sem("oT_read_act"), 1)

            def tail(layer):
                ps = wait_full(act, (layer, "pT"))
                free(nc.scalar.copy(pT[:].rearrange("p k t -> p (k t)"), ps[:, :]), (layer, "pT"))
                copies_T(layer, "xT", xT)
                act.wait_ge(sem("ln_done"), NT * (2 * layer + 1))
                nc.scalar.copy(x_part[0], x[:]).then_inc(sem("x_part"), 1)
                ps = wait_full(act, (layer, "logits"))
                free(af(score[:].rearrange("p t e -> p (t e)"), ps[:, 0:NT * NE], ACT.Sigmoid), (layer, "logits"))
                for s in range(1, 3):
                    act.wait_ge(sem("x_rest"), 2 * layer + s)
                    nc.scalar.copy(x_part[s], x_rest).then_inc(sem("x_part"), 1)
                ps = wait_full(act, (layer, "sh_gate"))
                free(af(silu[:, 1, :], ps[:, :], ACT.Silu), (layer, "sh_gate"))
                ps = wait_full(act, (layer, "xgL"))
                free(nc.scalar.copy(xg[:, 0:4, :].rearrange("p k c -> p (k c)"), ps[:, :]), (layer, "xgL"))
                with act.Fori(0, N_BODIES) as i:
                    def read(ins, g):
                        ins.then_inc(bank_free[loop_bank(layer, g)[0]], 1)

                    def copied(g, dst):
                        ps = loop_full(act, layer, g, i)
                        read(nc.scalar.copy(dst, ps[:, :]), g)

                    def gate(pair):
                        ps = loop_full(act, layer, ("gu", pair), i)
                        af(sil_e, ps[:, 0:FF], ACT.Silu).then_inc(sem("silu_ready"), 1)

                    xg_lo = xg[:, 0:4, :].rearrange("p k c -> p (k c)")
                    gate(0)
                    copied(("xgL", 1), xg_lo)
                    copied(("turn", 0), turned_e[0])
                    gate(1)
                    copied(("y", 0, 0), y_sb[:, 0:512])
                    copied(("turn", 1), turned_e[1])
                    copied(("xgL", 0), xg_lo)
                    copied(("y", 1, 0), y_sb[:, 0:512])
                act.wait_ge(more_done[layer], 1)
                s = more[layer]
                with act.Fori(0, MORE // MORE_PART) as part:
                    part_id = act.value_load(more_i[0:1, bass.ds(part * MORE_PART, 1)], min_val=0, max_val=NE * NBLK - 1)
                    with act.If(part_id > 0):
                        with act.Fori(0, MORE_PART // MORE_RUN) as run:
                            run_id = act.value_load(more_i[0:1, bass.ds(part * MORE_PART + run * MORE_RUN, 1)], min_val=0, max_val=NE * NBLK - 1)
                            with act.If(run_id > 0):
                                with act.Fori(0, MORE_RUN) as at:
                                    m = part * MORE_PART + run * MORE_RUN + at
                                    block_id = act.value_load(more_i[0:1, bass.ds(m, 1)], min_val=0, max_val=NE * NBLK - 1)
                                    with act.If(block_id > 0):
                                        act.wait_ge(s["xg"], m + 1)
                                        nc.scalar.copy(xg[:, :, 0:CAP], work[0][:, :].rearrange("p (k c) -> p k c", k=KD)).then_inc(s["xg_read"], 1)
                                        act.wait_ge(s["gu"], m + 1)
                                        af(sil_e[0:CAP], work[1][0:CAP, 0:FF], ACT.Silu).then_inc(s["silu"], 1)
                norm(2 * layer + 2)
                for g in (0, 1, 3):
                    t, half = g // 2, g % 2
                    act.wait_ge(sem("xT2_full"), 4 * layer + g + 1)
                    src = acc[:, t, half * 512:(half + 1) * 512].rearrange("p (k c) -> p k c", k=4)
                    nc.scalar.copy(xT[:, 4 * half:4 * half + 4, t * P:(t + 1) * P], src).then_inc(sem("xT2_read_act"), 1)
                for q in range(4):
                    act.wait_ge(sem("pg_full"), 4 * layer + q + 1)
                    c = slice((q % 2) * 512, (q % 2 + 1) * 512)
                    af(sig_o[:, q // 2, c], acc[:, q // 2, c], ACT.Sigmoid).then_inc(sem("sig_ready"), 1)

            mlstm()
            norm(1)
            tail(0)
            nsa()
            norm(3)
            tail(1)

        @block.vector
        def _(dve):
            chain = Chain(dve, sem("dve_step"))
            step = chain.step
            copy, ts, tt, stt = nc.vector.tensor_copy, nc.vector.tensor_scalar, nc.vector.tensor_tensor, nc.vector.scalar_tensor_tensor

            def copies_T(layer, name, dst):
                g = (layer, (name, 2))
                ps = wait_full(dve, g)
                free(copy(dst[:, 0:4, P:T], ps[:, :].rearrange("p (k c) -> p k c", k=4)), g)

            def mlstm():
                copies_T(0, "x0T", xT)
                nc.vector.memset(slot_of[:], -1.0)
                step(nc.vector.memset(cw[:], 0.0))
                step(nc.vector.memset(gbuf[:, 7, :], 1.0))
                ps = wait_full(dve, (0, "gates"))
                dve.wait_ge(sem("ld_gbias"), 32)
                ts(gbuf[:, 0, :], ps[0:MH, 0:T], gbias[:, 0:1], None, ALU.add)
                free(ts(gbuf[:, 1, :], ps[0:MH, T:2 * T], gbias[:, 1:2], None, ALU.add), (0, "gates"))
                wait_read(dve, (0, "gates"))
                stt(gbuf[:, 2, :], gbuf[:, 1, :], -1.0, gbuf[:, 1, :], ALU.mult, ALU.max).then_inc(sem("gabs"), 1)
                dve.wait_ge(sem("glog"), 1)
                step(stt(gbuf[:, 1, :], gbuf[:, 1, :], 0.0, gbuf[:, 2, :], ALU.min, ALU.subtract))
                step(nc.vector.tensor_tensor_scan(gbuf[:, 3, :], gbuf[:, 7, :], gbuf[:, 1, :], 0.0, ALU.mult, ALU.add))
                step(tt(gbuf[:, 4, :], gbuf[:, 0, :], gbuf[:, 3, :], ALU.subtract))
                step(nc.vector.tensor_tensor_scan(gbuf[:, 5, :], gbuf[:, 4, :], gbuf[:, 4, :], 0.0, ALU.max, ALU.max))
                step(stt(gbuf[:, 6, :], gbuf[:, 3, :], -1.0, gbuf[:, 5, :], ALU.mult, ALU.subtract))
                ts(gbuf[:, 5, :], gbuf[:, 5, :], -1.0, None, ALU.mult).then_inc(sem("gneg"), 1)
                ps = wait_full(dve, (0, "convT"))
                free(copy(conv_w[:], ps[:, 0:32]), (0, "convT"))
                wait_read(dve, (0, "convT"))
                for g in range(4):
                    ps = wait_full(dve, (0, ("qk", g)))
                    for c in range(2):
                        ch = 2 * g + c
                        y, src = qk[:, ch, :], ps[:, c * T:(c + 1) * T]
                        step(ts(y, src, conv_w[:, 3 * 8 + ch:3 * 8 + ch + 1], None, ALU.mult))
                        for back in range(1, MCONV):
                            j = (MCONV - 1 - back) * 8 + ch
                            last = stt(y[:, back:T], src[:, 0:T - back], conv_w[:, j:j + 1], y[:, back:T], ALU.mult, ALU.add)
                            if back < MCONV - 1:
                                step(last)
                    free(last, (0, ("qk", g)))
                ps = wait_full(dve, (0, "gateT"))
                free(copy(gtok[:].rearrange("p a h -> p (a h)"), ps[:, 0:4 * MH]), (0, "gateT"))
                wait_read(dve, (0, "gateT"))
                for g in range(4):
                    ps = wait_full(dve, (0, ("B", g)))
                    for i in range(2):
                        h = 2 * g + i
                        d = decay(h)
                        stt(d[:, 0:T], ps[:, i * T:(i + 1) * T], gtok[:, 0, h:h + 1], cst("mask_st"), ALU.add, ALU.min)
                        last = stt(d[:, T:T + P], ps[:, i * T + P:(i + 1) * T], gtok[:, 1, h:h + 1], cst("mask_st")[:, 0:P], ALU.add, ALU.min)
                    free(last, (0, ("B", g)))

                def weighted(h):
                    ps = wait_full(dve, (0, ("S", h)))
                    dve.wait_ge(sem("decay_ready"), h + 1)
                    free(stt(pt_m[h % 2], ps[:, 0:384], MDK ** -0.5, decay(h), ALU.mult, ALU.mult), (0, ("S", h)))

                def gain(g):
                    wait_read(dve, (0, ("o", g)))
                    c = slice(256 * g, 256 * (g + 1))
                    return tt(sig_o[:, :, c], sig_o[:, :, c], ln_p[:, 0, c].unsqueeze(1).to_broadcast([P, NT, 256]), ALU.mult)

                dve.wait_ge(sem("ld_norm"), 16)
                for g in range(3):
                    gain(g)
                weighted(0)
                for h in range(MH):
                    if h + 1 < MH:
                        weighted(h + 1)
                    if h == 0:
                        step(gain(3), sem("norm_g_used"))
                    ps = wait_full(dve, (0, ("num", h)))
                    v = ps[:, :].rearrange("p (t e) -> p t e", t=NT)
                    step(stt(den2[:], v[:, :, MDV], -1.0, gtok[:, 2:4, h], ALU.mult, ALU.max))
                    step(tt(den2[:], v[:, :, MDV], den2[:], ALU.max))
                    step(nc.vector.reciprocal(den2[:], den2[:]))
                    for t in range(NT):
                        last = ts(hm[:, t, h, :], v[:, t, 0:MDV], den2[:, t:t + 1], None, ALU.mult)
                    free(last, (0, ("num", h)))
                    wait_read(dve, (0, ("num", h)))
                    for t in range(NT):
                        last = nc.vector.bn_stats(hst[:, t, :], hm[:, t, h, :])
                    step(last)
                    for t in range(NT):
                        last = nc.vector.bn_aggr(hmv[:, t, h, :], hst[:, t, :])
                step(last)
                ts(hmv[:, :, :, 1], hmv[:, :, :, 1], EPS, None, ALU.add).then_inc(sem("hvar"), 1)
                dve.wait_ge(sem("hstd"), 1)
                step(nc.vector.reciprocal(hmv[:, :, :, 1], hmv[:, :, :, 1]))
                stt(hbias[:], hmv[:, 1, :, 0], -1.0, hmv[:, 1, :, 1], ALU.mult, ALU.mult).then_inc(sem("hbias"), 1)
                for h in range(MH):
                    last = ts(hm[:, 0, h, :], hm[:, 0, h, :], hmv[:, 0, h, 0:1], hmv[:, 0, h, 1:2], ALU.subtract, ALU.mult)
                step(last)
                for t in range(NT):
                    if t:
                        dve.wait_ge(sem("hnorm1"), 1)
                    tt(hm_flat[:, t, :], hm_flat[:, t, :], sig_o[:, t, :], ALU.mult).then_inc(sem("mix_ready"), 1)
                copies_T(0, "mT", mixT)

            iota_pair = cst("iota").unsqueeze(1).unsqueeze(1).to_broadcast([P, NT, 2, CAP])

            def norm(n):
                layer, k = (n - 1) // 2, (n - 1) % 2
                if k == 1:
                    dve.wait_ge(sem("experts_done"), layer + 1)

                def stats(t):
                    if k == 0 and t == 0:
                        dve.wait_ge(sem("out_tile0"), layer + 1)
                    elif k == 0:
                        dve.wait_ge(rows_used, ROWS_BEFORE_LOOP[layer] - 1)
                    step(stt(z[:, t, :], x[:, t, :], ALPHA, acc[:, t, :], ALU.mult, ALU.add), sem("acc_read") if t == NT - 1 else None)
                    for half in range(2):
                        last = nc.vector.bn_stats(lnst[:, t, half, :], z[:, t, half * 512:(half + 1) * 512])
                    step(last)
                    step(nc.vector.bn_aggr(lnmv[:, t, :], lnst[:, t].rearrange("p a b -> p (a b)")))
                    ts(lnmv[:, t, 1:2], lnmv[:, t, 1:2], EPS, None, ALU.add).then_inc(sem("ln_var"), 1)

                def apply(t):
                    dve.wait_ge(sem("ld_ln"), 32 * n)
                    stt(z[:, t, :], z[:, t, :], lnmv[:, t, 0:1], ln_p[:, 0, :], ALU.subtract, ALU.mult)
                    dve.wait_ge(sem("ln_std"), NT * (n - 1) + t + 1)
                    step(nc.vector.reciprocal(lnmv[:, t, 1:2], lnmv[:, t, 1:2]))
                    step(stt(x[:, t, :], z[:, t, :], lnmv[:, t, 1:2], ln_p[:, 1, :], ALU.mult, ALU.add), sem("ln_done"))

                for t in range(NT):
                    stats(t)
                    apply(t)

            def choose(layer):
                wait_read(dve, (layer, "logits"))
                dve.wait_ge(sem("ld_router"), 32 * (layer + 1))
                for t in range(NT):
                    last = tt(biased[:, t, :], score[:, t, :], rbias[:], ALU.add)
                step(last)
                for t in range(NT):
                    for g in range(NEG):
                        last = nc.vector.max(grp8[:, t * NEG + g, :], biased[:, t, g * 8:(g + 1) * 8])
                step(last)
                step(tt(grp[:], grp8[:, :, 0], grp8[:, :, 1], ALU.add))
                g3 = grp[:].rearrange("p (t g) -> p t g", t=NT)
                for t in range(NT):
                    other = g3[:, t, :].unsqueeze(1).to_broadcast([P, NEG, NEG])
                    own = g3[:, t, :].unsqueeze(2).to_broadcast([P, NEG, NEG])
                    tt(gcmp[:, t], other, own, ALU.is_gt)
                    last = tt(geq[:, t], other, own, ALU.is_equal)
                step(last)
                for t in range(NT):
                    last = tt(geq[:, t], geq[:, t], cst("before").rearrange("p (a b) -> p a b", a=NEG), ALU.mult)
                step(last)
                step(tt(gcmp[:], gcmp[:], geq[:], ALU.add))
                step(nc.vector.reduce_sum(rank[:], gcmp[:].rearrange("p t a b -> p (t a) b"), axis=AX.X))
                step(ts(grp[:], rank[:], float(TOPG) - 0.5, None, ALU.is_lt))
                e3 = [v[:].rearrange("p t (g e) -> p (t g) e", g=NEG) for v in (biased, cand)]
                step(ts(rank[:], grp[:], BIG, -BIG, ALU.mult, ALU.add))
                step(tt(e3[0], e3[0], grp[:].unsqueeze(2).to_broadcast([P, NT * NEG, 8]), ALU.mult))
                step(tt(e3[0], e3[0], rank[:].unsqueeze(2).to_broadcast([P, NT * NEG, 8]), ALU.add))
                for t in range(NT):
                    last = nc.vector.max(top8[:, t, :], biased[:, t, :])
                step(last)
                for t in range(NT):
                    last = nc.vector.match_replace(cand[:, t, :], top8[:, t, :], biased[:, t, :], -3e38)
                step(last)
                step(tt(cand[:], cand[:], biased[:], ALU.not_equal))
                step(tt(cw[:, :, 0:NE], cand[:], score[:], ALU.mult))
                step(nc.vector.reduce_sum(rsum[:], cw[:, :, 0:NE], axis=AX.X))
                step(nc.vector.reciprocal(rsum[:], rsum[:]))
                for t in range(NT):
                    last = ts(cw[:, t, 0:NE], cw[:, t, 0:NE], rsum[:, t:t + 1], SCALE_R, ALU.mult, ALU.mult)
                last.then_inc(sem("cw_ready"), 1)

            def assign_slots(layer):
                ps = wait_full(dve, (layer, "rank"))
                step(stt(slot_of[:, :, 0:NE], ps[:, 0:2 * NE].rearrange("p (t e) -> p t e", t=NT), 1.0, cand[:], ALU.add, ALU.mult))
                step(ts(slot_of[:, :, 0:NE], slot_of[:, :, 0:NE], -1.0, None, ALU.add))
                more_v = more_cand[:].rearrange("p e b -> p (e b)")
                count = ps[:, 2 * NE:3 * NE].unsqueeze(2).to_broadcast([P, NE, NBLK - 1])
                free(tt(more_cand[:], count, cst("blk_floor").rearrange("p (e b) -> p e b", e=NE), ALU.is_gt), (layer, "rank"))
                wait_read(dve, (layer, "rank"))
                make_hot(0)
                step(tt(more_v, more_v, cst("blk_id"), ALU.mult))
                for r in range(MORE // 8):
                    step(nc.vector.max(more_f[:, 8 * r:8 * r + 8], more_v))
                    step(nc.vector.match_replace(more_v, more_f[:, 8 * r:8 * r + 8], more_v, 0.0))
                step(copy(more_i[:], more_f[:]))
                step(ts(more_blk[:], more_i[:], NBLK - 1, None, ALU.bitwise_and))
                step(ts(more_base[:], more_blk[:], float(CAP), None, ALU.mult), more_done[layer])

            def make_hot(first):
                slot = slot_of[:, :, bass.ds(first, 2)].unsqueeze(3).to_broadcast([P, NT, 2, CAP])
                tt(onehot[:], iota_pair, slot, ALU.is_equal).then_inc(sem("hot_ready"), 1)

            def make_weighted(first):
                weight = cw[:, :, bass.ds(first, 2)].unsqueeze(3).to_broadcast([P, NT, 2, CAP])
                tt(weighted_1h[:], onehot[:], weight, ALU.mult).then_inc(sem("weighted_ready"), 1)

            def nsa():
                copies_T(1, "x1T", xT)
                step(copy(ident_bf[:], ident))
                step(copy(later_bf[:], cst("mask_ts")))
                ps = wait_full(dve, (1, "pos"))
                free(copy(posT[:].rearrange("p i l -> p (i l)"), ps[:, 0:2 * CBLK]), (1, "pos"))
                wait_read(dve, (1, "pos"))
                cos2 = cst("cos").unsqueeze(1).to_broadcast([P, 2, T])
                sin2 = cst("sin").unsqueeze(1).to_broadcast([P, 2, T])

                def rope(n, name, dst):
                    ps = wait_full(dve, (1, name))
                    raw = silu[:, n % 2, :].rearrange("p (c t) -> p c t", c=2)
                    tmp = hid[:, n % 2, :].rearrange("p (c t) -> p c t", c=2)
                    tt(dst, raw, cos2, ALU.mult)
                    free(tt(tmp, ps[:, :].rearrange("p (c t) -> p c t", c=2), sin2, ALU.mult), (1, name))
                    wait_read(dve, (1, name))
                    last = tt(dst, dst, tmp, ALU.add)
                    step(last, sem("rope_done"))

                def with_positions(i, name):
                    ps = wait_full(dve, (1, name))
                    for half in range(2):
                        for g in range(2):
                            src = ps[:, g * T:(g + 1) * T].rearrange("p (c l) -> p c l", l=CSTR)
                            pos = posT[:, i, half * CSTR:(half + 1) * CSTR].unsqueeze(1).to_broadcast([P, T // CSTR, CSTR])
                            last = tt(kp[:, i, half, g, :].rearrange("p (c l) -> p c l", l=CSTR), src, pos, ALU.add)
                    free(last, (1, name))

                rope(0, "rq0", qk[:, 0:2, :])
                rope(1, "rq1", qk[:, 2:4, :])
                rope(2, "rq2", qk[:, 4:6, :])
                with_positions(0, "kc")
                rope(3, "rq3", qk[:, 6:8, :])
                with_positions(1, "vc")
                rope(4, "rks", kT_sw[:, 0])
                rope(5, "rkw", kT_sw[:, 1])
                step(nc.vector.memset(kc_raw[:], 0.0))
                step(nc.vector.memset(vrep_in[:], 0.0))
                step(nc.vector.memset(silu[:], 0.0))
                for par in range(2):
                    rows = slice(par * NDH, (par + 1) * NDH)
                    ps = wait_full(dve, (1, f"cmp{par}"))
                    copy(kc_raw[rows, :, 0:NCMP], ps[rows, 0:2 * NCMP].rearrange("p (g c) -> p g c", g=2))
                    for g in range(2):
                        v = ps[rows, 32 + g * NCMP:32 + (g + 1) * NCMP].unsqueeze(1).to_broadcast([NDH, 4, NCMP])
                        last = copy(vrep_in[rows, g, :, 0:NCMP], v)
                    free(last, (1, f"cmp{par}"))
                    wait_read(dve, (1, f"cmp{par}"))
                ps = wait_full(dve, (1, "kcrot"))
                cc = cst("cos_c").unsqueeze(1).to_broadcast([P, 2, 16])
                sc = cst("sin_c").unsqueeze(1).to_broadcast([P, 2, 16])
                free(tt(kc_t[:], ps[:, 0:32].rearrange("p (g c) -> p g c", g=2), sc, ALU.mult), (1, "kcrot"))
                wait_read(dve, (1, "kcrot"))
                tt(kc_rot[:], kc_raw[:], cc, ALU.mult)
                step(nc.vector.memset(kcT[:], 0.0))
                for i in range(2):
                    rows = slice(i * NDH, (i + 1) * NDH)
                    last = tt(kcT[rows, :, i, :], kc_rot[rows], kc_t[rows], ALU.add)
                last.then_inc(sem("kc_ready"), 1)
                step(nc.vector.memset(v_blk[:], 0.0))
                ps = wait_full(dve, (1, "vcT"))
                for g in range(NG):
                    for j in range(NJ):
                        rows = slice(32 * j, 32 * (j + 1))
                        last = copy(v_blk[rows, g, j, :], ps[rows, g * NDH:(g + 1) * NDH])
                free(last, (1, "vcT"))
                madd = cst("cmask_add").rearrange("p (t c) -> p t c", t=NT)
                mmul = cst("cmask_mul").rearrange("p (t c) -> p t c", t=NT)
                for t in range(NT):
                    ps = wait_full(dve, (1, ("cs", t)))
                    src = ps[:, 0:256].rearrange("p (half j i c) -> p half i j c", half=2, j=NJ, i=2)
                    for half in range(2):
                        for i in range(2):
                            h = (2 * half + i) * NJ
                            mk = madd[:, t, 0:NCMP].unsqueeze(1).to_broadcast([P, NJ, NCMP])
                            last = tt(cs_s[:, t, h:h + NJ, 0:NCMP], src[:, half, i, :, 0:NCMP], mk, ALU.add)
                    free(last, (1, ("cs", t)))
                    wait_read(dve, (1, ("cs", t)))
                step(nc.vector.reduce_max(cst16[:], cs_s[:, :, :, 0:NCMP], axis=AX.X))
                for t in range(NT):
                    last = tt(cs_s[:, t, :, 0:NCMP], cs_s[:, t, :, 0:NCMP], cst16[:, t, :].unsqueeze(2).to_broadcast([P, NH, NCMP]), ALU.subtract)
                step(last, sem("cs_ready"))
                dve.wait_ge(sem("cs_exp"), 1)
                for t in range(NT):
                    mk = mmul[:, t, 0:NCMP].unsqueeze(1).to_broadcast([P, NH, NCMP])
                    last = tt(cs_s[:, t, :, 0:NCMP], cs_s[:, t, :, 0:NCMP], mk, ALU.mult)
                step(last)
                step(nc.vector.reduce_sum(cst16[:], cs_s[:, :, :, 0:NCMP], axis=AX.X))
                step(ts(cst16[:], cst16[:], 1e-30, None, ALU.max))
                step(nc.vector.reciprocal(cst16[:], cst16[:]))
                step(tt(cst16[:], cst16[:], gsig[:, :, :, 0], ALU.mult))
                for t in range(NT):
                    last = tt(cs_p[:, t, :, 0:NCMP], cs_s[:, t, :, 0:NCMP], cst16[:, t, :].unsqueeze(2).to_broadcast([P, NH, NCMP]), ALU.mult)
                last.then_inc(sem("pc_ready"), 1)

                def maxima(w, i):
                    ps = wait_full(dve, (1, ("US", w, i)))
                    m = nmax[:, w % 2, i]
                    if w >= 2:
                        wait_read(dve, (1, ("US", w - 2, i)))
                    nc.vector.reduce_max(m[:, 0:1], ps[:, 0:P], axis=AX.X, negate=True)
                    nc.vector.reduce_max(m[:, 1:2], ps[:, P:P + T], axis=AX.X, negate=True).then_inc(sem("u_max"), 1)

                def weighted_probs(w, i):
                    h, p = pair_heads(w)[i], u_p[w % 2][:, i]
                    wait_read(dve, (1, ("US", w, i)))
                    step(nc.vector.reciprocal(nden[:, :, h], nden[:, :, h]))
                    for t, cols in enumerate((slice(0, P), slice(P, P + T))):
                        last = ts(p[:, cols], p[:, cols], nden[:, t, h:h + 1], gsig[:, t, h, w // 8 + 1:w // 8 + 2], ALU.mult, ALU.mult)
                    last.then_inc(sem("u_scaled"), 1)

                for w in range(NPAIR):
                    maxima(w, 0)
                    if w:
                        weighted_probs(w - 1, 1)
                    maxima(w, 1)
                    weighted_probs(w, 0)
                weighted_probs(NPAIR - 1, 1)
                for half in range(2):
                    dve.wait_ge(sem("u_pv"), 2 * (8 + 4 * half + 4))
                    copy(mixT[:, 4 * half + 2:4 * half + 4], acc_pair[:, 4 * half + 2:4 * half + 4]).then_inc(sem("oT_read_dve"), 1)

            def tail(layer):
                copies_T(layer, "xT", xT)
                choose(layer)
                ps = wait_full(dve, (layer, "sh_up"))
                wait_read(dve, (layer, "sh_gate"))
                free(tt(hid[:, 1, :], silu[:, 1, :], ps[:, :], ALU.mult), (layer, "sh_up"))
                assign_slots(layer)
                hot0 = layer * (NE // 2 + 1)
                dve.wait_ge(sem("hot_ready"), hot0 + 1)
                make_weighted(0)
                ps = wait_full(dve, (layer, "xgH"))
                free(copy(xg[:, 4:8, :].rearrange("p k c -> p (k c)"), ps[:, :]), (layer, "xgH"))
                with dve.Fori(0, N_BODIES) as i:
                    def read(ins, g):
                        ins.then_inc(bank_free[loop_bank(layer, g)[0]], 1)

                    def hidden(pair):
                        ps = loop_full(dve, layer, ("gu", pair), i)
                        dve.wait_ge(sem("silu_ready"), i * 2 + (layer * (NE // 2) + pair + 1))
                        read(tt(hid_e, sil_e, ps[:, FF:2 * FF], ALU.mult), ("gu", pair))

                    def copied(g, dst):
                        ps = loop_full(dve, layer, g, i)
                        read(copy(dst, ps[:, :]), g)

                    xg_hi = xg[:, 4:8, :].rearrange("p k c -> p (k c)")
                    dve.wait_ge(sem("weighted_ready"), i * 2 + (hot0 + 1))
                    make_hot(i * EPB + 2)
                    hidden(0)
                    copied(("xgH", 1), xg_hi)
                    loop_full(dve, layer, ("turn", 0), i)
                    dve.wait_ge(sem("hot_ready"), i * 2 + (hot0 + 2))
                    make_weighted(i * EPB + 2)
                    dve.wait_ge(sem("weighted_ready"), i * 2 + (hot0 + 2))
                    make_hot(i * EPB + EPB)
                    hidden(1)
                    copied(("y", 0, 1), y_sb[:, 512:1024])
                    loop_full(dve, layer, ("turn", 1), i)
                    dve.wait_ge(sem("hot_ready"), i * 2 + (hot0 + 3))
                    make_weighted(i * EPB + EPB)
                    copied(("xgH", 0), xg_hi)
                    copied(("y", 1, 1), y_sb[:, 512:1024])
                s = more[layer]
                dve.wait_ge(sem("weighted_ready"), hot0 + NE // 2 + 1)
                with dve.Fori(0, MORE // MORE_PART) as part:
                    part_id = dve.value_load(more_i[0:1, bass.ds(part * MORE_PART, 1)], min_val=0, max_val=NE * NBLK - 1)
                    with dve.If(part_id > 0):
                        with dve.Fori(0, MORE_PART // MORE_RUN) as run:
                            run_id = dve.value_load(more_i[0:1, bass.ds(part * MORE_PART + run * MORE_RUN, 1)], min_val=0, max_val=NE * NBLK - 1)
                            with dve.If(run_id > 0):
                                with dve.Fori(0, MORE_RUN) as at:
                                    m = part * MORE_PART + run * MORE_RUN + at
                                    block_id = dve.value_load(more_i[0:1, bass.ds(m, 1)], min_val=0, max_val=NE * NBLK - 1)
                                    with dve.If(block_id > 0):
                                        dve.wait_ge(more_done[layer], m + 1)
                                        e = block_id // NBLK
                                        ts(shifted[:], slot_of[:, :, bass.ds(e, 1)].rearrange("p t e -> p (t e)"), more_base[:, bass.ds(m, 1)], None,
                                           ALU.subtract).then_inc(s["own"], 1)
                                        dve.wait_ge(s["own"], m * 2 + 1)
                                        iota = cst("iota").unsqueeze(1).to_broadcast([P, NT, CAP])
                                        tt(onehot[:, :, 0, :], iota, shifted[:].unsqueeze(2).to_broadcast([P, NT, CAP]), ALU.is_equal).then_inc(s["own"], 1)
                                        dve.wait_ge(s["own"], m * 2 + 2)
                                        weight = cw[:, :, bass.ds(e, 1)].to_broadcast([P, NT, CAP])
                                        tt(weighted_1h[:, :, 0, :], onehot[:, :, 0, :], weight, ALU.mult).then_inc(s["hot"], 1)
                                        dve.wait_ge(s["gu"], m + 1)
                                        dve.wait_ge(s["silu"], m + 1)
                                        tt(hid_e[0:CAP], sil_e[0:CAP], work[1][0:CAP, FF:2 * FF], ALU.mult).then_inc(s["hid"], 1)
                                        dve.wait_ge(s["turn"], m + 1)
                                        for k in range(2):
                                            copy(turned_e[0][:, k * P:k * P + CAP], work[2][:, k * P:k * P + CAP])
                                        copy(turned_e[0][0:CAP, 2 * P:4 * P], work[2][0:CAP, 2 * P:4 * P]).then_inc(s["turn_read"], 1)
                                        dve.wait_ge(s["y"], m + 1)
                                        copy(y_sb[0:CAP, 0:512], work[3][0:CAP, :])
                                        copy(y_sb[0:CAP, 512:1024], work[0][0:CAP, :]).then_inc(s["y_read"], 1)
                norm(2 * layer + 2)
                dve.wait_ge(sem("xT2_full"), 4 * layer + 3)
                copy(xT[:, 0:4, P:T], acc[:, 1, 0:512].rearrange("p (k c) -> p k c", k=4)).then_inc(sem("xT2_read_dve"), 1)
                for q in range(4):
                    t, c = q // 2, slice((q % 2) * 512, (q % 2 + 1) * 512)
                    ps = wait_full(dve, (layer, ("pw", q)))
                    dve.wait_ge(sem("sig_ready"), 4 * layer + q + 1)
                    free(tt(z[:, t, c], sig_o[:, t, c], ps[:, :], ALU.mult), (layer, ("pw", q)))
                    wait_read(dve, (layer, ("pw", q)))
                    last = tt(x[:, t, c], x[:, t, c], z[:, t, c], ALU.add)
                    if q % 2:
                        step(last, sem("ple_done"))

            mlstm()
            norm(1)
            tail(0)
            nsa()
            norm(3)
            tail(1)


_INS = ["x", "p", "ln_g", "ln_b", "mlstm_w_in", "mlstm_conv", "mlstm_ig_bias", "mlstm_fg_bias", "mlstm_norm_g",
        "mlstm_w_out", "nsa_w_in", "nsa_cmp_pos_k", "nsa_cmp_pos_v", "nsa_cmp_wk", "nsa_cmp_wv", "nsa_w_out",
        "router_w", "router_bias", "exp_w_gate", "exp_w_up", "exp_w_down", "sh_w_gate", "sh_w_up", "sh_w_down",
        "ple_w", "ple_gate_w"]


def kernel(**inputs):
    import concourse.bacc as _bacc
    from concourse.bass_utils import run_bass_kernel_spmd as _run

    nc = _bacc.Bacc("TRN2", target_bir_lowering=False, num_devices=1)
    arrays, aps = {}, {}
    for name in _INS:
        arr = np.ascontiguousarray(inputs[name])
        arrays[f"in_{name}"] = arr
        aps[name] = nc.dram_tensor(f"in_{name}", arr.shape, mybir.dt.from_np(arr.dtype), kind="ExternalInput").ap()
    arrays["consts"] = CONSTS
    aps["consts"] = nc.dram_tensor("consts", CONSTS.shape, F32, kind="ExternalInput").ap()
    out = nc.dram_tensor("out_0", (1, T, D), F32, kind="ExternalOutput").ap()
    build(nc, aps, out)
    r = _run(nc, [arrays], core_ids=[0])
    return r.results[0]["out_0"]
```
